# Optimizing a Trainium2 kernel written in Bass

```python
import math
import jax, jax.numpy as jnp
from jax import lax
import numpy as np

D_MODEL = 1024
BATCH = 1
SEQ = 256
DEPTH = 1

HEAD_DIM = 64
DA_HEADS = 8
DA_V_DIM = 2 * HEAD_DIM
NSA_HEADS = 16
NSA_GROUPS = 2
NSA_HPG = NSA_HEADS // NSA_GROUPS
CMP_BLOCK = 32
CMP_STRIDE = 16
CMP_HIDDEN = 256
SLC_BLOCK = 64
SLC_TOPN = 16
WIN = 512
Q_BLOCK = 128
SLC_Q_BLOCK = 64
D_FF = 2816
ROPE_THETA = 10000.0
EPS = 1e-6
NEG_INF = -1e30
FORCE_SCORE = 1e9

DA_QK_W = DA_HEADS * 2 * HEAD_DIM
DA_V_W = DA_HEADS * DA_V_DIM
NSA_Q_W = NSA_HEADS * HEAD_DIM
NSA_KV_W = NSA_GROUPS * HEAD_DIM
NSA_GATE_W = 3 * NSA_HEADS
IN_WIDTHS = (DA_QK_W, DA_QK_W, DA_V_W, NSA_Q_W) + (NSA_KV_W,) * 6 + (NSA_GATE_W, D_MODEL, D_MODEL)
D_IN = sum(IN_WIDTHS)


def rmsnorm(x, g):
    xf = x.astype(jnp.float32)
    y = xf * lax.rsqrt(jnp.mean(xf * xf, axis=-1, keepdims=True) + EPS)
    return (y * g.astype(jnp.float32)).astype(x.dtype)

def swiglu(h, w1, w3, w2):
    return (jax.nn.silu(h @ w1) * (h @ w3)) @ w2

def rope_tables(T, dim):
    pos = jnp.arange(T, dtype=jnp.float32)
    inv = 1.0 / (ROPE_THETA ** (jnp.arange(0, dim, 2, dtype=jnp.float32) / dim))
    ang = pos[:, None] * inv[None, :]
    return jnp.cos(ang), jnp.sin(ang)

def apply_rope(x, cos, sin):
    half = x.shape[-1] // 2
    shape = (1, x.shape[1]) + (1,) * (x.ndim - 3) + (half,)
    c = cos.reshape(shape).astype(x.dtype)
    s = sin.reshape(shape).astype(x.dtype)
    x1, x2 = x[..., :half], x[..., half:]
    return jnp.concatenate([x1 * c - x2 * s, x2 * c + x1 * s], axis=-1)

def _sweep(block_fn, n_blocks):
    out = lax.map(block_fn, jnp.arange(n_blocks))
    out = jnp.moveaxis(out, 0, 1)
    return out.reshape((out.shape[0], n_blocks * out.shape[2]) + out.shape[3:])

def diff_attention(q, k, v, cos, sin, lam_params, head_gain, lam_init):
    B, T = q.shape[0], q.shape[1]
    q = apply_rope(q, cos, sin)
    k = apply_rope(k, cos, sin)
    lp = lam_params.astype(jnp.float32)
    lam = jnp.exp(jnp.sum(lp[0] * lp[1])) - jnp.exp(jnp.sum(lp[2] * lp[3])) + lam_init
    kpos = jnp.arange(T)
    scale = HEAD_DIM ** -0.5

    def block(i):
        qb = lax.dynamic_slice_in_dim(q, i * Q_BLOCK, Q_BLOCK, axis=1)
        qpos = i * Q_BLOCK + jnp.arange(Q_BLOCK)
        s = jnp.einsum('bqhcd,bkhcd->bhcqk', qb, k).astype(jnp.float32) * scale
        s = jnp.where(kpos[None, :] <= qpos[:, None], s, NEG_INF)
        p = jax.nn.softmax(s, axis=-1)
        a = p[:, :, 0] - lam * p[:, :, 1]
        return jnp.einsum('bhqk,bkhe->bqhe', a.astype(v.dtype), v)

    o = _sweep(block, T // Q_BLOCK)
    o = rmsnorm(o, head_gain) * (1.0 - lam_init)
    return o.reshape(B, T, DA_V_W)

def compress(x_raw, pos, w1, w2):
    B, T = x_raw.shape[0], x_raw.shape[1]
    n_cmp = (T - CMP_BLOCK) // CMP_STRIDE + 1
    idx = np.arange(n_cmp)[:, None] * CMP_STRIDE + np.arange(CMP_BLOCK)[None, :]
    blocks = x_raw[:, idx] + pos[:, None, :]
    blocks = jnp.swapaxes(blocks, 2, 3).reshape(B, n_cmp, NSA_GROUPS, CMP_BLOCK * HEAD_DIM)
    return jax.nn.gelu(blocks @ w1) @ w2

def _overlap_matrix(n_cmp, n_slc):
    start = np.arange(n_cmp) * CMP_STRIDE
    sb = np.arange(n_slc) * SLC_BLOCK
    ov = (start[:, None] < sb[None, :] + SLC_BLOCK) & (start[:, None] + CMP_BLOCK > sb[None, :])
    return ov.astype(np.float32)

def nsa(q, k_cmp, v_cmp, k_slc, v_slc, k_win, v_win, gate_logits, cos, sin, cmp_pos, cmp_w1, cmp_w2):
    B, T = q.shape[0], q.shape[1]
    dt = q.dtype
    scale = HEAD_DIM ** -0.5
    t = jnp.arange(T)

    kc = compress(k_cmp, cmp_pos[0], cmp_w1[0], cmp_w2[0])
    vc = compress(v_cmp, cmp_pos[1], cmp_w1[1], cmp_w2[1])
    n_cmp = kc.shape[1]
    s = jnp.einsum('btgjd,bngd->btgjn', q, kc).astype(jnp.float32) * scale
    c_valid = ((jnp.arange(n_cmp) * CMP_STRIDE + CMP_BLOCK - 1)[None, :] <= t[:, None])[None, :, None, None, :]
    p_cmp = jnp.where(c_valid, jax.nn.softmax(jnp.where(c_valid, s, NEG_INF), axis=-1), 0.0)
    o_cmp = jnp.einsum('btgjn,bngd->btgjd', p_cmp.astype(dt), vc)

    n_slc = T // SLC_BLOCK
    overlap = jnp.asarray(_overlap_matrix(n_cmp, n_slc))
    imp = jnp.einsum('btgjn,ns->btgs', p_cmp, overlap)
    blk_t = t // SLC_BLOCK
    sblk = jnp.arange(n_slc)
    causal = sblk[None, :] <= blk_t[:, None]
    forced = (sblk[None, :] == 0) | (sblk[None, :] == blk_t[:, None]) | (sblk[None, :] == blk_t[:, None] - 1)
    score = jnp.where(forced[None, :, None, :], FORCE_SCORE,
                      jnp.where(causal[None, :, None, :], imp, -1.0))
    _, sel = lax.top_k(score, min(SLC_TOPN, n_slc))
    sel_valid = sel <= blk_t[None, :, None, None]

    qr = apply_rope(q, cos, sin)
    ks = apply_rope(k_slc, cos, sin)
    kw = apply_rope(k_win, cos, sin)

    ks_blk = ks.reshape(B, n_slc, SLC_BLOCK, NSA_GROUPS, HEAD_DIM).transpose(0, 3, 1, 2, 4)
    vs_blk = v_slc.reshape(B, n_slc, SLC_BLOCK, NSA_GROUPS, HEAD_DIM).transpose(0, 3, 1, 2, 4)
    bidx = jnp.arange(B)[:, None, None, None]
    gidx = jnp.arange(NSA_GROUPS)[None, None, :, None]

    def slc_block(i):
        qb = lax.dynamic_slice_in_dim(qr, i * SLC_Q_BLOCK, SLC_Q_BLOCK, axis=1)
        selb = lax.dynamic_slice_in_dim(sel, i * SLC_Q_BLOCK, SLC_Q_BLOCK, axis=1)
        validb = lax.dynamic_slice_in_dim(sel_valid, i * SLC_Q_BLOCK, SLC_Q_BLOCK, axis=1)
        qpos = i * SLC_Q_BLOCK + jnp.arange(SLC_Q_BLOCK)
        kg = ks_blk[bidx, gidx, selb]
        vg = vs_blk[bidx, gidx, selb]
        kpos = selb[..., None] * SLC_BLOCK + jnp.arange(SLC_BLOCK)
        mask = validb[..., None] & (kpos <= qpos[None, :, None, None, None])
        s = jnp.einsum('bqgjd,bqgnld->bqgjnl', qb, kg).astype(jnp.float32) * scale
        s = jnp.where(mask[:, :, :, None], s, NEG_INF)
        sh = s.shape
        p = jax.nn.softmax(s.reshape(sh[:4] + (-1,)), axis=-1).reshape(sh)
        return jnp.einsum('bqgjnl,bqgnld->bqgjd', p.astype(dt), vg)

    o_slc = _sweep(slc_block, T // SLC_Q_BLOCK)

    kw_pad = jnp.pad(kw, ((0, 0), (WIN, 0), (0, 0), (0, 0)))
    vw_pad = jnp.pad(v_win, ((0, 0), (WIN, 0), (0, 0), (0, 0)))

    def win_block(i):
        qb = lax.dynamic_slice_in_dim(qr, i * Q_BLOCK, Q_BLOCK, axis=1)
        qpos = i * Q_BLOCK + jnp.arange(Q_BLOCK)
        kb = lax.dynamic_slice_in_dim(kw_pad, i * Q_BLOCK, WIN + Q_BLOCK, axis=1)
        vb = lax.dynamic_slice_in_dim(vw_pad, i * Q_BLOCK, WIN + Q_BLOCK, axis=1)
        kpos = i * Q_BLOCK - WIN + jnp.arange(WIN + Q_BLOCK)
        mask = (kpos[None, :] >= 0) & (kpos[None, :] <= qpos[:, None]) & (kpos[None, :] > qpos[:, None] - WIN)
        s = jnp.einsum('bqgjd,bkgd->bqgjk', qb, kb).astype(jnp.float32) * scale
        s = jnp.where(mask[None, :, None, None, :], s, NEG_INF)
        p = jax.nn.softmax(s, axis=-1)
        return jnp.einsum('bqgjk,bkgd->bqgjd', p.astype(dt), vb)

    o_win = _sweep(win_block, T // Q_BLOCK)

    g = jax.nn.sigmoid(gate_logits.astype(jnp.float32)).astype(dt).reshape(B, T, NSA_GROUPS, NSA_HPG, 3)
    o = g[..., 0:1] * o_cmp + g[..., 1:2] * o_slc + g[..., 2:3] * o_win
    return o.reshape(B, T, NSA_Q_W)

def token_mix(h, w_in, da_lambda, da_head_norm, cmp_pos, cmp_w1, cmp_w2, w_proj_da, w_proj_nsa, w_out, lam_init):
    B, T = h.shape[0], h.shape[1]
    proj = h @ w_in
    offs = []
    acc = 0
    for w in IN_WIDTHS[:-1]:
        acc += w
        offs.append(acc)
    (q_da, k_da, v_da, q_ns, kc_raw, vc_raw, ks_raw, vs_raw, kw_raw, vw_raw,
     g_ns, g_a, g_b) = jnp.split(proj, offs, axis=-1)
    cos, sin = rope_tables(T, HEAD_DIM)
    y_da = diff_attention(q_da.reshape(B, T, DA_HEADS, 2, HEAD_DIM),
                          k_da.reshape(B, T, DA_HEADS, 2, HEAD_DIM),
                          v_da.reshape(B, T, DA_HEADS, DA_V_DIM),
                          cos, sin, da_lambda, da_head_norm, lam_init)
    kv = lambda a: a.reshape(B, T, NSA_GROUPS, HEAD_DIM)
    y_ns = nsa(q_ns.reshape(B, T, NSA_GROUPS, NSA_HPG, HEAD_DIM),
               kv(kc_raw), kv(vc_raw), kv(ks_raw), kv(vs_raw), kv(kw_raw), kv(vw_raw),
               g_ns, cos, sin, cmp_pos, cmp_w1, cmp_w2)
    merged = jax.nn.sigmoid(g_a) * (y_da @ w_proj_da) + jax.nn.sigmoid(g_b) * (y_ns @ w_proj_nsa)
    return merged @ w_out

def first_inputs(seed: int = 0) -> dict:
    key = jax.random.key(seed)
    ks = jax.random.split(key, 24)
    f32 = jnp.float32

    def w(k, shape, fan_in):
        return jax.random.normal(k, shape, f32) * fan_in ** -0.5

    def gain(k, shape):
        return 1.0 + 0.05 * jax.random.normal(k, shape, f32)

    return {
        'x': jax.random.normal(ks[0], (BATCH, SEQ, D_MODEL), f32),
        'ffn1_norm': gain(ks[1], (DEPTH, D_MODEL)),
        'ffn1_w1': w(ks[2], (DEPTH, D_MODEL, D_FF), D_MODEL),
        'ffn1_w3': w(ks[3], (DEPTH, D_MODEL, D_FF), D_MODEL),
        'ffn1_w2': w(ks[4], (DEPTH, D_FF, D_MODEL), D_FF),
        'mix_norm': gain(ks[5], (DEPTH, D_MODEL)),
        'w_in': w(ks[6], (DEPTH, D_MODEL, D_IN), D_MODEL),
        'da_lambda': 0.1 * jax.random.normal(ks[7], (DEPTH, 4, HEAD_DIM), f32),
        'da_head_norm': gain(ks[8], (DEPTH, DA_HEADS, DA_V_DIM)),
        'cmp_pos': 0.1 * jax.random.normal(ks[9], (DEPTH, 2, CMP_BLOCK, HEAD_DIM), f32),
        'cmp_w1': w(ks[10], (DEPTH, 2, CMP_BLOCK * HEAD_DIM, CMP_HIDDEN), CMP_BLOCK * HEAD_DIM),
        'cmp_w2': w(ks[11], (DEPTH, 2, CMP_HIDDEN, HEAD_DIM), CMP_HIDDEN),
        'w_proj_da': w(ks[12], (DEPTH, DA_V_W, D_MODEL), DA_V_W),
        'w_proj_nsa': w(ks[13], (DEPTH, NSA_Q_W, D_MODEL), NSA_Q_W),
        'w_out': w(ks[14], (DEPTH, D_MODEL, D_MODEL), D_MODEL),
        'ffn2_norm': gain(ks[15], (DEPTH, D_MODEL)),
        'ffn2_w1': w(ks[16], (DEPTH, D_MODEL, D_FF), D_MODEL),
        'ffn2_w3': w(ks[17], (DEPTH, D_MODEL, D_FF), D_MODEL),
        'ffn2_w2': w(ks[18], (DEPTH, D_FF, D_MODEL), D_FF),
        'final_norm': gain(ks[19], (D_MODEL,)),
    }

def first_block(x, ffn1_norm, ffn1_w1, ffn1_w3, ffn1_w2, mix_norm, w_in, da_lambda, da_head_norm,
              cmp_pos, cmp_w1, cmp_w2, w_proj_da, w_proj_nsa, w_out,
              ffn2_norm, ffn2_w1, ffn2_w3, ffn2_w2, final_norm):
    for l in range(DEPTH):
        lam_init = 0.8 - 0.6 * math.exp(-0.3 * l)
        h = rmsnorm(x, ffn1_norm[l])
        x = x + 0.5 * swiglu(h, ffn1_w1[l], ffn1_w3[l], ffn1_w2[l])
        h = rmsnorm(x, mix_norm[l])
        x = x + token_mix(h, w_in[l], da_lambda[l], da_head_norm[l], cmp_pos[l], cmp_w1[l], cmp_w2[l],
                          w_proj_da[l], w_proj_nsa[l], w_out[l], lam_init)
        h = rmsnorm(x, ffn2_norm[l])
        x = x + 0.5 * swiglu(h, ffn2_w1[l], ffn2_w3[l], ffn2_w2[l])
    return rmsnorm(x, final_norm)


DEPTH_2 = 2

N_A_LAYERS = DEPTH_2 // 2
N_B_LAYERS = DEPTH_2 - N_A_LAYERS
CONV_WIDTH = 31
N_HEADS = 16
HEAD_DIM_2 = D_MODEL // N_HEADS
D_FF_2 = 4 * D_MODEL
D_PLE = 256
NEG_BIG = -1e30


def rmsnorm_2(x, g):
    xf = x.astype(jnp.float32)
    y = xf * lax.rsqrt(jnp.mean(xf * xf, axis=-1, keepdims=True) + EPS)
    return (y * g.astype(jnp.float32)).astype(x.dtype)

def layernorm(x, g, b):
    xf = x.astype(jnp.float32)
    mu = jnp.mean(xf, axis=-1, keepdims=True)
    xc = xf - mu
    var = jnp.mean(xc * xc, axis=-1, keepdims=True)
    y = xc * lax.rsqrt(var + EPS)
    return (y * g.astype(jnp.float32) + b.astype(jnp.float32)).astype(x.dtype)

def conformer_conv(hn, w_pw1, b_pw1, w_dw, b_dw, ln_g, ln_b, w_pw2, b_pw2):
    u = hn @ w_pw1 + b_pw1
    a, g = jnp.split(u, 2, axis=-1)
    u = a * jax.nn.sigmoid(g)
    kern = w_dw[:, None, :].astype(u.dtype)
    u = lax.conv_general_dilated(
        u, kern, window_strides=(1,), padding=((CONV_WIDTH - 1, 0),),
        dimension_numbers=("NWC", "WIO", "NWC"),
        feature_group_count=D_MODEL) + b_dw
    u = layernorm(u, ln_g, ln_b)
    u = jax.nn.silu(u)
    return u @ w_pw2 + b_pw2

def shared_kv(h, kv_norm, w_kvf, b_f):
    B, S, _ = h.shape
    u = rmsnorm_2(h, kv_norm) @ w_kvf
    k = u[..., :D_MODEL].reshape(B, S, N_HEADS, HEAD_DIM_2)
    v = u[..., D_MODEL:2 * D_MODEL].reshape(B, S, N_HEADS, HEAD_DIM_2)
    f_logit = (u[..., 2 * D_MODEL:] + b_f).astype(jnp.float32)
    log_f = jax.nn.log_sigmoid(f_logit)
    c = jnp.cumsum(log_f, axis=1)
    return k, v, jnp.transpose(c, (0, 2, 1))

def fox_attention(hn, w_q, w_o, k, v, c_bhs):
    B, S, _ = hn.shape
    nb = S // Q_BLOCK
    q = (hn @ w_q).reshape(B, S, N_HEADS, HEAD_DIM_2) * (HEAD_DIM_2 ** -0.5)
    qb = jnp.transpose(q.reshape(B, nb, Q_BLOCK, N_HEADS, HEAD_DIM_2), (1, 0, 2, 3, 4))
    cb = jnp.transpose(c_bhs.reshape(B, N_HEADS, nb, Q_BLOCK), (2, 0, 1, 3))
    k_pos = jnp.arange(S)

    def one_block(args):
        q_blk, c_blk, i = args
        s = jnp.einsum("bqhd,bkhd->bhqk", q_blk, k,
                       preferred_element_type=jnp.float32)
        bias = c_blk[:, :, :, None] - c_bhs[:, :, None, :]
        q_pos = i * Q_BLOCK + jnp.arange(Q_BLOCK)
        causal = k_pos[None, :] <= q_pos[:, None]
        s = jnp.where(causal, s + bias, NEG_BIG)
        pr = jax.nn.softmax(s, axis=-1)
        return jnp.einsum("bhqk,bkhd->bqhd", pr.astype(v.dtype), v)

    o = lax.map(one_block, (qb, cb, jnp.arange(nb)))
    o = jnp.transpose(o, (1, 0, 2, 3, 4)).reshape(B, S, D_MODEL)
    return o @ w_o

def second_inputs(seed: int = 0) -> dict:
    key = jax.random.key(seed)
    ks = jax.random.split(key, 32)
    f32 = jnp.float32
    nrm = lambda k, shape, scale: (jax.random.normal(k, shape, f32) * scale)
    gain = lambda k, shape: 1.0 + 0.05 * jax.random.normal(k, shape, f32)
    D = D_MODEL
    x = jax.random.normal(ks[0], (BATCH, SEQ, D), f32)
    p = jax.random.normal(ks[1], (DEPTH_2, BATCH, SEQ, D_PLE), f32)
    mix_norm = gain(ks[2], (DEPTH_2, D))
    conv_w_pw1 = nrm(ks[3], (N_A_LAYERS, D, 2 * D), D ** -0.5)
    conv_b_pw1 = nrm(ks[4], (N_A_LAYERS, 2 * D), 0.02)
    conv_w_dw = nrm(ks[5], (N_A_LAYERS, CONV_WIDTH, D), CONV_WIDTH ** -0.5)
    conv_b_dw = nrm(ks[6], (N_A_LAYERS, D), 0.02)
    conv_ln_g = gain(ks[7], (N_A_LAYERS, D))
    conv_ln_b = nrm(ks[8], (N_A_LAYERS, D), 0.02)
    conv_w_pw2 = nrm(ks[9], (N_A_LAYERS, D, D), 0.5 * D ** -0.5)
    conv_b_pw2 = nrm(ks[10], (N_A_LAYERS, D), 0.02)
    kv_norm = gain(ks[11], (D,))
    w_kvf = jnp.concatenate([
        nrm(ks[12], (D, 2 * D), D ** -0.5),
        nrm(ks[13], (D, N_HEADS), 0.1 * D ** -0.5),
    ], axis=1)
    b_f = jax.random.uniform(ks[14], (N_HEADS,), f32, 1.0, 6.0)
    attn_w_q = nrm(ks[15], (N_B_LAYERS, D, D), D ** -0.5)
    attn_w_o = nrm(ks[16], (N_B_LAYERS, D, D), 0.5 * D ** -0.5)
    ffn_norm = gain(ks[17], (DEPTH_2, D))
    ffn_w1 = nrm(ks[18], (DEPTH_2, D, D_FF_2), D ** -0.5)
    ffn_w2 = nrm(ks[19], (DEPTH_2, D_FF_2, D), 0.5 * D_FF_2 ** -0.5)
    ple_norm = gain(ks[20], (DEPTH_2, D))
    ple_w_gate = nrm(ks[21], (DEPTH_2, D, D), D ** -0.5)
    ple_w_proj = nrm(ks[22], (DEPTH_2, D_PLE, D), 0.5 * D_PLE ** -0.5)
    final_norm = gain(ks[23], (D,))
    return {"x": x, "p": p, "mix_norm": mix_norm,
            "conv_w_pw1": conv_w_pw1, "conv_b_pw1": conv_b_pw1,
            "conv_w_dw": conv_w_dw, "conv_b_dw": conv_b_dw,
            "conv_ln_g": conv_ln_g, "conv_ln_b": conv_ln_b,
            "conv_w_pw2": conv_w_pw2, "conv_b_pw2": conv_b_pw2,
            "kv_norm": kv_norm, "w_kvf": w_kvf, "b_f": b_f,
            "attn_w_q": attn_w_q, "attn_w_o": attn_w_o,
            "ffn_norm": ffn_norm, "ffn_w1": ffn_w1, "ffn_w2": ffn_w2,
            "ple_norm": ple_norm, "ple_w_gate": ple_w_gate, "ple_w_proj": ple_w_proj,
            "final_norm": final_norm}

def second_block(x, p, mix_norm, conv_w_pw1, conv_b_pw1, conv_w_dw, conv_b_dw,
              conv_ln_g, conv_ln_b, conv_w_pw2, conv_b_pw2, kv_norm, w_kvf, b_f,
              attn_w_q, attn_w_o, ffn_norm, ffn_w1, ffn_w2, ple_norm, ple_w_gate,
              ple_w_proj, final_norm):
    h = x
    k = v = c_bhs = None
    for i in range(DEPTH_2):
        hn = rmsnorm_2(h, mix_norm[i])
        if i < N_A_LAYERS:
            h = h + conformer_conv(hn, conv_w_pw1[i], conv_b_pw1[i], conv_w_dw[i],
                                   conv_b_dw[i], conv_ln_g[i], conv_ln_b[i],
                                   conv_w_pw2[i], conv_b_pw2[i])
        else:
            j = i - N_A_LAYERS
            if j == 0:
                k, v, c_bhs = shared_kv(h, kv_norm, w_kvf, b_f)
            h = h + fox_attention(hn, attn_w_q[j], attn_w_o[j], k, v, c_bhs)
        hn = rmsnorm_2(h, ffn_norm[i])
        h = h + jnp.square(jax.nn.relu(hn @ ffn_w1[i])) @ ffn_w2[i]
        gate = jax.nn.sigmoid(rmsnorm_2(h, ple_norm[i]) @ ple_w_gate[i])
        h = h + gate * (p[i] @ ple_w_proj[i])
    return rmsnorm_2(h, final_norm)


def setup_inputs(seed=0):
    out = dict(first_inputs(seed))
    for name, value in second_inputs(seed + 1).items():
        if name != "x":
            out[name + "_2"] = value
    return out


def reference(
    x, ffn1_norm, ffn1_w1, ffn1_w3, ffn1_w2, mix_norm, w_in, da_lambda, da_head_norm, cmp_pos,
    cmp_w1, cmp_w2, w_proj_da, w_proj_nsa, w_out, ffn2_norm, ffn2_w1, ffn2_w3, ffn2_w2,
    final_norm, p_2, mix_norm_2, conv_w_pw1_2, conv_b_pw1_2, conv_w_dw_2, conv_b_dw_2,
    conv_ln_g_2, conv_ln_b_2, conv_w_pw2_2, conv_b_pw2_2, kv_norm_2, w_kvf_2, b_f_2, attn_w_q_2,
    attn_w_o_2, ffn_norm_2, ffn_w1_2, ffn_w2_2, ple_norm_2, ple_w_gate_2, ple_w_proj_2,
    final_norm_2,
):
    x = first_block(
        x, ffn1_norm, ffn1_w1, ffn1_w3, ffn1_w2, mix_norm, w_in, da_lambda, da_head_norm,
        cmp_pos, cmp_w1, cmp_w2, w_proj_da, w_proj_nsa, w_out, ffn2_norm, ffn2_w1, ffn2_w3,
        ffn2_w2, final_norm,
    )
    return second_block(
        x, p_2, mix_norm_2, conv_w_pw1_2, conv_b_pw1_2, conv_w_dw_2, conv_b_dw_2, conv_ln_g_2,
        conv_ln_b_2, conv_w_pw2_2, conv_b_pw2_2, kv_norm_2, w_kvf_2, b_f_2, attn_w_q_2,
        attn_w_o_2, ffn_norm_2, ffn_w1_2, ffn_w2_2, ple_norm_2, ple_w_gate_2, ple_w_proj_2,
        final_norm_2,
    )


_drawn_inputs = setup_inputs


def setup_inputs(seed=0):
    import zlib

    import numpy as np

    out = dict(_drawn_inputs(seed))
    spreads = {}
    factors = {'da_head_norm': 2.89,
     'cmp_pos': 3.552,
     'ffn2_norm': 3.022,
     'mix_norm_2': 3.41,
     'conv_b_pw1_2': 8.0,
     'conv_b_dw_2': 4.125,
     'conv_ln_g_2': 3.139,
     'conv_ln_b_2': 8.0,
     'conv_b_pw2_2': 2.698,
     'kv_norm_2': 5.931,
     'ple_norm_2': 8.0}
    for name, (base, spread) in spreads.items():
        noise = np.random.default_rng([zlib.crc32(name.encode()), seed]).standard_normal(out[name].shape)
        drawn = base * np.exp(spread * noise) if base else spread * noise
        out[name] = __import__('jax').numpy.asarray(drawn.astype(out[name].dtype))
    for name, factor in factors.items():
        out[name] = (out[name] * factor).astype(out[name].dtype)
    return out
```

```python
from contextlib import ExitStack

import numpy as np
import concourse.bass as bass
from concourse import mybir

F32 = mybir.dt.float32
F32R = mybir.dt.float32r
BF16 = mybir.dt.bfloat16
ALU = mybir.AluOpType
ACT = mybir.ActivationFunctionType
AX_X = mybir.AxisListType.X

P = 128
T = 256
TT = T // P
D = 1024
KD = D // P
F1 = 2816
F2 = 4096
CH = 512
RING = 4
UNIT = 4 * CH
AHEAD = 2
EPS = 1e-6
NEG = -1e30
N_CMP = 15
TAPS = 31
LAM_INIT = 0.2
QSCALE = 0.125
HEADS = 16

IN_KV = 4 * D
IN_KW = IN_KV + CH
KW_W = 256 + 48
IN_GATES = IN_KW + KW_W

GAINS = ["ffn1_norm", "mix_norm", "ffn2_norm", "mix_norm_2.0", "mix_norm_2.1", "kv_norm_2", "ffn_norm_2.0",
         "ffn_norm_2.1", "ple_norm_2.0", "ple_norm_2.1", "conv_ln_g_2", "conv_ln_b_2", "conv_b_dw_2", "da_head_norm"]
GAIN = {n: i for i, n in enumerate(GAINS)}


def constants():
    f = np.float32
    parts, at, off = [], {}, 0

    def put(name, a):
        nonlocal off
        a = np.asarray(a, f).reshape(P, -1)
        at[name] = (off, a.shape[1])
        off += a.shape[1]
        parts.append(a)

    i = np.arange(P)
    put("ident", np.eye(P))
    tri = (i[:, None] <= i[None, :])
    put("inv_d", np.full((P, P), 1.0 / D))
    put("tri", np.concatenate([np.zeros((P, P)), tri, np.ones((P, P))], 1))
    inv = (1.0 / (f(10000.0) ** (np.arange(0, 64, 2, dtype=f) / f(64)))).astype(f)
    pos = (i[:, None] + P * np.arange(TT)[None, :]).astype(f)
    ang = (pos[:, :, None] * inv).astype(f)
    put("cos", np.concatenate([np.cos(ang), np.cos(ang)], 2))
    put("sin", np.concatenate([-np.sin(ang), np.sin(ang)], 2))
    n = np.arange(16)
    valid = (n[None, None, :] * 16 + 31 <= pos[:, :, None]) & (n < N_CMP)
    put("cmask", np.where(valid, 0.0, NEG))
    put("cvalid", valid)
    put("onehot_c", (i[:, None] - 16 == n[None, :]))
    put("onehot_1", (i[:, None] == n[None, :]))
    put("left_scale", (i < 16))
    put("left_shift", np.where((i >= 16) & (i < 32), -1.0, 0.0))
    put("causal", np.where(i[None, :] <= i[:, None], 0.0, NEG))
    return np.concatenate(parts, 1), at


CONST_AT = constants()[1]
N_CONST = CONST_AT["causal"][0]


class Chunk:

    def __init__(self, cols, width, units, reader="dve"):
        self.cols, self.width, self.units, self.reader = cols, width, units, reader
        self.second = {}


def plan(W):
    def kview(w):
        return w.rearrange("(kt p) n -> p kt n", p=P)

    def layer(name, chunks):
        for c in chunks:
            c.index = len(order)
            order.append(c)
            c.u0 = len(units)
            k = 0
            for nk in c.units:
                units.append((c, k, nk))
                k += nk
        layers[name] = chunks

    def plain(w, n, k_units, width=CH, start=0, reader="dve"):
        v = kview(w)
        return [Chunk([(v, start + i * width)], width, k_units, reader) for i in range(n)]

    def dual(a, b, n, b0=0):
        return [Chunk([(kview(a), i * 256), (kview(b), b0 + i * 256)], 256, [4, 4]) for i in range(n)]

    layers, order, units = {}, [], []
    kd, kf1, kf2 = [4, 4], [4] * 5 + [2], [4] * 8
    layer("ffn1_up", dual(W["ffn1_w1"][0], W["ffn1_w3"][0], F1 // 256))
    layer("ffn1_down", plain(W["ffn1_w2"][0], 2, kf1))
    w_in = W["w_in"][0]
    layer("in_a", plain(w_in, 8, kd))
    layer("in_b", plain(w_in, 1, kd, CH, IN_KV) + plain(w_in, 1, kd, KW_W, IN_KW))
    layer("cmp", [plain(W["cmp_w1"][0, i], 1, [8, 8], 256, 0, "act")[0] for i in range(2)])
    layer("gates", plain(w_in, 4, kd, CH, IN_GATES, "act"))
    layer("proj_da", plain(W["w_proj_da"][0], 2, kd))
    layer("proj_ns", plain(W["w_proj_nsa"][0], 2, kd))
    layer("out", plain(W["w_out"][0], 2, kd))
    layer("ffn2_up", dual(W["ffn2_w1"][0], W["ffn2_w3"][0], F1 // 256))
    layer("ffn2_down", plain(W["ffn2_w2"][0], 2, kf1))
    pw1 = W["conv_w_pw1_2"][0]
    layer("pw1", dual(pw1, pw1, 4, D))
    layer("pw2", plain(W["conv_w_pw2_2"][0], 2, kd))
    for i in range(2):
        layer(f"up{i}", plain(W["ffn_w1_2"][i], F2 // CH, kd))
        layer(f"down{i}", plain(W["ffn_w2_2"][i], 2, kf2))
        gate = plain(W["ple_w_gate_2"][i], 2, kd, reader="act")
        proj = plain(W["ple_w_proj_2"][i], 2, [2])
        layer(f"ple{i}", [gate[0], proj[0], gate[1], proj[1]])
        if i == 0:
            layer("kv", plain(W["w_kvf_2"], 4, kd))
            layer("f", plain(W["w_kvf_2"], 1, [8], HEADS, 2 * D))
            layer("q", plain(W["attn_w_q_2"][0], 2, kd))
            layer("o", plain(W["attn_w_o_2"][0], 2, kd))
    on_slot = [0] * RING
    for u, (c, _, _) in enumerate(units):
        if len(c.cols) == 2:
            on_slot[u % RING] += 1
        c.second[u] = on_slot[u % RING]
    read = {"dve": 0, "act": 0}
    for c in order:
        read[c.reader] += 1
        c.nth_read = read[c.reader]
    return layers, order, units


T_GROUPS = [("norm0", 4), ("ffn1_up", 11), ("norm1", 4), ("y_da", 4), ("y_ns", 4), ("m", 4), ("norm2", 4),
            ("ffn2_up", 11), ("norm3", 4), ("norm4", 4), ("up0", 16), ("norm5", 4), ("emb0", 1), ("norm6", 4),
            ("norm6q", 4), ("y_fox", 4), ("norm7", 4), ("up1", 16), ("norm8", 4), ("emb1", 1)]
T_AT = {}
_n = 0
for _name, _k in T_GROUPS:
    T_AT[_name] = _n
    _n += _k

A_GROUPS = [("const", 4), ("raw_cmp", 2), ("kk", 2), ("q_cmp", 4), ("hidden_cmp", 1), ("kc", 1), ("vc", 1), ("s_cmp", 1),
            ("p_cmp", 2), ("qk_da", 8), ("q_ns", 4), ("glu", 4), ("qk_fox", 8), ("cum", 1)]
A_AT = {}
_n = 0
for _name, _k in A_GROUPS:
    A_AT[_name] = _n
    _n += _k


ACT_PARTS = {"ffn1_up": 0, "ffn2_up": 11, "pw1": 22, "up0": 26, "up1": 34}


class Steps:

    def __init__(self, eng, sem):
        self.eng, self.sem, self.n, self.loop = eng, sem, 0, 0

    def done(self, ins):
        ins.then_inc(self.sem, 1)
        self.n += 1
        self.eng.wait_ge(self.sem, self.n + self.loop)


def block_kernel(nc, W, consts, out):
    layers, order, units = plan(W)
    with ExitStack() as ctx:
        sb = lambda n, s, d=F32: ctx.enter_context(nc.sbuf_tensor(n, s, d))
        sem = lambda n: ctx.enter_context(nc.semaphore(n))

        def scoped(*specs):
            with ExitStack() as c:
                return [c.enter_context(nc.sbuf_tensor(n, sh, d)) for n, sh, d in specs]

        raw = sb("raw", [P, RING, UNIT])
        w_hi = sb("w_hi", [P, RING, UNIT], F32R)
        w_lo = sb("w_lo", [P, RING, UNIT], F32R)
        x = sb("x", [P, TT, D])
        hT_hi = sb("hT_hi", [P, KD, T], F32R)
        hT_lo = sb("hT_lo", [P, KD, T], F32R)
        blocks_hi, blocks_lo = scoped(("blocks_hi", [P, 2, 16, 30], F32R), ("blocks_lo", [P, 2, 16, 30], F32R))
        xn = sb("xn", [P, TT, D])
        s = sb("s", [P, 2, TT, CH])
        cst = sb("cst", [P, N_CONST])
        identb = sb("identb", [P, P], BF16)
        causalb = sb("causalb", [P, 2 * P], BF16)
        gcol = sb("gcol", [P, len(GAINS), KD])
        taps = sb("taps", [P, KD, TAPS])
        sums = sb("sums", [P, 4])
        mean = sb("mean", [P, 4])
        rstd = sb("rstd", [P, 4])
        half = sb("half", [P, 32])
        pos = sb("pos", [P, 2, 16])
        lam = sb("lam", [P, 8])
        negmax = sb("negmax", [P, 2, 4])
        rowsum = sb("rowsum", [P, 8, 4])
        rowinv = sb("rowinv", [P, 8, 4])
        weight = sb("weight", [P, 2, 4])

        gT_hi, gT_lo = scoped(("gT_hi", [P, F2 // P, T], F32R), ("gT_lo", [P, F2 // P, T], F32R))
        with ExitStack() as mix:
            msb = lambda n, sh, d=F32: mix.enter_context(nc.sbuf_tensor(n, sh, d))
            mixbuf = msb("mixbuf", [P, 4, TT, CH])
            yT_hi, yT_lo, gatebuf, m_buf = scoped(("yT_hi", [P, KD, T], F32R), ("yT_lo", [P, KD, T], F32R),
                                                  ("gatebuf", [P, 4, TT, CH], F32), ("m_buf", [P, TT, D], F32))
            v_da = msb("v_da", [P, TT, D])
            qa = msb("qa", [P, TT, D])
            qr = msb("qr", [P, TT, D])
            kT = msb("kT", [P, KD, T])
            ksT = msb("ksT", [P, 2, T])
            kwT = msb("kwT", [P, 2, T])
            vs = msb("vs", [P, TT, P])
            vw = msb("vw", [P, TT, P])
            gl = msb("gl", [P, TT, 48])
            gates = msb("gates", [P, TT, 48])
            w2k = msb("w2k", [P, 2, 2, 64])
            w2v = msb("w2v", [P, 2, 64])
            kcT = msb("kcT", [P, 2, 16])
            vcb = msb("vcb", [P, 2, 4, 64])
            g1k = msb("g1k", [P, 2, 2, 16])
            g1v = msb("g1v", [P, 2, 2, 4, 32])
            cstat = msb("cstat", [P, 3, TT * HEADS])
            pcT = msb("pcT", [P, TT, 4, P])
        ubuf, conv, sq, b_pw1, stat, b_pw2 = scoped(
            ("ubuf", [P, KD, TAPS - 1 + T], F32), ("conv", [P, KD, T], F32), ("sq", [P, KD, T], F32),
            ("b_pw1", [P, 2 * D], F32), ("stat", [P, 2, T], F32), ("b_pw2", [P, D], F32))
        qf, kf, vf, qT, kTf, bias_r, bias_l, cum, fz, lfd, b_f = scoped(
            ("qf", [P, TT, D], F32), ("kf", [P, TT, D], F32), ("vf", [P, TT, D], F32), ("qT", [P, KD, T], F32),
            ("kTf", [P, KD, T], F32), ("bias_r", [P, HEADS, T], F32), ("bias_l", [P, T], F32), ("cum", [32, T], F32),
            ("fz", [P, 4, TT, HEADS], F32), ("lfd", [P, TT, 2, HEADS], F32), ("b_f", [P, HEADS], F32))
        emb, eT_hi, eT_lo = scoped(("emb", [P, TT, 256], F32), ("eT_hi", [P, 2, T], F32R), ("eT_lo", [P, 2, T], F32R))
        qaT = qa[:].rearrange("p a b -> p (a b)").rearrange("p (k t) -> p k t", t=T)
        y_mix = mixbuf[:].rearrange("p a b c -> p (a b c)").rearrange("p (i t n) -> p i t n", i=2, t=TT)
        blk_full = s[:].rearrange("p a b c -> p (a b c)")[:, 0:960].rearrange("p (v j r) -> p v j r", v=2, j=16)
        g1 = s[:].rearrange("p a b c -> p (a b c)")[:, 1024:1536].rearrange("p (v n) -> p v n", v=2)
        sc = s[:].rearrange("p a b c -> p (a b c)")[:, 0:512].rearrange("p (t b h n) -> p t b h n", t=TT, b=2, h=8)
        pc = xn[:].rearrange("p a b -> p (a b)")[:, 0:1024].rearrange("p (t h n) -> p t h n", t=TT, h=HEADS)
        kvd = xn[:].rearrange("p t (v g u d) -> p t v g u d", v=4, g=2, u=2)
        probs = s[:].rearrange("p a b c -> p a (b c)")
        probsT = xn
        rows_g = s[:].rearrange("p a b c -> p (a b c)")[:, 1024:1152]
        rows_w = s[:].rearrange("p a b c -> p (a b c)")[:, 0:1024]
        lam_in = s[:].rearrange("p a b c -> p (a b c)")[:, 1536:1792].rearrange("p (a d) -> p a d", a=4)
        causal_in = s[:].rearrange("p a b c -> p (a b c)")[:, 1408:1536]
        rows_p = s[:].rearrange("p a b c -> p (a b c)")[:, 1152:1408]
        cin = [s[:].rearrange("p a b c -> p (a b c)")[:, 1536 + 256 * k:1792 + 256 * k].rearrange("p (g m) -> p g m", g=2)
               for k in range(2)]
        fin_gain = s[:].rearrange("p a b c -> p a (b c)")
        ps = ctx.enter_context(nc.psum_tensor("ps", [P, 8, CH], F32))
        psT = ps[:, 4:8, :]

        def rot_tmp(t):
            return s[:].rearrange("p a b c -> p (a b c)")[:, 1536 + P * t:1536 + P * (t + 1)]

        def const(name):
            o, w = CONST_AT[name]
            return cst[:, o:o + w]

        ident = const("ident")
        tri = const("tri")
        cos = const("cos").rearrange("p (t d) -> p t d", t=TT)
        sin = const("sin").rearrange("p (t d) -> p t d", t=TT)
        cmask = const("cmask").rearrange("p (t n) -> p t n", t=TT)
        cvalid = const("cvalid").rearrange("p (t n) -> p t n", t=TT)

        raw_a = [sem(f"raw_a{i}") for i in range(RING)]
        raw_b = [sem(f"raw_b{i}") for i in range(RING)]
        hi_ready = sem("hi_ready")
        lo_ready = sem("lo_ready")
        unit_used = sem("unit_used")
        read_dve = sem("read_dve")
        read_act = sem("read_act")
        act_part = sem("act_part")
        bias_in = sem("bias_in")
        g_ready = sem("g_ready")
        tr_done = sem("tr_done")
        t_hi = sem("t_hi")
        t_lo = sem("t_lo")
        aux_tr = sem("aux_tr")
        aux_cp = sem("aux_cp")
        dve_step = sem("dve_step")
        pool_step = sem("pool_step")
        act_step = sem("act_step")
        x_in = sem("x_in")
        const_in = sem("const_in")
        consts_ready = sem("consts_ready")
        x_ready = sem("x_ready")
        sum_dve = sem("sum_dve")
        sum_act = sem("sum_act")
        rstd_ready = sem("rstd_ready")
        xn_ready = sem("xn_ready")
        lam_sum = sem("lam_sum")
        lam_exp = sem("lam_exp")
        kv_ready = sem("kv_ready")
        blocks_ready = sem("blocks_ready")
        w2_in = sem("w2_in")
        cmp_sub = sem("cmp_sub")
        cmp_exp = sem("cmp_exp")
        cmp_p = sem("cmp_p")
        gl_ready = sem("gl_ready")
        gates_ready = sem("gates_ready")
        scores_done = sem("scores_done")
        max_done = sem("max_done")
        exp_done = sem("exp_done")
        probs_ready = sem("probs_ready")
        probs_tr = sem("probs_tr")
        probsT_ready = sem("probsT_ready")
        pv_done = sem("pv_done")
        o_read = sem("o_read")
        y_sum = sem("y_sum")
        y_rstd = sem("y_rstd")
        conv_in = sem("conv_in")
        tile_in = sem("tile_in")
        conv_dve = sem("conv_dve")
        conv_pool = sem("conv_pool")
        mean_done = sem("mean_done")
        centred = sem("centred")
        squared = sem("squared")
        var_done = sem("var_done")
        std_ready = sem("std_ready")
        normed = sem("normed")
        silu_done = sem("silu_done")
        cT_hi = sem("cT_hi")
        cT_lo = sem("cT_lo")
        emb_in = sem("emb_in")
        bf_in = sem("bf_in")
        f_abs = sem("f_abs")
        f_exp = sem("f_exp")
        f_ln = sem("f_ln")
        lf_ready = sem("lf_ready")
        zero_ready = sem("zero_ready")
        bias_rows = sem("bias_rows")
        fin_in = sem("fin_in")
        r_free = sem("r_free")
        out_ready = sem("out_ready")
        out_done = sem("out_done")

        def unit_view(t, u_slot, nk, w):
            return t[:, u_slot, 0:nk * w].rearrange("p (k w) -> p k w", w=w)

        def width(c):
            return c.width * len(c.cols)

        def first_unit(name):
            return layers[name][0].u0

        def pairs(name, lag):
            n = len(layers[name])
            loops = (n - lag) // 2
            return n, loops

        block = ctx.enter_context(nc.Block())

        @block.sync
        def _(sp):
            xv = W["x"].rearrange("b (t p) d -> p (b t) d", p=P)
            sp.dma_start(x[:], xv).then_inc(x_in, 16)

            def load(u, i=None, step=0, per=0, turns=0):
                c, k0, nk = units[u]
                shift = 0 if i is None else i
                if u >= RING or i is not None:
                    sp.wait_ge(lo_ready, u + 1 + per * shift)
                for q, (v, col) in enumerate(c.cols):
                    dst = raw[:, u % RING, 0:nk * width(c)].rearrange("p (k h w) -> p k h w", k=nk, w=c.width)[:, :, q, :]
                    cols = slice(col, col + c.width) if i is None else bass.ds(col + step * i, c.width)
                    sp.dma_start(dst, v[:, k0:k0 + nk, cols]).then_inc((raw_a, raw_b)[q][u % RING], 16)

            for name, chunks in layers.items():
                n, loops = pairs(name, 0)
                if n >= 4 and not name.startswith("ple"):
                    with sp.Fori(0, loops) as i:
                        for c in chunks[0:2]:
                            for u in range(c.u0, c.u0 + 2):
                                load(u, i, 2 * c.width, 4)
                    rest = chunks[2 * loops:]
                else:
                    rest = chunks
                for c in rest:
                    for u in range(c.u0, c.u0 + len(c.units)):
                        load(u)
            sp.wait_ge(out_ready, 1)
            sp.dma_start(out.rearrange("b (t p) d -> p (b t) d", p=P), x[:]).then_inc(out_done, 16)
            sp.wait_ge(out_done, 16)

        def split_shape(u):
            c, _, nk = units[u]
            return slice(0, nk * width(c))

        NORM = {n: i for i, n in enumerate(["norm0", "norm1", "norm2", "fin0", "norm3", "norm4", "norm5", "norm6",
                                            "norm7", "norm8", "fin1"])}
        SRC = {n: i + 1 for i, n in enumerate(["norm0", "norm1", "y_da", "y_ns", "m", "norm2", "norm3", "norm4",
                                               "norm5", "norm6", "y_fox", "norm7", "norm8"])}
        ATT = {"da": 0, "ns": 8, "fox": 24}
        ATT_STEPS = {"da": 4, "ns": 8, "fox": 4}
        DVE_TILES = [0, 2, 3, 5, 6]
        POOL_TILES = [1, 4, 7]

        @block.gpsimd
        def _(pool):
            g = nc.gpsimd
            steps = Steps(pool, pool_step)
            for k in range(RING):
                g.memset(half[:, k:k + 1], -0.5).then_inc(lo_ready, 1)
            for k in range(RING):
                g.memset(half[:, RING + k:RING + k + 1], -0.5).then_inc(unit_used, 1)
            for k in range(2):
                g.memset(half[:, 8 + k:9 + k], -0.5).then_inc(read_dve, 1)
                g.memset(half[:, 10 + k:11 + k], -0.5).then_inc(read_act, 1)
                g.memset(half[:, 12 + k:13 + k], -0.5).then_inc(t_lo, 1)
            steps.done(g.memset(half[:, 14:32], -0.5))

            def rsqrt(n, name):
                pool.wait_ge(sum_dve, n + 1)
                pool.wait_ge(sum_act, n + 1)
                steps.done(g.tensor_scalar(mean[:, 0:2], sums[:, 0:2], 1.0 / D, EPS, ALU.mult, ALU.add))
                g.tensor_tensor(out=rstd[:, 0:2], in0=mean[:, 0:2], in1=half[:, 0:2], op=ALU.pow).then_inc(rstd_ready, 1)

            rsqrt(NORM["norm0"], "norm0")
            pool.wait_ge(r_free, 1)
            w2 = W["cmp_w2"][0]
            for d_ in range(2):
                pool.dma_start(w2k[:, :, d_, :], w2[0].rearrange("(k p) d -> p k d", p=P)).then_inc(w2_in, 16)
            pool.dma_start(w2v[:], w2[1].rearrange("(k p) d -> p k d", p=P)).then_inc(w2_in, 16)
            rsqrt(NORM["norm1"], "norm1")
            pool.wait_ge(y_sum, 1)
            steps.done(g.tensor_scalar(cstat[:, 1, 0:16], cstat[:, 0, 0:16], 1.0 / P, EPS, ALU.mult, ALU.add))
            g.tensor_tensor(out=cstat[:, 2, 0:16], in0=cstat[:, 1, 0:16], in1=half[:, 0:16], op=ALU.pow).then_inc(y_rstd, 1)
            rsqrt(NORM["norm2"], "norm2")
            pool.wait_ge(r_free, 2)
            pool.dma_start(fin_gain[:, 0], W["final_norm"].rearrange("(a d) -> a d", a=1).partition_broadcast(P)).then_inc(fin_in, 16)
            pool.dma_start(b_pw1[:], W["conv_b_pw1_2"].partition_broadcast(P)).then_inc(conv_in, 16)
            pool.dma_start(b_pw2[:], W["conv_b_pw2_2"].partition_broadcast(P)).then_inc(conv_in, 16)
            g.memset(ubuf[:, :, 0:TAPS - 1], 0.0).then_inc(zero_ready, 1)
            rsqrt(NORM["fin0"], "fin0")
            rsqrt(NORM["norm3"], "norm3")
            for ct in POOL_TILES:
                pool.wait_ge(tile_in, ct // 2 + 1)
                steps.done(g.tensor_scalar(conv[:, ct], ubuf[:, ct, 0:T], taps[:, ct, 0:1],
                                           gcol[:, GAIN["conv_b_dw_2"], ct:ct + 1], ALU.mult, ALU.add))
                for k in range(1, TAPS):
                    steps.done(g.tensor_scalar(sq[:, ct], ubuf[:, ct, k:k + T], taps[:, ct, k:k + 1], 0.0,
                                               ALU.mult, ALU.add))
                    last = g.tensor_tensor(out=conv[:, ct], in0=conv[:, ct], in1=sq[:, ct], op=ALU.add)
                    if k < TAPS - 1:
                        steps.done(last)
                last.then_inc(conv_pool, 1)
            rsqrt(NORM["norm4"], "norm4")
            pool.wait_ge(r_free, 3)
            pool.dma_start(emb[:], W["p_2"][0].rearrange("b (t p) d -> p (b t) d", p=P)).then_inc(emb_in, 16)
            rsqrt(NORM["norm5"], "norm5")
            pool.wait_ge(r_free, 4)
            pool.dma_start(b_f[:], W["b_f_2"].rearrange("(a d) -> a d", a=1).partition_broadcast(P)).then_inc(bf_in, 16)
            g.memset(bias_r[:], 0.0).then_inc(zero_ready, 1)
            g.memset(bias_l[:], 0.0).then_inc(zero_ready, 1)
            rsqrt(NORM["norm6"], "norm6")
            rsqrt(NORM["norm7"], "norm7")
            pool.wait_ge(r_free, 5)
            pool.dma_start(emb[:], W["p_2"][1].rearrange("b (t p) d -> p (b t) d", p=P)).then_inc(emb_in, 16)
            rsqrt(NORM["norm8"], "norm8")
            pool.wait_ge(r_free, 6)
            pool.dma_start(fin_gain[:, 0], W["final_norm_2"].rearrange("(a d) -> a d", a=1).partition_broadcast(P)).then_inc(fin_in, 16)
            rsqrt(NORM["fin1"], "fin1")

        @block.scalar
        def _(act):
            a = nc.scalar
            loads = [(cst[:], consts[:, 0:N_CONST]), (causal_in, consts[:, N_CONST:N_CONST + P])]
            for i, n in enumerate(GAINS):
                base, _, layer = n.partition(".")
                src = W[base]
                src = src[int(layer)] if layer else src
                if base == "da_head_norm":
                    src = src[0]
                elif len(src.shape) == 2:
                    src = src[0].rearrange("(a d) -> a d", d=P)
                else:
                    src = src.rearrange("(a d) -> a d", d=P)
                loads.append((rows_g[KD * i:KD * i + KD, :], src))
            loads.append((rows_w[0:TAPS, :], W["conv_w_dw_2"][0]))
            for k in range(2):
                loads.append((rows_p[0:16, k * P:(k + 1) * P], W["cmp_pos"][0, k].rearrange("(j h) d -> j (h d)", h=2)))
            loads.append((lam_in, W["da_lambda"].rearrange("a b c -> a (b c)").partition_broadcast(P)
                          .rearrange("q p (b c) -> q (p b) c", b=4)))
            for dst, src in loads:
                act.dma_start(dst, src).then_inc(const_in, 16)
            n_const = 16 * len(loads)

            def split(u, i=None, per=0):
                c, _, _ = units[u]
                k = 0 if i is None else i
                turn = per // RING
                act.wait_ge(unit_used, u + 1 + per * k)
                act.wait_ge(raw_a[u % RING], 16 * (u // RING + 1) + 16 * turn * k)
                if len(c.cols) == 2:
                    act.wait_ge(raw_b[u % RING], 16 * c.second[u] + 16 * turn * k)
                n = split_shape(u)
                a.activation(w_hi[:, u % RING, n], raw[:, u % RING, n], ACT.Copy).then_inc(hi_ready, 1)

            def split_next(c, i=None, per=0):
                end = c.u0 + len(c.units)
                for u in range(end - len(c.units) + AHEAD, min(end + AHEAD, len(units))):
                    split(u, i, per)

            def chunk_done(c, i=None, per=0):
                act.wait_ge(unit_used, RING + c.u0 + len(c.units) + (per * i if i is not None else 0))

            def hi_group(t, dst, scale=1.0, bank=None, i=None, per=0, ordered=True):
                k = 0 if i is None else per * i
                act.wait_ge(consts_ready, 1)
                act.wait_ge(tr_done, t + 1 + k)
                return a.activation(dst, bank, ACT.Copy, scale=scale)

            def hi_groups(name, dst, gain=None, cnt=4):
                for j in range(cnt):
                    t = T_AT[name] + j
                    act.wait_ge(tr_done, t + 1)
                    bank = psT[:, j, :].rearrange("p (k t) -> p k t", k=2)
                    for k in range(2):
                        kt = 2 * j + k
                        sc_ = 1.0 if gain is None else gcol[:, GAIN[gain], kt:kt + 1]
                        ins = a.activation(dst[:, kt, :], bank[:, k, :], ACT.Copy, scale=sc_)
                    ins.then_inc(t_hi, 1)

            def norm(name, gain):
                n = NORM[name]
                act.wait_ge(x_ready, n + 1)
                a.activation(xn[:, 1, :], x[:, 1, :], ACT.Square, accum_out=sums[:, 1:2]).then_inc(sum_act, 1)
                if gain:
                    hi_groups(name, hT_hi, gain)

            def up(name, func, w):
                chunks = layers[name]
                n, loops = pairs(name, 1)
                groups = w // 256
                loops = (n - 2) // 2
                dst = gT_hi[:].rearrange("p k t -> p (k t)")

                def one(j, i=None):
                    c = chunks[j]
                    k = 0 if i is None else i
                    split_next(c, i, 4)
                    chunk_done(c, i, 4)
                    for t in range(TT):
                        ins = a.activation(s[:, c.index % 2, t, 0:w], ps[:, 2 * (c.index % 2) + t, 0:w], func)
                    ins.then_inc(act_part, 1)
                    if j > 0:
                        lag(j - 1, i)

                def lag(j, i=None):
                    for q in range(groups):
                        t = T_AT[name] + j * groups + q
                        at = (j * groups + q) * 512
                        if i is None:
                            d = dst[:, at:at + 512]
                        else:
                            d = dst[:, bass.ds(at + i * (2 * groups * 512), 512)]
                        hi_group(t, d, 1.0, psT[:, t % 2, :], i, 2 * groups).then_inc(t_hi, 1)

                one(0)
                with act.Fori(0, loops) as i:
                    one(1, i)
                    one(2, i)
                for j in range(1 + 2 * loops, n):
                    one(j)
                lag(n - 1)

            def attention(kind):
                for tok in range(TT):
                    w = P * (tok + 1)
                    for q in range(ATT_STEPS[kind]):
                        st = ATT[kind] + tok * ATT_STEPS[kind] + q
                        act.wait_ge(max_done, st + 1)
                        if st >= 2:
                            act.wait_ge(probs_tr, st - 1)
                        for b in range(2):
                            for m in range(2):
                                o = m * 2 + b if kind == "fox" else b * 2 + m
                                ins = a.activation(probs[:, st % 2, (2 * b + m) * T:(2 * b + m) * T + w],
                                                   ps[:, 2 * (st % 2) + b, m * w:m * w + w], ACT.Exp,
                                                   bias=negmax[:, st % 2, 2 * b + m:2 * b + m + 1],
                                                   accum_out=rowsum[:, st % 8, o:o + 1])
                        ins.then_inc(exp_done, 1)

            split(0)
            split(1)
            act.wait_ge(lam_sum, 1)
            a.activation(lam[:, 2:4], lam[:, 0:2], ACT.Exp).then_inc(lam_exp, 1)
            act.wait_ge(x_in, 16)
            act.wait_ge(consts_ready, 1)
            norm("norm0", "ffn1_norm")
            up("ffn1_up", ACT.Silu, 256)
            for c in layers["ffn1_down"]:
                split_next(c)
            norm("norm1", "mix_norm")
            with act.Fori(0, 4) as i:
                for c in layers["in_a"][0:2]:
                    split_next(c, i, 4)
            for c in layers["in_b"]:
                split_next(c)
            act.wait_ge(gl_ready, 1)
            a.activation(gates[:], gl[:], ACT.Sigmoid).then_inc(gates_ready, 1)
            for v, c in enumerate(layers["cmp"]):
                split_next(c)
                chunk_done(c)
                a.activation(g1[0:30, v, :], ps[0:30, 2 * (c.index % 2), 0:256], ACT.Gelu_apprx_tanh).then_inc(read_act, 1)
            act.wait_ge(cmp_sub, 1)
            a.activation(sc[:], sc[:], ACT.Exp).then_inc(cmp_exp, 1)
            attention("da")
            attention("ns")

            def gate_chunk(c, dst, i=None):
                chunk_done(c, i, 4)
                for t in range(TT):
                    ins = a.activation(dst(t), ps[:, 2 * (c.index % 2) + t, :], ACT.Sigmoid)
                ins.then_inc(read_act, 1)

            with act.Fori(0, 2) as i:
                for j, c in enumerate(layers["gates"][0:2]):
                    split_next(c, i, 4)
                    act.wait_ge(o_read, 8)
                    gate_chunk(c, lambda t, j=j, i=i: gatebuf[:].rearrange("p a b c -> p (a b c)")[
                        :, bass.ds((j * TT + t) * CH + i * (2 * TT * CH), CH)], i)
            hi_groups("y_da", yT_hi, "da_head_norm")
            for c in layers["proj_da"]:
                split_next(c)
            hi_groups("y_ns", hT_hi)
            for c in layers["proj_ns"]:
                split_next(c)
            hi_groups("m", hT_hi)
            for c in layers["out"]:
                split_next(c)
            norm("norm2", "ffn2_norm")
            up("ffn2_up", ACT.Silu, 256)
            for c in layers["ffn2_down"]:
                split_next(c)
            norm("fin0", None)
            norm("norm3", "mix_norm_2.0")
            for j, c in enumerate(layers["pw1"]):
                split_next(c)
                act.wait_ge(bias_in, j + 1)
                for t in range(TT):
                    ins = a.activation(s[:, c.index % 2, t, 256:512], s[:, c.index % 2, t, 256:512], ACT.Sigmoid)
                ins.then_inc(act_part, 1)
            act.wait_ge(centred, 1)
            a.activation(sq[:], conv[:], ACT.Square).then_inc(squared, 1)
            act.wait_ge(std_ready, 1)
            a.activation(stat[:, 1, :], stat[:, 0, :], ACT.Sqrt).then_inc(std_ready, 1)
            act.wait_ge(normed, 1)
            for ct in range(KD):
                a.activation(conv[:, ct], conv[:, ct], ACT.Silu, scale=gcol[:, GAIN["conv_ln_g_2"], ct:ct + 1],
                             bias=gcol[:, GAIN["conv_ln_b_2"], ct:ct + 1]).then_inc(silu_done, 1)
            for ct in range(KD):
                act.wait_ge(silu_done, ct + 1)
                a.activation(hT_hi[:, ct, :], conv[:, ct], ACT.Copy).then_inc(cT_hi, 1)
            for c in layers["pw2"]:
                split_next(c)

            def ffn_ple(i, n_a, n_b):
                norm(n_a, f"ffn_norm_2.{i}")
                up(f"up{i}", ACT.Relu, 512)
                for c in layers[f"down{i}"]:
                    split_next(c)
                norm(n_b, f"ple_norm_2.{i}")
                act.wait_ge(tr_done, T_AT[f"emb{i}"] + 1)
                a.activation(eT_hi[:].rearrange("p k t -> p (k t)"), psT[:, 0, :], ACT.Copy).then_inc(t_hi, 1)
                for j, c in enumerate(layers[f"ple{i}"]):
                    split_next(c)
                    if c.reader == "act":
                        gate_chunk(c, lambda t, j=j: s[:, j // 2, t, :])

            ffn_ple(0, "norm4", "norm5")
            norm("norm6", "kv_norm_2")
            with act.Fori(0, 1) as i:
                for c in layers["kv"][0:2]:
                    split_next(c, i, 4)
            for c in layers["kv"][2:] + layers["f"]:
                split_next(c)
            act.wait_ge(f_abs, 1)
            a.activation(fz[:, 2], fz[:, 1], ACT.Exp).then_inc(f_exp, 1)
            act.wait_ge(f_exp, 1)
            a.activation(fz[:, 3], fz[:, 2], ACT.Ln, bias=1.0).then_inc(f_ln, 1)
            chunk_done(layers["f"][0])
            hi_groups("norm6q", hT_hi, "mix_norm_2.1")
            for c in layers["q"]:
                split_next(c)
            attention("fox")
            hi_groups("y_fox", hT_hi)
            for c in layers["o"]:
                split_next(c)
            ffn_ple(1, "norm7", "norm8")
            norm("fin1", None)

        @block.vector
        def _(dve):
            v = nc.vector
            steps = Steps(dve, dve_step)

            def split(u, i=None, per=0):
                k = 0 if i is None else i
                dve.wait_ge(hi_ready, u + 1 + per * k)
                n = split_shape(u)
                v.tensor_tensor(w_lo[:, u % RING, n], raw[:, u % RING, n], w_hi[:, u % RING, n].bitcast(F32),
                                ALU.subtract).then_inc(lo_ready, 1)

            def split_next(c, i=None, per=0):
                end = c.u0 + len(c.units)
                for u in range(end - len(c.units) + AHEAD, min(end + AHEAD, len(units))):
                    split(u, i, per)

            def chunk_done(c, i=None, per=0):
                dve.wait_ge(unit_used, RING + c.u0 + len(c.units) + (per * i if i is not None else 0))

            def bank(c, t):
                return ps[:, 2 * (c.index % 2) + t, :]

            def lo_groups(name, hi, lo, gain=None, cnt=4):
                for j in range(cnt):
                    t = T_AT[name] + j
                    dve.wait_ge(t_hi, t + 1)
                    bk = psT[:, j, :].rearrange("p (k t) -> p k t", k=2)
                    for k in range(2):
                        kt = 2 * j + k
                        g_ = 1.0 if gain is None else gcol[:, GAIN[gain], kt:kt + 1]
                        ins = v.scalar_tensor_tensor(out=lo[:, kt, :], in0=bk[:, k, :], scalar=g_,
                                                     in1=hi[:, kt, :].bitcast(F32), op0=ALU.mult, op1=ALU.subtract)
                    ins.then_inc(t_lo, 1)

            def norm(name, gain):
                n = NORM[name]
                v.tensor_tensor_reduce(out=xn[:, 0, :], in0=x[:, 0, :], in1=x[:, 0, :], scale=1.0, scalar=0.0,
                                       op0=ALU.mult, op1=ALU.add, accum_out=sums[:, 0:1]).then_inc(sum_dve, 1)
                dve.wait_ge(rstd_ready, n + 1)
                if gain:
                    for t in range(TT):
                        ins = v.tensor_scalar(xn[:, t, :], x[:, t, :], rstd[:, t:t + 1], None, ALU.mult)
                    ins.then_inc(xn_ready, 1)
                    lo_groups(name, hT_hi, hT_lo, gain)
                else:
                    dve.wait_ge(fin_in, 16 * (1 if name == "fin0" else 2))
                    for t in range(TT):
                        ins = v.scalar_tensor_tensor(out=x[:, t, :], in0=x[:, t, :], scalar=rstd[:, t:t + 1],
                                                     in1=fin_gain[:, 0], op0=ALU.mult, op1=ALU.mult)
                    steps.done(ins)

            def x_final():
                v.tensor_copy(weight[:, 0, 0:1], x[:, 0, 0:1]).then_inc(x_ready, 1)

            def up(name, w, off):
                chunks = layers[name]
                n = len(chunks)
                loops = (n - 2) // 2
                groups = w // 256
                lo = gT_lo[:].rearrange("p k t -> p (k t)")
                hi = gT_hi[:].rearrange("p k t -> p (k t)")
                part0 = ACT_PARTS[name]

                def one(j, i=None):
                    c = chunks[j]
                    k = 0 if i is None else 2 * i
                    split_next(c, i, 4)
                    dve.wait_ge(act_part, part0 + j + 1 + k)
                    for t in range(TT):
                        ins = v.tensor_tensor(s[:, c.index % 2, t, 0:w], s[:, c.index % 2, t, 0:w],
                                              bank(c, t)[:, off:off + w], ALU.mult)
                    ins.then_inc(read_dve, 1)
                    if j > 0:
                        lag(j - 1, i)

                def lag(j, i=None):
                    for q in range(groups):
                        t = T_AT[name] + j * groups + q
                        at = (j * groups + q) * 512
                        k = 0 if i is None else 2 * groups * i
                        sl = slice(at, at + 512) if i is None else bass.ds(at + i * (2 * groups * 512), 512)
                        dve.wait_ge(t_hi, t + 1 + k)
                        v.tensor_tensor(lo[:, sl], psT[:, t % 2, :], hi[:, sl].bitcast(F32),
                                        ALU.subtract).then_inc(t_lo, 1)

                one(0)
                with dve.Fori(0, loops) as i:
                    one(1, i)
                    one(2, i)
                for j in range(1 + 2 * loops, n):
                    one(j)
                lag(n - 1)

            def residual(name, scale):
                for n, c in enumerate(layers[name]):
                    split_next(c)
                    chunk_done(c)
                    for t in range(TT):
                        ins = v.scalar_tensor_tensor(out=x[:, t, n * CH:(n + 1) * CH], in0=bank(c, t), scalar=scale,
                                                     in1=x[:, t, n * CH:(n + 1) * CH], op0=ALU.mult, op1=ALU.add)
                    steps_read(ins, n == 1)

            def steps_read(ins, last):
                ins.then_inc(read_dve, 1)
                if last:
                    dve.wait_ge(read_dve, 2 + layers_read[0])

            layers_read = [0]

            def rotary(src, dst, heads, t):
                tmp = s[:].rearrange("p a b c -> p (a b c)")[:, CH * t:CH * t + heads * 64].rearrange(
                    "p (h d) -> p h d", d=64)
                sv = src.rearrange("p (h d) -> p h d", d=64)
                dv = dst.rearrange("p (h d) -> p h d", d=64)
                v.tensor_tensor(dv, sv, cos[:, t, :].unsqueeze(1).broadcast_to([P, heads, 64]), ALU.mult)
                v.tensor_tensor(tmp[:, :, 0:32], sv[:, :, 32:64],
                                sin[:, t, 0:32].unsqueeze(1).broadcast_to([P, heads, 32]), ALU.mult)
                steps.done(v.tensor_tensor(tmp[:, :, 32:64], sv[:, :, 0:32],
                                           sin[:, t, 32:64].unsqueeze(1).broadcast_to([P, heads, 32]), ALU.mult))
                return v.tensor_tensor(dv, dv, tmp, ALU.add)

            def aux(name, j=0):
                n = A_AT[name] + j
                dve.wait_ge(aux_tr, n + 1)
                return psT[:, n % 4, :]

            def copied(ins):
                ins.then_inc(aux_cp, 1)

            def copy_groups(name, first, dst, scale):
                for j in range(4):
                    b = aux(name, first + j)
                    copied(v.tensor_scalar(dst[:, 2 * j:2 * j + 2, :], b.rearrange("p (k t) -> p k t", k=2), scale,
                                           None, ALU.mult))

            n_const = 16 * (len(GAINS) + 6)
            dve.wait_ge(const_in, n_const)
            v.tensor_copy(identb[:], ident)
            v.memset(causalb[:, 0:P], 0.0)
            v.tensor_copy(causalb[:, P:2 * P], causal_in)
            lp = lam_in.rearrange("p (a b) c -> p a b c", a=2)
            steps.done(v.tensor_tensor(lam_in[:, 0:4:2, :], lp[:, :, 0, :], lp[:, :, 1, :], ALU.mult))
            v.tensor_reduce(lam[:, 0:2], lam_in[:, 0:4:2, :], AX_X, ALU.add).then_inc(lam_sum, 1)
            b = aux("const", 0)
            copied(v.tensor_copy(gcol[:].rearrange("p g k -> p (g k)"), b[:, 0:KD * len(GAINS)]))
            for h in range(2):
                b = aux("const", 1 + h)
                copied(v.tensor_copy(taps[:, 4 * h:4 * h + 4, :],
                                     b[:, 0:4 * P].rearrange("p (k w) -> p k w", k=4)[:, :, 0:TAPS]))
            copied(v.tensor_copy(pos[:].rearrange("p k j -> p (k j)"), aux("const", 3)[:, 0:32]))
            dve.wait_ge(aux_cp, 4)
            g_da = gcol[:, GAIN["da_head_norm"], :]
            steps.done(v.tensor_scalar(g_da, g_da, 1.0 - LAM_INIT, None, ALU.mult))
            dve.wait_ge(lam_exp, 1)
            steps.done(v.tensor_tensor(lam[:, 5:6], lam[:, 3:4], lam[:, 2:3], ALU.subtract))
            v.tensor_scalar(lam[:, 4:5], lam[:, 5:6], -LAM_INIT, None, ALU.add).then_inc(consts_ready, 1)
            dve.wait_ge(x_in, 16)
            x_final()
            split(0)
            split(1)
            norm("norm0", "ffn1_norm")
            up("ffn1_up", 256, 256)
            layers_read[0] = layers["ffn1_down"][1].nth_read
            residual("ffn1_down", 0.5)
            v.tensor_copy(weight[:, 0, 1:2], x[:, 0, 0:1]).then_inc(r_free, 1)
            x_final()
            norm("norm1", "mix_norm")

            mix_flat = mixbuf[:].rearrange("p a b c -> p (a b c)")
            in_a, in_b = layers["in_a"], layers["in_b"]
            before = steps.n
            with dve.Fori(0, 2) as i:
                steps.loop = i * 4
                for j, c in enumerate(in_a[0:2]):
                    split_next(c, i, 4)
                    chunk_done(c, i, 4)
                    for t in range(TT):
                        ins = rotary(bank(c, t), mix_flat[:, bass.ds((j * TT + t) * CH + i * (2 * TT * CH), CH)], 8, t)
                    ins.then_inc(read_dve, 1)
            assert steps.n - before == 4
            steps.n, steps.loop = before + 8, 0
            for j, c in enumerate(in_a[4:8]):
                split_next(c)
                chunk_done(c)
                dst = (v_da, v_da, qa, qa)[j]
                lo_col = (j % 2) * CH
                for t in range(TT):
                    ins = v.tensor_copy(dst[:, t, lo_col:lo_col + CH], bank(c, t))
                ins.then_inc(read_dve, 1)
                if j >= 2:
                    dve.wait_ge(read_dve, 2 + c.nth_read)
                    for t in range(TT):
                        ins = rotary(qa[:, t, lo_col:lo_col + CH], qr[:, t, lo_col:lo_col + CH], 8, t)
                    steps.done(ins)
            c = in_b[0]
            split_next(c)
            chunk_done(c)
            for t in range(TT):
                for q in range(2):
                    v.tensor_copy(kvd[:, t, q], bank(c, t)[:, q * P:(q + 1) * P].rearrange("p (g d) -> p g d", g=2)
                                  .unsqueeze(2).broadcast_to([P, 2, 2, 64]))
                v.tensor_copy(vs[:, t, :], bank(c, t)[:, 3 * P:4 * P])
                ins = rotary(bank(c, t)[:, 2 * P:3 * P], rot_tmp(t), 2, t)
                if t == TT - 1:
                    ins.then_inc(read_dve, 1)
                    dve.wait_ge(read_dve, 2 + c.nth_read)
                else:
                    steps.done(ins)
            for t in range(TT):
                steps.done(v.tensor_copy(kvd[:, t, 2], rot_tmp(t).rearrange("p (g d) -> p g d", g=2)
                                         .unsqueeze(2).broadcast_to([P, 2, 2, 64])))
            c = in_b[1]
            split_next(c)
            chunk_done(c)
            for t in range(TT):
                v.tensor_copy(vw[:, t, :], bank(c, t)[:, P:2 * P])
                v.tensor_copy(gl[:, t, :], bank(c, t)[:, 2 * P:2 * P + 48])
                ins = rotary(bank(c, t)[:, 0:P], rot_tmp(t), 2, t)
                if t == TT - 1:
                    ins.then_inc(read_dve, 1)
                    dve.wait_ge(read_dve, 2 + c.nth_read)
                else:
                    steps.done(ins)
            for t in range(TT):
                ins = v.tensor_copy(kvd[:, t, 3], rot_tmp(t).rearrange("p (g d) -> p g d", g=2)
                                    .unsqueeze(2).broadcast_to([P, 2, 2, 64]))
                if t == 0:
                    ins.then_inc(gl_ready, 1)
            ins.then_inc(kv_ready, 1)

            for k in range(2):
                b = aux("raw_cmp", k).rearrange("p (g t) -> p g t", g=2)
                for h in range(2):
                    ins = v.tensor_copy(cin[k][64 * h:64 * h + 64], b[64 * h:64 * h + 64, :, h:T:2])
                copied(ins)
            copied(v.tensor_copy(ksT[:].rearrange("p g t -> p (g t)"), aux("kk", 0)))
            copied(v.tensor_copy(kwT[:].rearrange("p g t -> p (g t)"), aux("kk", 1)))
            dve.wait_ge(aux_cp, A_AT["raw_cmp"] + 2)
            for k in range(2):
                for g_ in range(2):
                    src = cin[k][:, g_, :].rearrange("p (n j) -> p j n", j=8)
                    for jh in range(2):
                        ins = v.tensor_tensor(blk_full[:, k, 8 * jh:8 * jh + 8, 15 * g_:15 * g_ + 15],
                                              src[:, :, jh:jh + 15],
                                              pos[:, k, 8 * jh:8 * jh + 8].unsqueeze(2).broadcast_to([P, 8, 15]), ALU.add)
            steps.done(ins)
            steps.done(v.tensor_copy(blocks_hi[:], blk_full))
            v.tensor_tensor(blocks_lo[:], blk_full, blocks_hi[:].bitcast(F32), ALU.subtract).then_inc(blocks_ready, 1)
            copy_groups("q_cmp", 0, kT, QSCALE)
            for c in layers["cmp"]:
                split_next(c)
            b = aux("hidden_cmp")
            v.memset(g1k[:], 0.0)
            v.memset(g1v[:], 0.0)
            steps.done(v.memset(vcb[:], 0.0))
            bh = b[:, 0:128].rearrange("p (v k r) -> p v k r", v=2, k=2)[:, :, :, 0:30]
            for kt in range(2):
                v.tensor_copy(g1k[:, kt, :, 0:15], bh[:, 0, kt, :].rearrange("p (g n) -> p g n", g=2))
                for g_ in range(2):
                    ins = v.tensor_copy(g1v[:, kt, g_, :, 0:15],
                                        bh[:, 1, kt, 15 * g_:15 * g_ + 15].unsqueeze(1).broadcast_to([P, 4, 15]))
            copied(ins)
            copied(v.tensor_copy(kcT[:], aux("kc")[:, 0:32].rearrange("p (g n) -> p g n", g=2)))
            b = aux("vc")[:, 0:128].rearrange("p (g d) -> p g d", g=2)
            for j in range(4):
                ins = v.tensor_copy(vcb[32 * j:32 * j + 32, :, j, :], b[32 * j:32 * j + 32])
            copied(ins)
            for h in range(2):
                if h == 0:
                    aux("s_cmp")
                for t in range(TT):
                    ins = v.tensor_tensor(sc[:, t, h], ps[:, h, t * 128:(t + 1) * 128].rearrange("p (h n) -> p h n", h=8),
                                          cmask[:, t, :].unsqueeze(1).broadcast_to([P, 8, 16]), ALU.add)
            copied(ins)
            dve.wait_ge(aux_cp, A_AT["s_cmp"] + 1)
            scf = sc.rearrange("p t b h n -> p (t b h) n")
            steps.done(v.tensor_reduce(cstat[:, 0, :], scf, AX_X, ALU.max))
            v.tensor_tensor(scf, scf, cstat[:, 0, :].unsqueeze(2).broadcast_to([P, 32, 16]), ALU.subtract).then_inc(cmp_sub, 1)
            v.memset(pc, 0.0)
            dve.wait_ge(cmp_exp, 1)
            steps.done(v.tensor_reduce(cstat[:, 0, :], scf, AX_X, ALU.add))
            steps.done(v.reciprocal(cstat[:, 1, :], cstat[:, 0, :]))
            dve.wait_ge(gates_ready, 1)
            cw = cstat[:, 2, :].rearrange("p (t b h) -> p t b h", t=TT, b=2)
            ci = cstat[:, 1, :].rearrange("p (t b h) -> p t b h", t=TT, b=2)
            gv = gates[:].rearrange("p t (h b r) -> p t b h r", b=2, r=3)
            for t in range(TT):
                ins = v.tensor_tensor(cw[:, t], ci[:, t], gv[:, t, :, :, 0], ALU.mult)
            steps.done(ins)
            for t in range(TT):
                for h in range(2):
                    ins = v.tensor_tensor(sc[:, t, h], sc[:, t, h],
                                          cvalid[:, t, :].unsqueeze(1).broadcast_to([P, 8, 16]), ALU.mult)
            steps.done(ins)
            for t in range(TT):
                for h in range(2):
                    ins = v.tensor_tensor(pc[:, t, h:HEADS:2, 0:16], sc[:, t, h],
                                          cw[:, t, h].unsqueeze(2).broadcast_to([P, 8, 16]), ALU.mult)
            ins.then_inc(cmp_p, 1)
            for j in range(2):
                copied(v.tensor_copy(pcT[:, j].rearrange("p q t -> p (q t)"), aux("p_cmp", j)))
            copy_groups("qk_da", 0, qaT, QSCALE)
            copy_groups("qk_da", 4, kT, 1.0)

            def attention(kind, o_out):
                n = ATT_STEPS[kind]
                total = TT * n

                def info(q):
                    tok = q // n
                    return ATT[kind] + q, tok, q % n, P * (tok + 1)

                def maxima(q):
                    st, tok, _, w = info(q)
                    dve.wait_ge(scores_done, st + 1)
                    v.tensor_reduce(negmax[:, st % 2, :], ps[:, 2 * (st % 2):2 * (st % 2) + 2, 0:2 * w]
                                    .rearrange("p b (m w) -> p b m w", m=2), AX_X, ALU.max,
                                    negate=True).then_inc(max_done, 1)

                def scale(q):
                    st, tok, h, w = info(q)
                    dve.wait_ge(exp_done, st + 1)
                    pr = probs[:, st % 2].rearrange("p (m w) -> p m w", m=4)
                    steps_r = v.reciprocal(rowinv[:, st % 8, :], rowsum[:, st % 8, :])
                    if kind == "fox":
                        steps_r.then_inc(probs_ready, 1)
                        return
                    steps.done(steps_r)
                    if kind == "da":
                        steps.done(v.scalar_tensor_tensor(out=weight[:, st % 2, 0:2], in0=rowinv[:, st % 8, 2:4],
                                                          scalar=lam[:, 4:5], in1=rowsum[:, st % 8, 0:2],
                                                          op0=ALU.mult, op1=ALU.mult))
                        for m in range(2):
                            ins = v.scalar_tensor_tensor(out=pr[:, m, 0:w], in0=pr[:, 2 + m, 0:w],
                                                         scalar=weight[:, st % 2, m:m + 1], in1=pr[:, m, 0:w],
                                                         op0=ALU.mult, op1=ALU.add)
                    else:
                        steps.done(v.tensor_tensor(weight[:, st % 2, :].rearrange("p (b m) -> p b m", b=2),
                                                   rowinv[:, st % 8, :].rearrange("p (b m) -> p b m", b=2),
                                                   gates[:, tok, 6 * h:6 * h + 6].rearrange("p (b r) -> p b r", b=2)[:, :, 1:3],
                                                   ALU.mult))
                        for m in range(4):
                            ins = v.tensor_scalar(pr[:, m, 0:w], pr[:, m, 0:w], weight[:, st % 2, m:m + 1], None, ALU.mult)
                    ins.then_inc(probs_ready, 1)

                def copy_t(q):
                    st, tok, h, w = info(q)
                    blocks = (2 if kind == "da" else 4) * (tok + 1)
                    dve.wait_ge(probs_tr, st + 1)
                    if q >= 2:
                        dve.wait_ge(pv_done, st - 1)
                    v.tensor_copy(probsT[:, st % 2, 0:blocks * P],
                                  ps[:, 6:8, :].rearrange("p a b -> p (a b)")[:, 0:blocks * P]).then_inc(probsT_ready, 1)

                def read_o(tok, b):
                    st = ATT[kind] + tok * n + (b + 1) * n // 2
                    dve.wait_ge(pv_done, st)
                    o_out(tok, b, st % 8).then_inc(o_read, 1)

                for q in range(total + 3):
                    if q < total:
                        maxima(q)
                    if 2 <= q < total + 2:
                        copy_t(q - 2)
                    if 1 <= q < total + 1:
                        scale(q - 1)
                    done = q - 2
                    if done > 0 and done % (n // 2) == 0 and done <= total:
                        read_o((done - 1) // n, ((done - 1) % n) // (n // 2))

            y_da, y_ns = y_mix[:, 0], y_mix[:, 1]

            def o_da(tok, b, st):
                s0 = (tok * 4 + 2 * b) % 8
                return v.tensor_tensor(y_da[:, tok, b * CH:(b + 1) * CH].rearrange("p (s m e) -> p s m e", s=2, m=2),
                                       ps[:, 4 + b, :].rearrange("p (s m e) -> p s m e", s=2, m=2),
                                       rowinv[:, s0:s0 + 2, 0:2].unsqueeze(3).broadcast_to([P, 2, 2, P]), ALU.mult)

            def o_ns(tok, b, st):
                return v.tensor_copy(y_ns[:, tok, b * CH:(b + 1) * CH], ps[:, 4 + b, :])

            attention("da", o_da)
            copy_groups("q_ns", 0, qaT, QSCALE)
            attention("ns", o_ns)
            dve.wait_ge(o_read, 8)
            sqv = xn[:].rearrange("p t n -> p (t n)")
            yv = y_da.rearrange("p t n -> p (t n)")
            steps.done(v.tensor_tensor(sqv, yv, yv, ALU.mult))
            v.tensor_reduce(cstat[:, 0, 0:16], sqv.rearrange("p (h e) -> p h e", e=P), AX_X, ALU.add).then_inc(y_sum, 1)
            dve.wait_ge(y_rstd, 1)
            yh = yv.rearrange("p (h e) -> p h e", e=P)
            v.tensor_tensor(yh, yh, cstat[:, 2, 0:16].unsqueeze(2).broadcast_to([P, 16, P]), ALU.mult).then_inc(xn_ready, 2)

            with dve.Fori(0, 2) as i:
                for c in layers["gates"][0:2]:
                    split_next(c, i, 4)
            lo_groups("y_da", yT_hi, yT_lo, "da_head_norm")

            def merged(name, first, at):
                for n, c in enumerate(layers[name]):
                    split_next(c)
                    chunk_done(c)
                    for t in range(TT):
                        g_ = gatebuf[:, at + n, t, :]
                        d = m_buf[:, t, n * CH:(n + 1) * CH]
                        if first:
                            ins = v.tensor_tensor(d, bank(c, t), g_, ALU.mult)
                        else:
                            ins = v.tensor_tensor(g_, bank(c, t), g_, ALU.mult)
                    ins.then_inc(read_dve, 1)
                    if not first:
                        dve.wait_ge(read_dve, 2 + c.nth_read)
                        for t in range(TT):
                            d = m_buf[:, t, n * CH:(n + 1) * CH]
                            ins = v.tensor_tensor(d, d, gatebuf[:, at + n, t, :], ALU.add)
                        if n == 1:
                            ins.then_inc(xn_ready, 1)

            merged("proj_da", True, 0)
            lo_groups("y_ns", hT_hi, hT_lo)
            merged("proj_ns", False, 2)
            lo_groups("m", hT_hi, hT_lo)
            layers_read[0] = layers["out"][1].nth_read
            residual("out", 1.0)
            x_final()
            norm("norm2", "ffn2_norm")
            up("ffn2_up", 256, 256)
            layers_read[0] = layers["ffn2_down"][1].nth_read
            residual("ffn2_down", 0.5)
            v.tensor_copy(weight[:, 0, 1:2], x[:, 0, 0:1]).then_inc(r_free, 1)
            x_final()
            norm("fin0", None)

            x_final()
            norm("norm3", "mix_norm_2.0")
            dve.wait_ge(conv_in, 32)
            dve.wait_ge(zero_ready, 1)
            for t in range(TT):
                ins = v.tensor_tensor(x[:, t, :], x[:, t, :], b_pw2[:], ALU.add)
            steps.done(ins)
            bp = b_pw1[:].rearrange("p (h n) -> p h n", h=2)

            def conv_tile(ct):
                steps.done(v.tensor_scalar(conv[:, ct], ubuf[:, ct, 0:T], taps[:, ct, 0:1],
                                           gcol[:, GAIN["conv_b_dw_2"], ct:ct + 1], ALU.mult, ALU.add))
                for k in range(1, TAPS):
                    ins = v.scalar_tensor_tensor(out=conv[:, ct], in0=ubuf[:, ct, k:k + T], scalar=taps[:, ct, k:k + 1],
                                                 in1=conv[:, ct], op0=ALU.mult, op1=ALU.add)
                    if k < TAPS - 1:
                        steps.done(ins)
                ins.then_inc(conv_dve, 1)

            for j, c in enumerate(layers["pw1"]):
                split_next(c)
                chunk_done(c)
                for t in range(TT):
                    ins = v.tensor_tensor(s[:, c.index % 2, t, :].rearrange("p (h n) -> p h n", h=2),
                                          bank(c, t).rearrange("p (h n) -> p h n", h=2),
                                          bp[:, :, 256 * j:256 * j + 256], ALU.add)
                ins.then_inc(read_dve, 1)
                dve.wait_ge(read_dve, 2 + c.nth_read)
                v.tensor_copy(weight[:, 0, 2:3], s[:, c.index % 2, 0, 0:1]).then_inc(bias_in, 1)
                dve.wait_ge(act_part, ACT_PARTS["pw1"] + j + 1)
                for t in range(TT):
                    ins = v.tensor_tensor(s[:, c.index % 2, t, 0:256], s[:, c.index % 2, t, 0:256],
                                          s[:, c.index % 2, t, 256:512], ALU.mult)
                ins.then_inc(g_ready, 1)
                b = aux("glu", j)
                copied(v.tensor_copy(ubuf[:, 2 * j:2 * j + 2, TAPS - 1:TAPS - 1 + T], b.rearrange("p (k t) -> p k t", k=2)))
                dve.wait_ge(aux_cp, A_AT["glu"] + j + 1)
                v.tensor_copy(weight[:, 0, 3:4], ubuf[:, 2 * j, TAPS - 1:TAPS]).then_inc(tile_in, 1)
                for ct in DVE_TILES:
                    if ct // 2 == j - 1:
                        conv_tile(ct)
            for ct in DVE_TILES:
                if ct // 2 == 3:
                    conv_tile(ct)
            dve.wait_ge(conv_dve, len(DVE_TILES))
            dve.wait_ge(conv_pool, len(POOL_TILES))
            dve.wait_ge(mean_done, 1)
            v.tensor_tensor(conv[:], conv[:], ps[:, 0, 0:T].unsqueeze(1).broadcast_to([P, KD, T]),
                            ALU.subtract).then_inc(centred, 1)
            dve.wait_ge(var_done, 1)
            v.tensor_scalar(stat[:, 0, :], ps[:, 1, 0:T], EPS, None, ALU.add).then_inc(std_ready, 1)
            dve.wait_ge(std_ready, 2)
            steps.done(v.reciprocal(stat[:, 0, :], stat[:, 1, :]))
            dve.wait_ge(centred, 1)
            v.tensor_tensor(conv[:], conv[:], stat[:, 0, :].unsqueeze(1).broadcast_to([P, KD, T]),
                            ALU.mult).then_inc(normed, 1)
            for ct in range(KD):
                dve.wait_ge(cT_hi, ct + 1)
                v.tensor_tensor(hT_lo[:, ct, :], conv[:, ct], hT_hi[:, ct, :].bitcast(F32), ALU.subtract).then_inc(cT_lo, 1)
            layers_read[0] = layers["pw2"][1].nth_read
            residual("pw2", 1.0)

            def ffn_ple(i, n_a, n_b):
                x_final()
                norm(n_a, f"ffn_norm_2.{i}")
                up(f"up{i}", 512, 0)
                layers_read[0] = layers[f"down{i}"][1].nth_read
                residual(f"down{i}", 1.0)
                v.tensor_copy(weight[:, 0, 1:2], x[:, 0, 0:1]).then_inc(r_free, 1)
                x_final()
                norm(n_b, f"ple_norm_2.{i}")
                dve.wait_ge(t_hi, T_AT[f"emb{i}"] + 1)
                v.tensor_tensor(eT_lo[:].rearrange("p k t -> p (k t)"), psT[:, 0, :],
                                eT_hi[:].rearrange("p k t -> p (k t)").bitcast(F32), ALU.subtract).then_inc(t_lo, 1)
                for j, c in enumerate(layers[f"ple{i}"]):
                    split_next(c)
                    if c.reader == "act":
                        continue
                    dve.wait_ge(read_act, 2 + layers[f"ple{i}"][j - 1].nth_read)
                    chunk_done(c)
                    n = j // 2
                    for t in range(TT):
                        ins = v.tensor_tensor(s[:, n, t, :], s[:, n, t, :], bank(c, t), ALU.mult)
                    ins.then_inc(read_dve, 1)
                    dve.wait_ge(read_dve, 2 + c.nth_read)
                    for t in range(TT):
                        d = x[:, t, n * CH:(n + 1) * CH]
                        ins = v.tensor_tensor(d, d, s[:, n, t, :], ALU.add)
                    steps.done(ins)
                v.tensor_copy(weight[:, 0, 1:2], x[:, 0, 0:1]).then_inc(r_free, 1)
                x_final()

            ffn_ple(0, "norm4", "norm5")
            norm("norm6", "kv_norm_2")
            for j, c in enumerate(layers["kv"]):
                split_next(c)
                chunk_done(c)
                dst = (kf, kf, vf, vf)[j]
                for t in range(TT):
                    ins = v.tensor_copy(dst[:, t, (j % 2) * CH:(j % 2 + 1) * CH], bank(c, t))
                ins.then_inc(read_dve, 1)
            c = layers["f"][0]
            split_next(c)
            chunk_done(c)
            dve.wait_ge(bf_in, 16)
            for t in range(TT):
                ins = v.tensor_tensor(fz[:, 0, t], bank(c, t)[:, 0:HEADS], b_f[:], ALU.add)
            ins.then_inc(read_dve, 1)
            dve.wait_ge(read_dve, 2 + c.nth_read)
            steps.done(v.tensor_scalar(fz[:, 1], fz[:, 0], -1.0, None, ALU.mult))
            v.tensor_tensor(fz[:, 1], fz[:, 1], fz[:, 0], ALU.min).then_inc(f_abs, 1)
            steps.done(v.tensor_scalar(fz[:, 0], fz[:, 0], 0.0, None, ALU.min))
            lo_groups("norm6q", hT_hi, hT_lo, "mix_norm_2.1")
            dve.wait_ge(f_ln, 1)
            for d_ in range(2):
                ins = v.tensor_tensor(lfd[:, :, d_, :], fz[:, 0], fz[:, 3], ALU.subtract)
            ins.then_inc(lf_ready, 1)
            for n, c in enumerate(layers["q"]):
                split_next(c)
                chunk_done(c)
                for t in range(TT):
                    ins = v.tensor_copy(qf[:, t, n * CH:(n + 1) * CH], bank(c, t))
                ins.then_inc(read_dve, 1)
            dve.wait_ge(read_dve, 2 + layers["q"][1].nth_read)
            v.tensor_copy(weight[:, 0, 1:2], qf[:, 0, 0:1]).then_inc(kv_ready, 1)
            copy_groups("qk_fox", 0, qT, QSCALE)
            copy_groups("qk_fox", 4, kTf, 1.0)
            copied(v.tensor_copy(cum[:], aux("cum")[0:32, 0:T]))
            dve.wait_ge(aux_cp, A_AT["cum"] + 1)
            dve.wait_ge(zero_ready, 3)
            v.tensor_scalar(bias_l[0:32, :], cum[:], const("left_scale")[0:32], const("left_shift")[0:32],
                            ALU.mult, ALU.add)
            steps.done(v.tensor_tensor(bias_r[0:32], cum[:].unsqueeze(1).broadcast_to([32, HEADS, T]),
                                       const("onehot_c")[0:32].unsqueeze(2).broadcast_to([32, HEADS, T]), ALU.mult))
            v.tensor_tensor(bias_r[0:32], bias_r[0:32],
                            const("onehot_1")[0:32].unsqueeze(2).broadcast_to([32, HEADS, T]), ALU.add).then_inc(bias_rows, 1)

            def o_fox(tok, b, st):
                s0 = (tok * 4 + 2 * b) % 8
                return v.tensor_tensor(qf[:, tok, b * CH:(b + 1) * CH].rearrange("p (h e) -> p h e", e=64),
                                       ps[:, 4 + b, :].rearrange("p (h e) -> p h e", e=64),
                                       rowinv[:, s0:s0 + 2, :].rearrange("p s m -> p (s m)").unsqueeze(2)
                                       .broadcast_to([P, 8, 64]), ALU.mult)

            attention("fox", o_fox)
            dve.wait_ge(o_read, 12)
            v.tensor_copy(weight[:, 0, 1:2], qf[:, 0, 0:1]).then_inc(xn_ready, 1)
            lo_groups("y_fox", hT_hi, hT_lo)
            layers_read[0] = layers["o"][1].nth_read
            residual("o", 1.0)
            ffn_ple(1, "norm7", "norm8")
            norm("fin1", None)
            v.tensor_copy(weight[:, 0, 0:1], x[:, 0, 0:1]).then_inc(out_ready, 1)

        @block.tensor
        def _(pe):
            t_ = nc.tensor

            def products(c, lhs_hi, lhs_lo, i=None, per=0, need=None, rows=P, tiles=TT):
                k_ = 0 if i is None else per * i
                w = width(c)
                n_k = sum(c.units)
                k0 = 0
                for q, nk in enumerate(c.units):
                    u = c.u0 + q
                    if need:
                        need(k0 + nk - 1)
                    pe.wait_ge(lo_ready, RING + u + 1 + k_)
                    hi, lo = (unit_view(x_, u % RING, nk, w) for x_ in (w_hi, w_lo))
                    for k in range(nk):
                        kt = k0 + k
                        for t in range(tiles):
                            o = ps[0:rows, 2 * (c.index % 2) + t, 0:w]
                            ah, al = lhs_hi(kt, t), lhs_lo(kt, t)
                            t_.matmul(o, ah, hi[:, k, :], start=(kt == 0), stop=False)
                            t_.matmul(o, ah, lo[:, k, :], start=False, stop=False)
                            ins = t_.matmul(o, al, hi[:, k, :], start=False, stop=(kt == n_k - 1))
                    ins.then_inc(unit_used, 1)
                    k0 += nk

            def banks_free(c):
                if c.index >= 2:
                    b = order[c.index - 2]
                    pe.wait_ge({"dve": read_dve, "act": read_act}[b.reader], 2 + b.nth_read)

            def tokens(t, hi):
                return lambda kt, tok: t[:, kt, tok * P:(tok + 1) * P]

            h_hi, h_lo = tokens(hT_hi, 1), tokens(hT_lo, 0)
            g_hi, g_lo = tokens(gT_hi, 1), tokens(gT_lo, 0)
            y_hi, y_lo = tokens(yT_hi, 1), tokens(yT_lo, 0)

            def need_groups(name):
                return lambda kt: pe.wait_ge(t_lo, 2 + T_AT[name] + kt // 2 + 1)

            def transposes(name, src, src_count):
                pe.wait_ge(xn_ready, src_count)
                if T_AT[name]:
                    pe.wait_ge(t_lo, 2 + T_AT[name])
                for j in range(4):
                    for k in range(2):
                        for t in range(TT):
                            kt = 2 * j + k
                            ins = t_.transpose(psT[:, j, (k * TT + t) * P:(k * TT + t + 1) * P],
                                               src(t)[:, kt * P:(kt + 1) * P], ident)
                    ins.then_inc(tr_done, 1)

            def norm_t(name, count):
                transposes(name, lambda t: xn[:, t, :], count)

            def plain(name, lhs_hi, lhs_lo, need):
                for c in layers[name]:
                    banks_free(c)
                    products(c, lhs_hi, lhs_lo, need=need)

            def paired(name, lhs_hi, lhs_lo, need):
                chunks = layers[name]
                banks_free(chunks[0])
                banks_free(chunks[1])
                need(KD - 1)
                free = {"dve": read_dve, "act": read_act}[chunks[0].reader]
                with pe.Fori(0, len(chunks) // 2) as i:
                    for j, c in enumerate(chunks[0:2]):
                        pe.wait_ge(free, c.nth_read + i * 2)
                        products(c, lhs_hi, lhs_lo, i, 4)

            def up(name, w, norm_name):
                chunks = layers[name]
                n = len(chunks)
                loops = (n - 2) // 2
                groups = w // 256

                def tr(j, i=None):
                    c = chunks[j]
                    k_ = 0 if i is None else 2 * i
                    pe.wait_ge(read_dve, 2 + c.nth_read + k_)
                    for q in range(groups):
                        t0 = T_AT[name] + j * groups + q
                        pe.wait_ge(t_lo, t0 + 1 + k_ * groups)
                        for f in range(2):
                            for t in range(TT):
                                ins = t_.transpose(psT[:, t0 % 2, (f * TT + t) * P:(f * TT + t + 1) * P],
                                                   s[:, c.index % 2, t, (2 * q + f) * P:(2 * q + f + 1) * P], ident)
                        ins.then_inc(tr_done, 1)

                need = need_groups(norm_name)
                for j in range(2):
                    banks_free(chunks[j])
                products(chunks[0], h_hi, h_lo, need=need)

                def one(j, i=None):
                    c = chunks[j]
                    pe.wait_ge(read_dve, c.nth_read + (0 if i is None else 2 * i))
                    products(c, h_hi, h_lo, i, 4)
                    tr(j - 1, i)

                with pe.Fori(0, loops) as i:
                    one(1, i)
                    one(2, i)
                for j in range(1 + 2 * loops, n):
                    one(j)
                tr(n - 1)

            def down(name, up_name):
                need = lambda kt: pe.wait_ge(t_lo, 2 + T_AT[up_name] + kt // 2 + 1)
                for n, c in enumerate(layers[name]):
                    banks_free(c)
                    products(c, g_hi, g_lo, need=need if n == 0 else None)

            def aux_bank(name, j=0):
                n = A_AT[name] + j
                if n >= 4:
                    pe.wait_ge(aux_cp, n - 3)
                return psT[:, n % 4, :]

            def aux_groups(name, first, src):
                for j in range(4):
                    b = aux_bank(name, first + j)
                    for k in range(2):
                        for t in range(TT):
                            ins = t_.transpose(b[:, (k * TT + t) * P:(k * TT + t + 1) * P], src(2 * j + k, t), ident)
                    ins.then_inc(aux_tr, 1)

            pe.wait_ge(const_in, 16 * (len(GAINS) + 6))
            n_g = KD * len(GAINS)
            t_.transpose(aux_bank("const")[:, 0:n_g], rows_g[0:n_g, :], ident[0:n_g, 0:n_g]).then_inc(aux_tr, 1)
            for h in range(2):
                b = aux_bank("const", 1 + h)
                for k in range(4):
                    kt = 4 * h + k
                    ins = t_.transpose(b[:, k * P:k * P + TAPS], rows_w[0:TAPS, kt * P:(kt + 1) * P], ident[0:TAPS, 0:TAPS])
                ins.then_inc(aux_tr, 1)
            b = aux_bank("const", 3)
            for k in range(2):
                ins = t_.transpose(b[:, 16 * k:16 * k + 16], rows_p[0:16, k * P:(k + 1) * P], ident[0:16, 0:16])
            ins.then_inc(aux_tr, 1)
            pe.wait_ge(aux_cp, 4)

            norm_t("norm0", SRC["norm0"])
            up("ffn1_up", 256, "norm0")
            down("ffn1_down", "ffn1_up")
            norm_t("norm1", SRC["norm1"])
            paired("in_a", h_hi, h_lo, need_groups("norm1"))
            plain("in_b", h_hi, h_lo, None)

            pe.wait_ge(kv_ready, 1)
            for k in range(2):
                b = aux_bank("raw_cmp", k)
                for g_ in range(2):
                    for t in range(TT):
                        ins = t_.transpose(b[:, (g_ * TT + t) * P:(g_ * TT + t + 1) * P],
                                           kvd[:, t, k, g_].rearrange("p u d -> p (u d)"), ident)
                ins.then_inc(aux_tr, 1)
            for k in range(2):
                b = aux_bank("kk", k)
                for g_ in range(2):
                    for t in range(TT):
                        ins = t_.transpose(b[:, (g_ * TT + t) * P:(g_ * TT + t + 1) * P],
                                           kvd[:, t, 2 + k, g_].rearrange("p u d -> p (u d)"), ident)
                ins.then_inc(aux_tr, 1)
            aux_groups("q_cmp", 0, lambda kt, t: qa[:, t, kt * P:(kt + 1) * P])
            pe.wait_ge(blocks_ready, 1)
            for k, c in enumerate(layers["cmp"]):
                banks_free(c)
                products(c, lambda kt, t, k=k: blocks_hi[:, k, kt, :], lambda kt, t, k=k: blocks_lo[:, k, kt, :],
                         rows=30, tiles=1)
            pe.wait_ge(read_act, 2 + layers["cmp"][1].nth_read)
            b = aux_bank("hidden_cmp")
            for k in range(2):
                for kt in range(2):
                    ins = t_.transpose(b[:, (k * 2 + kt) * 32:(k * 2 + kt) * 32 + 30], g1[0:30, k, kt * P:(kt + 1) * P],
                                       ident[0:30, 0:30])
            ins.then_inc(aux_tr, 1)
            pe.wait_ge(aux_cp, A_AT["hidden_cmp"] + 1)
            pe.wait_ge(w2_in, 48)
            b = aux_bank("kc")
            for kt in range(2):
                ins = t_.matmul(b[:, 0:32], w2k[:, kt].rearrange("p u d -> p (u d)"),
                                g1k[:, kt].rearrange("p g n -> p (g n)"), start=(kt == 0), stop=(kt == 1))
            ins.then_inc(aux_tr, 1)
            b = aux_bank("vc")
            for g_ in range(2):
                for kt in range(2):
                    ins = t_.matmul(b[:, g_ * 64:(g_ + 1) * 64], g1v[:, kt, g_].rearrange("p u n -> p (u n)"),
                                    w2v[:, kt], start=(kt == 0), stop=(kt == 1))
            ins.then_inc(aux_tr, 1)
            pe.wait_ge(aux_cp, A_AT["vc"] + 1)
            pe.wait_ge(read_act, 2 + layers["cmp"][1].nth_read)
            for h in range(2):
                for t in range(TT):
                    for hp in range(8):
                        at = (t * 8 + hp) * 16
                        ins = t_.matmul(ps[:, h, at:at + 16], kT[64 * h:64 * h + 64, hp, t * P:(t + 1) * P],
                                        kcT[64 * h:64 * h + 64, hp // 4, :], start=True, stop=True)
            ins.then_inc(aux_tr, 1)
            pe.wait_ge(cmp_p, 1)
            for t in range(TT):
                b = aux_bank("p_cmp", t)
                for q in range(4):
                    ins = t_.transpose(b[:, q * P:(q + 1) * P], pc[:, t, 4 * q:4 * q + 4, :].rearrange("p h n -> p (h n)"),
                                       ident)
                ins.then_inc(aux_tr, 1)

            aux_groups("qk_da", 0, lambda kt, t: mixbuf[:, kt // 4, t, (kt % 4) * P:(kt % 4 + 1) * P])
            aux_groups("qk_da", 4, lambda kt, t: mixbuf[:, 2 + kt // 4, t, (kt % 4) * P:(kt % 4 + 1) * P])

            def attention(kind, q_op, k_op, v_op, o_at):
                n = ATT_STEPS[kind]
                total = TT * n

                def scores(q):
                    st, tok, h = ATT[kind] + q, q // n, q % n
                    w = P * (tok + 1)
                    if q >= 2:
                        pe.wait_ge(exp_done, st - 1)
                    for b in range(2):
                        for m in range(2):
                            o = ps[:, 2 * (st % 2) + b, m * w:(m + 1) * w]
                            first = True
                            if kind == "fox":
                                t_.matmul(o, bias_l[:, tok * P:(tok + 1) * P], bias_r[:, 4 * h + 2 * m + b, 0:w],
                                          start=True, stop=False)
                                first = False
                            t_.matmul(o, q_op(h, b, m, tok), k_op(h, b, m, w), start=first, stop=False)
                            ins = t_.matmul(o, identb[:], causalb[:, 2 * P - w:2 * P], start=False, stop=True)
                    ins.then_inc(scores_done, 1)

                def turn(q):
                    st, tok = ATT[kind] + q, q // n
                    pe.wait_ge(probs_ready, st + 1)
                    if q >= 1:
                        pe.wait_ge(probsT_ready, st)
                    maps = 2 if kind == "da" else 4
                    for m in range(maps):
                        for kb in range(tok + 1):
                            r = m * (tok + 1) + kb
                            ins = t_.transpose(ps[:, 6 + r // 4, (r % 4) * P:(r % 4 + 1) * P],
                                               probs[:, st % 2, m * T + kb * P:m * T + (kb + 1) * P], ident)
                    ins.then_inc(probs_tr, 1)

                def pv(q):
                    st, tok, h = ATT[kind] + q, q // n, q % n
                    pe.wait_ge(probsT_ready, st + 1)
                    bank = h // (n // 2)
                    fresh = h % (n // 2) == 0
                    if fresh and (kind != "da" or tok > 0):
                        reads = {"da": 0, "ns": 4, "fox": 8}[kind] + 2 * tok + bank
                        pe.wait_ge(o_read, reads - 1)
                    if fresh and kind == "ns":
                        for quad in range(2):
                            t_.matmul(ps[:, 4 + bank, quad * 256:(quad + 1) * 256], pcT[:, tok, 2 * bank + quad, :],
                                      vcb[:, bank].rearrange("p j d -> p (j d)"), start=(quad == 0), stop=False,
                                      skip_group_check=True)
                        fresh = False
                    maps = 2 if kind == "da" else 4
                    for m in range(maps):
                        for kb in range(tok + 1):
                            r = m * (tok + 1) + kb
                            rhs = v_op(h, m, kb)
                            at = o_at(h, m)
                            last = h % (n // 2) == n // 2 - 1 and m == maps - 1 and kb == tok
                            ins = t_.matmul(ps[:, 4 + bank, at:at + rhs.shape[-1]], probsT[:, st % 2, r * P:(r + 1) * P],
                                            rhs, start=fresh, stop=last, skip_group_check=True)
                            fresh = False
                    ins.then_inc(pv_done, 1)

                for q in range(total + 2):
                    if q < total:
                        scores(q)
                    if 1 <= q < total + 1:
                        turn(q - 1)
                    if q >= 2:
                        pv(q - 2)

            pe.wait_ge(aux_cp, A_AT["qk_da"] + 8)
            attention("da", lambda h, b, m, tok: qaT[64 * b:64 * b + 64, 2 * h + m, tok * P:(tok + 1) * P],
                      lambda h, b, m, w: kT[64 * b:64 * b + 64, 2 * h + m, 0:w],
                      lambda h, m, kb: v_da[:, kb, (2 * h + m) * P:(2 * h + m + 1) * P],
                      lambda h, m: ((2 * h + m) % 4) * P)
            pe.wait_ge(o_read, 4)
            aux_groups("q_ns", 0, lambda kt, t: qr[:, t, kt * P:(kt + 1) * P])
            pe.wait_ge(aux_cp, A_AT["q_ns"] + 4)
            attention("ns", lambda h, b, m, tok: qaT[64 * b:64 * b + 64, h, tok * P:(tok + 1) * P],
                      lambda h, b, m, w: (ksT, kwT)[m][64 * b:64 * b + 64, h // 4, 0:w],
                      lambda h, m, kb: (vs, vw)[m % 2][:, kb, 64 * (h // 4):64 * (h // 4) + 64],
                      lambda h, m: ((2 * h + m // 2) % 8) * 64)

            pe.wait_ge(exp_done, ATT["ns"] + 16)
            paired("gates", h_hi, h_lo, lambda kt: None)
            transposes("y_da", lambda t: y_mix[:, 0, t, :], SRC["y_da"])
            plain("proj_da", y_hi, y_lo, need_groups("y_da"))
            transposes("y_ns", lambda t: y_mix[:, 1, t, :], SRC["y_ns"])
            plain("proj_ns", h_hi, h_lo, need_groups("y_ns"))
            transposes("m", lambda t: m_buf[:, t, :], SRC["m"])
            plain("out", h_hi, h_lo, need_groups("m"))
            norm_t("norm2", SRC["norm2"])
            up("ffn2_up", 256, "norm2")
            down("ffn2_down", "ffn2_up")

            norm_t("norm3", SRC["norm3"])
            chunks = layers["pw1"]

            def turn_glu(j):
                c = chunks[j]
                pe.wait_ge(g_ready, j + 1)
                b = aux_bank("glu", j)
                for f in range(2):
                    for t in range(TT):
                        ins = t_.transpose(b[:, (f * TT + t) * P:(f * TT + t + 1) * P],
                                           s[:, c.index % 2, t, f * P:(f + 1) * P], ident)
                ins.then_inc(aux_tr, 1)

            for j, c in enumerate(chunks):
                banks_free(c)
                products(c, h_hi, h_lo, need=need_groups("norm3") if j == 0 else None)
                turn_glu(j)
            pe.wait_ge(conv_dve, len(DVE_TILES))
            pe.wait_ge(conv_pool, len(POOL_TILES))
            pe.wait_ge(read_dve, 2 + chunks[3].nth_read)
            for ct in range(KD):
                ins = t_.matmul(ps[:, 0, 0:T], const("inv_d"), conv[:, ct], start=(ct == 0), stop=(ct == KD - 1))
            ins.then_inc(mean_done, 1)
            pe.wait_ge(squared, 1)
            for ct in range(KD):
                ins = t_.matmul(ps[:, 1, 0:T], const("inv_d"), sq[:, ct], start=(ct == 0), stop=(ct == KD - 1))
            ins.then_inc(var_done, 1)
            pe.wait_ge(std_ready, 1)
            plain("pw2", h_hi, h_lo, lambda kt: pe.wait_ge(cT_lo, kt + 1))

            def ffn_ple(i, n_a, n_b):
                norm_t(n_a, SRC[n_a])
                up(f"up{i}", 512, n_a)
                down(f"down{i}", f"up{i}")
                norm_t(n_b, SRC[n_b])
                pe.wait_ge(emb_in, 16 * (i + 1))
                t0 = T_AT[f"emb{i}"]
                pe.wait_ge(t_lo, 2 + t0)
                for k in range(2):
                    for t in range(TT):
                        ins = t_.transpose(psT[:, 0, (k * TT + t) * P:(k * TT + t + 1) * P],
                                           emb[:, t, k * P:(k + 1) * P], ident)
                ins.then_inc(tr_done, 1)
                e_hi, e_lo = tokens(eT_hi, 1), tokens(eT_lo, 0)
                for j, c in enumerate(layers[f"ple{i}"]):
                    banks_free(c)
                    if c.reader == "act":
                        products(c, h_hi, h_lo, need=need_groups(n_b) if j == 0 else None)
                    else:
                        products(c, e_hi, e_lo, need=lambda kt: pe.wait_ge(t_lo, 2 + t0 + 1))

            ffn_ple(0, "norm4", "norm5")
            norm_t("norm6", SRC["norm6"])
            paired("kv", h_hi, h_lo, need_groups("norm6"))
            plain("f", h_hi, h_lo, None)
            transposes("norm6q", lambda t: xn[:, t, :], SRC["norm6"])
            plain("q", h_hi, h_lo, need_groups("norm6q"))
            pe.wait_ge(kv_ready, 2)
            pe.wait_ge(t_lo, 2 + T_AT["norm6q"] + 4)
            aux_groups("qk_fox", 0, lambda kt, t: qf[:, t, kt * P:(kt + 1) * P])
            aux_groups("qk_fox", 4, lambda kt, t: kf[:, t, kt * P:(kt + 1) * P])
            pe.wait_ge(lf_ready, 1)
            b = aux_bank("cum")
            t_.matmul(b[0:32, 0:T], lfd[:, 0].rearrange("p u h -> p (u h)"), tri[:, P:3 * P], start=True, stop=False)
            t_.matmul(b[0:32, 0:T], lfd[:, 1].rearrange("p u h -> p (u h)"), tri[:, 0:2 * P], start=False,
                      stop=True).then_inc(aux_tr, 1)
            pe.wait_ge(bias_rows, 1)
            attention("fox", lambda h, b, m, tok: qT[64 * b:64 * b + 64, 2 * h + m, tok * P:(tok + 1) * P],
                      lambda h, b, m, w: kTf[64 * b:64 * b + 64, 2 * h + m, 0:w],
                      lambda h, m, kb: vf[:, kb, (4 * h + 2 * (m % 2) + m // 2) * 64:(4 * h + 2 * (m % 2) + m // 2 + 1) * 64],
                      lambda h, m: ((4 * h + 2 * (m % 2) + m // 2) % 8) * 64)
            transposes("y_fox", lambda t: qf[:, t, :], SRC["y_fox"])
            plain("o", h_hi, h_lo, need_groups("y_fox"))
            ffn_ple(1, "norm7", "norm8")


_INS = ["x", "ffn1_norm", "ffn1_w1", "ffn1_w3", "ffn1_w2", "mix_norm", "w_in", "da_lambda", "da_head_norm",
        "cmp_pos", "cmp_w1", "cmp_w2", "w_proj_da", "w_proj_nsa", "w_out", "ffn2_norm", "ffn2_w1", "ffn2_w3",
        "ffn2_w2", "final_norm", "p_2", "mix_norm_2", "conv_w_pw1_2", "conv_b_pw1_2", "conv_w_dw_2", "conv_b_dw_2",
        "conv_ln_g_2", "conv_ln_b_2", "conv_w_pw2_2", "conv_b_pw2_2", "kv_norm_2", "w_kvf_2", "b_f_2",
        "attn_w_q_2", "attn_w_o_2", "ffn_norm_2", "ffn_w1_2", "ffn_w2_2", "ple_norm_2", "ple_w_gate_2",
        "ple_w_proj_2", "final_norm_2"]


def kernel(**inputs):
    import numpy as _np
    import concourse.bacc as _bacc
    from concourse import mybir as _mybir
    from concourse.bass_utils import run_bass_kernel_spmd as _run

    nc = _bacc.Bacc("TRN2", target_bir_lowering=False, num_devices=1)
    arrays, args = {}, {}
    for name in _INS:
        a = _np.ascontiguousarray(inputs[name])
        arrays[f"in_{name}_dram"] = a
        args[name] = nc.dram_tensor(f"in_{name}_dram", a.shape, _mybir.dt.from_np(a.dtype), kind="ExternalInput").ap()
    table = constants()[0]
    arrays["in_constants_dram"] = table
    consts = nc.dram_tensor("in_constants_dram", table.shape, _mybir.dt.from_np(table.dtype), kind="ExternalInput").ap()
    out = nc.dram_tensor("out_0_dram", (1, T, D), F32, kind="ExternalOutput").ap()
    block_kernel(nc, args, consts, out)
    r = _run(nc, [arrays], core_ids=[0])
    return r.results[0]["out_0_dram"]
```

```python
from contextlib import ExitStack

import numpy as np
import concourse.bass as bass
from concourse import mybir

F32 = mybir.dt.float32
F32R = mybir.dt.float32r
BF16 = mybir.dt.bfloat16
ALU = mybir.AluOpType
ACT = mybir.ActivationFunctionType
AX_X = mybir.AxisListType.X

P = 128
T = 256
TT = T // P
D = 1024
KD = D // P
F1 = 2816
F2 = 4096
CH = 512
RING = 4
UNIT = 4 * CH
AHEAD = 2
EPS = 1e-6
NEG = -1e30
N_CMP = 15
TAPS = 31
LAM_INIT = 0.2
QSCALE = 0.125
HEADS = 16

IN_KV = 4 * D
IN_KW = IN_KV + CH
KW_W = 256 + 48
IN_GATES = IN_KW + KW_W

GAINS = ["ffn1_norm", "mix_norm", "ffn2_norm", "mix_norm_2.0", "mix_norm_2.1", "kv_norm_2", "ffn_norm_2.0",
         "ffn_norm_2.1", "ple_norm_2.0", "ple_norm_2.1", "conv_ln_g_2", "conv_ln_b_2", "conv_b_dw_2", "da_head_norm"]
GAIN = {n: i for i, n in enumerate(GAINS)}


def constants():
    f = np.float32
    parts, at, off = [], {}, 0

    def put(name, a):
        nonlocal off
        a = np.asarray(a, f).reshape(P, -1)
        at[name] = (off, a.shape[1])
        off += a.shape[1]
        parts.append(a)

    i = np.arange(P)
    put("ident", np.eye(P))
    tri = (i[:, None] <= i[None, :])
    put("inv_d", np.full((P, P), 1.0 / D))
    put("tri", np.concatenate([np.zeros((P, P)), tri, np.ones((P, P))], 1))
    inv = (1.0 / (f(10000.0) ** (np.arange(0, 64, 2, dtype=f) / f(64)))).astype(f)
    pos = (i[:, None] + P * np.arange(TT)[None, :]).astype(f)
    ang = (pos[:, :, None] * inv).astype(f)
    put("cos", np.concatenate([np.cos(ang), np.cos(ang)], 2))
    put("sin", np.concatenate([-np.sin(ang), np.sin(ang)], 2))
    n = np.arange(16)
    valid = (n[None, None, :] * 16 + 31 <= pos[:, :, None]) & (n < N_CMP)
    put("cmask", np.where(valid, 0.0, NEG))
    put("cvalid", valid)
    put("onehot_c", (i[:, None] - 32 == n[None, :]))
    put("onehot_1", (i[:, None] == n[None, :]))
    put("causal", np.where(i[None, :] <= i[:, None], 0.0, NEG))
    return np.concatenate(parts, 1), at


CONST_AT = constants()[1]
N_CONST = CONST_AT["causal"][0]


class Chunk:

    def __init__(self, cols, width, units, reader="dve"):
        self.cols, self.width, self.units, self.reader = cols, width, units, reader
        self.second = {}


def plan(W):
    def kview(w):
        return w.rearrange("(kt p) n -> p kt n", p=P)

    def layer(name, chunks):
        for c in chunks:
            c.index = len(order)
            order.append(c)
            c.u0 = len(units)
            k = 0
            for nk in c.units:
                units.append((c, k, nk))
                k += nk
        layers[name] = chunks

    def plain(w, n, k_units, width=CH, start=0, reader="dve"):
        v = kview(w)
        return [Chunk([(v, start + i * width)], width, k_units, reader) for i in range(n)]

    def dual(a, b, n, b0=0):
        return [Chunk([(kview(a), i * 256), (kview(b), b0 + i * 256)], 256, [4, 4]) for i in range(n)]

    layers, order, units = {}, [], []
    kd, kf1, kf2 = [4, 4], [4] * 5 + [2], [4] * 8
    layer("ffn1_up", dual(W["ffn1_w1"][0], W["ffn1_w3"][0], F1 // 256))
    layer("ffn1_down", plain(W["ffn1_w2"][0], 2, kf1))
    w_in = W["w_in"][0]
    layer("in_a", plain(w_in, 8, kd))
    layer("in_b", plain(w_in, 1, kd, CH, IN_KV) + plain(w_in, 1, kd, KW_W, IN_KW))
    layer("cmp", [plain(W["cmp_w1"][0, i], 1, [8, 8], 256, 0, "act")[0] for i in range(2)])
    layer("gates", plain(w_in, 4, kd, CH, IN_GATES, "act"))
    layer("proj_da", plain(W["w_proj_da"][0], 2, kd))
    layer("proj_ns", plain(W["w_proj_nsa"][0], 2, kd))
    layer("out", plain(W["w_out"][0], 2, kd))
    layer("ffn2_up", dual(W["ffn2_w1"][0], W["ffn2_w3"][0], F1 // 256))
    layer("ffn2_down", plain(W["ffn2_w2"][0], 2, kf1))
    pw1 = W["conv_w_pw1_2"][0]
    layer("pw1", dual(pw1, pw1, 4, D))
    layer("pw2", plain(W["conv_w_pw2_2"][0], 2, kd))
    for i in range(2):
        layer(f"up{i}", plain(W["ffn_w1_2"][i], F2 // CH, kd))
        layer(f"down{i}", plain(W["ffn_w2_2"][i], 2, kf2))
        gate = plain(W["ple_w_gate_2"][i], 2, kd, reader="act")
        proj = plain(W["ple_w_proj_2"][i], 2, [2])
        layer(f"ple{i}", [gate[0], proj[0], gate[1], proj[1]])
        if i == 0:
            layer("kv", plain(W["w_kvf_2"], 4, kd))
            layer("f", plain(W["w_kvf_2"], 1, [8], HEADS, 2 * D))
            layer("q", plain(W["attn_w_q_2"][0], 2, kd))
            layer("o", plain(W["attn_w_o_2"][0], 2, kd))
    on_slot = [0] * RING
    for u, (c, _, _) in enumerate(units):
        if len(c.cols) == 2:
            on_slot[u % RING] += 1
        c.second[u] = on_slot[u % RING]
    read = {"dve": 0, "act": 0}
    for c in order:
        read[c.reader] += 1
        c.nth_read = read[c.reader]
    return layers, order, units


T_GROUPS = [("norm0", 4), ("ffn1_up", 11), ("norm1", 4), ("y_da", 4), ("y_ns", 4), ("m", 4), ("norm2", 4),
            ("ffn2_up", 11), ("norm3", 4), ("norm4", 4), ("up0", 16), ("norm5", 4), ("emb0", 1), ("norm6", 4),
            ("norm6q", 4), ("y_fox", 4), ("norm7", 4), ("up1", 16), ("norm8", 4), ("emb1", 1)]
T_AT = {}
_n = 0
for _name, _k in T_GROUPS:
    T_AT[_name] = _n
    _n += _k

A_GROUPS = [("const", 4), ("raw_cmp", 2), ("kk", 2), ("q_cmp", 4), ("hidden_cmp", 1), ("kc", 1), ("vc", 1), ("s_cmp", 1),
            ("p_cmp", 2), ("qk_da", 8), ("q_ns", 4), ("glu", 4), ("cum", 1), ("k_fox", 4), ("q_fox", 4)]
A_AT = {}
_n = 0
for _name, _k in A_GROUPS:
    A_AT[_name] = _n
    _n += _k


ACT_PARTS = {"ffn1_up": 0, "ffn2_up": 11, "pw1": 22, "up0": 26, "up1": 34}


class Steps:

    def __init__(self, eng, sem):
        self.eng, self.sem, self.n, self.loop = eng, sem, 0, 0

    def done(self, ins):
        ins.then_inc(self.sem, 1)
        self.n += 1
        self.eng.wait_ge(self.sem, self.n + self.loop)


def block_kernel(nc, W, consts, out):
    layers, order, units = plan(W)
    with ExitStack() as ctx:
        sb = lambda n, s, d=F32: ctx.enter_context(nc.sbuf_tensor(n, s, d))
        sem = lambda n: ctx.enter_context(nc.semaphore(n))

        def scoped(*specs):
            with ExitStack() as c:
                return [c.enter_context(nc.sbuf_tensor(n, sh, d)) for n, sh, d in specs]

        raw = sb("raw", [P, RING, UNIT])
        w_hi = sb("w_hi", [P, RING, UNIT], F32R)
        w_lo = sb("w_lo", [P, RING, UNIT], F32R)
        x = sb("x", [P, TT, D])
        hT_hi = sb("hT_hi", [P, KD, T], F32R)
        hT_lo = sb("hT_lo", [P, KD, T], F32R)
        blocks_hi, blocks_lo = scoped(("blocks_hi", [P, 2, 16, 30], F32R), ("blocks_lo", [P, 2, 16, 30], F32R))
        xn = sb("xn", [P, TT, D])
        s = sb("s", [P, 2, TT, CH])
        cst = sb("cst", [P, N_CONST])
        identb = sb("identb", [P, P], BF16)
        causalb = sb("causalb", [P, 2 * P], BF16)
        gcol = sb("gcol", [P, len(GAINS), KD])
        taps = sb("taps", [P, KD, TAPS])
        sums = sb("sums", [P, 4])
        mean = sb("mean", [P, 4])
        rstd = sb("rstd", [P, 4])
        half = sb("half", [P, 32])
        pos = sb("pos", [P, 2, 16])
        lam = sb("lam", [P, 8])
        negmax = sb("negmax", [P, 2, 4])
        rowsum = sb("rowsum", [P, 8, 4])
        rowinv = sb("rowinv", [P, 8, 4])
        weight = sb("weight", [P, 2, 4])

        gT_hi, gT_lo = scoped(("gT_hi", [P, F2 // P, T], F32R), ("gT_lo", [P, F2 // P, T], F32R))
        with ExitStack() as mix:
            msb = lambda n, sh, d=F32: mix.enter_context(nc.sbuf_tensor(n, sh, d))
            mixbuf = msb("mixbuf", [P, 4, TT, CH])
            yT_hi, yT_lo, gatebuf, m_buf = scoped(("yT_hi", [P, KD, T], F32R), ("yT_lo", [P, KD, T], F32R),
                                                  ("gatebuf", [P, 4, TT, CH], F32), ("m_buf", [P, TT, D], F32))
            v_da = msb("v_da", [P, TT, D])
            qa = msb("qa", [P, TT, D])
            qr = msb("qr", [P, TT, D])
            kT = msb("kT", [P, KD, T])
            ksT = msb("ksT", [P, 2, T])
            kwT = msb("kwT", [P, 2, T])
            vs = msb("vs", [P, TT, P])
            vw = msb("vw", [P, TT, P])
            gl = msb("gl", [P, TT, 48])
            gates = msb("gates", [P, TT, 48])
            w2k = msb("w2k", [P, 2, 2, 64])
            w2v = msb("w2v", [P, 2, 64])
            kcT = msb("kcT", [P, 2, 2, 16])
            vcb = msb("vcb", [P, 2, 4, 64])
            g1k = msb("g1k", [P, 2, 2, 16])
            g1v = msb("g1v", [P, 2, 2, 4, 32])
            cstat = msb("cstat", [P, 3, TT * HEADS])
            pcT = msb("pcT", [P, TT, 4, P])
        ubuf, conv, sq, b_pw1, stat, b_pw2, diag_w = scoped(
            ("ubuf", [P, KD, TAPS - 1 + T], F32), ("conv", [P, KD, T], F32), ("sq", [P, KD, T], F32),
            ("b_pw1", [P, 2 * D], F32), ("stat", [P, 2, TT], F32), ("b_pw2", [P, D], F32),
            ("diag_w", [P, TAPS, P], F32))
        qf, kf, vf, qT, kTf, bias_r, bias_l, cum, fz, lfd, b_f = scoped(
            ("qf", [P, TT, D], F32), ("kf", [P, TT, D], F32), ("vf", [P, TT, D], F32), ("qT", [P, KD, T], F32),
            ("kTf", [P, KD, T], F32), ("bias_r", [P, HEADS, T], F32), ("bias_l", [P, T], F32), ("cum", [48, T], F32),
            ("fz", [P, 4, TT, HEADS], F32), ("lfd", [P, TT, 3, HEADS], F32), ("b_f", [P, HEADS], F32))
        emb, eT_hi, eT_lo = scoped(("emb", [P, TT, 256], F32), ("eT_hi", [P, 2, T], F32R), ("eT_lo", [P, 2, T], F32R))
        qaT = qa[:].rearrange("p a b -> p (a b)").rearrange("p (k t) -> p k t", t=T)
        diag = kT[:].rearrange("p a b -> p (a b)").rearrange("p (i m q) -> p i m q", i=4, m=4)
        y_mix = mixbuf[:].rearrange("p a b c -> p (a b c)").rearrange("p (i t n) -> p i t n", i=2, t=TT)
        blk_full = s[:].rearrange("p a b c -> p (a b c)")[:, 0:960].rearrange("p (v j r) -> p v j r", v=2, j=16)
        g1 = s[:].rearrange("p a b c -> p (a b c)")[:, 1024:1536].rearrange("p (v n) -> p v n", v=2)
        sc = s[:].rearrange("p a b c -> p (a b c)")[:, 0:512].rearrange("p (t h n) -> p t h n", t=TT, h=HEADS)
        pc = xn[:].rearrange("p a b -> p (a b)")[:, 0:1024].rearrange("p (t h n) -> p t h n", t=TT, h=HEADS)
        kvd = xn[:].rearrange("p t (v g u d) -> p t v g u d", v=4, g=2, u=2)
        probs = s[:].rearrange("p a b c -> p a (b c)")
        probsT = xn
        rows_g = s[:].rearrange("p a b c -> p (a b c)")[:, 1024:1152]
        rows_w = s[:].rearrange("p a b c -> p (a b c)")[:, 0:1024]
        lam_in = s[:].rearrange("p a b c -> p (a b c)")[:, 1536:1792].rearrange("p (a d) -> p a d", a=4)
        causal_in = s[:].rearrange("p a b c -> p (a b c)")[:, 1408:1536]
        rows_p = s[:].rearrange("p a b c -> p (a b c)")[:, 1152:1408]
        cin = [s[:].rearrange("p a b c -> p (a b c)")[:, 1536 + 256 * k:1792 + 256 * k].rearrange("p (g m) -> p g m", g=2)
               for k in range(2)]
        fin_gain = xn[:, 1, :]
        cos_x = s[:].rearrange("p a b c -> p (a b c)")[:, 1024:1152].rearrange("p (t d) -> p t d", t=TT)
        sin_x = s[:].rearrange("p a b c -> p (a b c)")[:, 1152:1280].rearrange("p (t d) -> p t d", t=TT)
        ps = ctx.enter_context(nc.psum_tensor("ps", [P, 8, CH], F32))
        psT = ps[:, 4:8, :]

        def rot_tmp(t):
            return s[:].rearrange("p a b c -> p (a b c)")[:, 1536 + P * t:1536 + P * (t + 1)]

        def const(name):
            o, w = CONST_AT[name]
            return cst[:, o:o + w]

        ident = const("ident")
        tri = const("tri")
        cos = const("cos").rearrange("p (t d) -> p t d", t=TT)
        sin = const("sin").rearrange("p (t d) -> p t d", t=TT)
        cmask = const("cmask").rearrange("p (t n) -> p t n", t=TT)
        cvalid = const("cvalid").rearrange("p (t n) -> p t n", t=TT)

        raw_a = [sem(f"raw_a{i}") for i in range(RING)]
        raw_b = [sem(f"raw_b{i}") for i in range(RING)]
        hi_ready = sem("hi_ready")
        lo_ready = sem("lo_ready")
        unit_used = sem("unit_used")
        read_dve = sem("read_dve")
        read_act = sem("read_act")
        act_part = sem("act_part")
        g_ready = sem("g_ready")
        tr_done = sem("tr_done")
        t_hi = sem("t_hi")
        t_lo = sem("t_lo")
        aux_tr = sem("aux_tr")
        aux_cp = sem("aux_cp")
        dve_step = sem("dve_step")
        pool_step = sem("pool_step")
        act_step = sem("act_step")
        x_in = sem("x_in")
        const_in = sem("const_in")
        consts_ready = sem("consts_ready")
        x_half = sem("x_half")
        sum_dve = sem("sum_dve")
        sum_act = sem("sum_act")
        rstd_ready = sem("rstd_ready")
        xn_ready = sem("xn_ready")
        lam_sum = sem("lam_sum")
        lam_exp = sem("lam_exp")
        kv_ready = sem("kv_ready")
        blocks_ready = sem("blocks_ready")
        w2_in = sem("w2_in")
        cmp_sub = sem("cmp_sub")
        cmp_exp = sem("cmp_exp")
        cmp_p = sem("cmp_p")
        gl_ready = sem("gl_ready")
        gates_ready = sem("gates_ready")
        scores_done = sem("scores_done")
        max_done = sem("max_done")
        exp_done = sem("exp_done")
        probs_ready = sem("probs_ready")
        probs_tr = sem("probs_tr")
        probsT_ready = sem("probsT_ready")
        weight_ready = sem("weight_ready")
        pv_done = sem("pv_done")
        o_read = sem("o_read")
        y_sum = sem("y_sum")
        y_rstd = sem("y_rstd")
        conv_in = sem("conv_in")
        diag_ready = sem("diag_ready")
        diag_used = sem("diag_used")
        conv_pe = sem("conv_pe")
        conv_act = sem("conv_act")
        conv_dve = sem("conv_dve")
        conv_pool = sem("conv_pool")
        mean_done = sem("mean_done")
        centred = sem("centred")
        squared = sem("squared")
        var_done = sem("var_done")
        std_ready = sem("std_ready")
        std_spread = sem("std_spread")
        normed = sem("normed")
        silu_done = sem("silu_done")
        cT_hi = sem("cT_hi")
        cT_lo = sem("cT_lo")
        emb_in = sem("emb_in")
        bf_in = sem("bf_in")
        f_abs = sem("f_abs")
        f_exp = sem("f_exp")
        f_ln = sem("f_ln")
        lf_ready = sem("lf_ready")
        zero_ready = sem("zero_ready")
        bias_rows = sem("bias_rows")
        fin_in = sem("fin_in")
        out_ready = sem("out_ready")
        out_done = sem("out_done")

        def unit_view(t, u_slot, nk, w):
            return t[:, u_slot, 0:nk * w].rearrange("p (k w) -> p k w", w=w)

        def width(c):
            return c.width * len(c.cols)

        def first_unit(name):
            return layers[name][0].u0

        def pairs(name, lag):
            n = len(layers[name])
            loops = (n - lag) // 2
            return n, loops

        block = ctx.enter_context(nc.Block())

        @block.sync
        def _(sp):
            xv = W["x"].rearrange("b (t p) d -> p (b t) d", p=P)
            sp.dma_start(x[:], xv).then_inc(x_in, 16)

            def load(u, i=None, step=0, per=0, turns=0):
                c, k0, nk = units[u]
                shift = 0 if i is None else i
                if u >= RING or i is not None:
                    sp.wait_ge(lo_ready, u + 1 + per * shift)
                for q, (v, col) in enumerate(c.cols):
                    dst = raw[:, u % RING, 0:nk * width(c)].rearrange("p (k h w) -> p k h w", k=nk, w=c.width)[:, :, q, :]
                    cols = slice(col, col + c.width) if i is None else bass.ds(col + step * i, c.width)
                    sp.dma_start(dst, v[:, k0:k0 + nk, cols]).then_inc((raw_a, raw_b)[q][u % RING], 16)

            for name, chunks in layers.items():
                n, loops = pairs(name, 0)
                if n >= 4 and not name.startswith("ple"):
                    with sp.Fori(0, loops) as i:
                        for c in chunks[0:2]:
                            for u in range(c.u0, c.u0 + 2):
                                load(u, i, 2 * c.width, 4)
                    rest = chunks[2 * loops:]
                else:
                    rest = chunks
                for c in rest:
                    for u in range(c.u0, c.u0 + len(c.units)):
                        load(u)
            for h in range(2):
                sp.wait_ge(out_ready, h + 1)
                sp.dma_start(out.rearrange("b (t p) d -> p (b t) d", p=P)[:, :, h * CH:(h + 1) * CH],
                             x[:, :, h * CH:(h + 1) * CH]).then_inc(out_done, 16)
            sp.wait_ge(out_done, 32)

        def split_shape(u):
            c, _, nk = units[u]
            return slice(0, nk * width(c))

        NORM = {n: i for i, n in enumerate(["norm0", "norm1", "norm2", "fin0", "norm3", "norm4", "norm5", "norm6",
                                            "norm7", "norm8", "fin1"])}
        SRC = {n: i + 1 for i, n in enumerate(["y_da", "y_ns", "m", "y_fox"])}

        def half_ready(name, h):
            after = {"norm1": "ffn1_down", "norm2": "out", "fin0": "ffn2_down", "norm4": "pw2", "norm5": "down0",
                     "norm7": "o", "norm8": "down1"}
            if name == "norm0":
                return x_in, 16
            if name in after:
                return read_dve, 2 + layers[after[name]][h].nth_read
            return x_half, {"norm3": 0, "norm6": 2, "fin1": 4}[name] + h + 1
        ATT = {"da": 0, "ns": 8, "fox": 24}
        ATT_STEPS = {"da": 4, "ns": 8, "fox": 4}
        DVE_TILES = [0, 2, 4, 5]
        POOL_TILES = [1, 3]
        PE_TILES = [6, 7]
        TAP_BATCHES = [range(k, min(k + 8, TAPS)) for k in range(0, TAPS, 8)]

        @block.gpsimd
        def _(pool):
            g = nc.gpsimd
            steps = Steps(pool, pool_step)
            for k in range(RING):
                g.memset(half[:, k:k + 1], -0.5).then_inc(lo_ready, 1)
            for k in range(RING):
                g.memset(half[:, RING + k:RING + k + 1], -0.5).then_inc(unit_used, 1)
            for k in range(2):
                g.memset(half[:, 8 + k:9 + k], -0.5).then_inc(read_dve, 1)
                g.memset(half[:, 10 + k:11 + k], -0.5).then_inc(read_act, 1)
                g.memset(half[:, 12 + k:13 + k], -0.5).then_inc(t_lo, 1)
            steps.done(g.memset(half[:, 14:32], -0.5))

            def rsqrt(n, name):
                pool.wait_ge(sum_dve, 2 * n + 2)
                pool.wait_ge(sum_act, 2 * n + 2)
                steps.done(g.tensor_tensor(out=mean[:, 2:4], in0=sums[:, 0:2], in1=sums[:, 2:4], op=ALU.add))
                steps.done(g.tensor_scalar(mean[:, 0:2], mean[:, 2:4], 1.0 / D, EPS, ALU.mult, ALU.add))
                g.tensor_tensor(out=rstd[:, 0:2], in0=mean[:, 0:2], in1=half[:, 0:2], op=ALU.pow).then_inc(rstd_ready, 1)

            rsqrt(NORM["norm0"], "norm0")
            pool.wait_ge(read_dve, 2 + layers["ffn1_down"][1].nth_read)
            w2 = W["cmp_w2"][0]
            for d_ in range(2):
                pool.dma_start(w2k[:, :, d_, :], w2[0].rearrange("(k p) d -> p k d", p=P)).then_inc(w2_in, 16)
            pool.dma_start(w2v[:], w2[1].rearrange("(k p) d -> p k d", p=P)).then_inc(w2_in, 16)
            rsqrt(NORM["norm1"], "norm1")
            n = TT * ATT_STEPS["ns"]
            for q in range(n):
                st = ATT["ns"] + q
                pool.wait_ge(weight_ready, q + 1)
                if q >= 2:
                    pool.wait_ge(probs_tr, st - 1)
                g.tensor_tensor(out=diag[:, st % 2], in0=ident.unsqueeze(1).broadcast_to([P, 4, P]),
                                in1=weight[:, st % 2, :].unsqueeze(2).broadcast_to([P, 4, P]),
                                op=ALU.mult).then_inc(probs_ready, 1)
            pool.wait_ge(y_sum, 1)
            steps.done(g.tensor_scalar(cstat[:, 1, 0:16], cstat[:, 0, 0:16], 1.0 / P, EPS, ALU.mult, ALU.add))
            g.tensor_tensor(out=cstat[:, 2, 0:16], in0=cstat[:, 1, 0:16], in1=half[:, 0:16], op=ALU.pow).then_inc(y_rstd, 1)
            rsqrt(NORM["norm2"], "norm2")
            pool.wait_ge(read_dve, 2 + layers["out"][1].nth_read)
            pool.dma_start(fin_gain, W["final_norm"].rearrange("(a d) -> a d", a=1).partition_broadcast(P)).then_inc(fin_in, 16)
            pool.wait_ge(read_dve, 2 + layers["ffn2_down"][1].nth_read)
            pool.dma_start(b_pw1[:], W["conv_b_pw1_2"].partition_broadcast(P)).then_inc(conv_in, 16)
            pool.dma_start(b_pw2[:], W["conv_b_pw2_2"].partition_broadcast(P)).then_inc(conv_in, 16)
            g.memset(ubuf[:, :, 0:TAPS - 1], 0.0).then_inc(zero_ready, 1)
            rsqrt(NORM["fin0"], "fin0")
            rsqrt(NORM["norm3"], "norm3")
            for ct in POOL_TILES:
                pool.wait_ge(aux_cp, A_AT["glu"] + ct // 2 + 1)
                steps.done(g.tensor_scalar(conv[:, ct], ubuf[:, ct, 0:T], taps[:, ct, 0:1],
                                           gcol[:, GAIN["conv_b_dw_2"], ct:ct + 1], ALU.mult, ALU.add))
                for k in range(1, TAPS):
                    steps.done(g.tensor_scalar(sq[:, ct], ubuf[:, ct, k:k + T], taps[:, ct, k:k + 1], 0.0,
                                               ALU.mult, ALU.add))
                    last = g.tensor_tensor(out=conv[:, ct], in0=conv[:, ct], in1=sq[:, ct], op=ALU.add)
                    if k < TAPS - 1:
                        steps.done(last)
                last.then_inc(conv_pool, 1)
            pool.wait_ge(std_ready, 1)
            steps.done(g.tensor_tensor(out=stat[:, 1, :], in0=stat[:, 0, :], in1=half[:, 0:2], op=ALU.pow))
            g.tensor_tensor(out=diag_w[:, 0:2, :], in0=ident.unsqueeze(1).broadcast_to([P, TT, P]),
                            in1=stat[:, 1, :].unsqueeze(2).broadcast_to([P, TT, P]), op=ALU.mult).then_inc(std_ready, 1)
            rsqrt(NORM["norm4"], "norm4")
            pool.wait_ge(read_dve, 2 + layers["down0"][1].nth_read)
            pool.dma_start(emb[:], W["p_2"][0].rearrange("b (t p) d -> p (b t) d", p=P)).then_inc(emb_in, 16)
            rsqrt(NORM["norm5"], "norm5")
            pool.wait_ge(x_half, 4)
            pool.dma_start(b_f[:], W["b_f_2"].rearrange("(a d) -> a d", a=1).partition_broadcast(P)).then_inc(bf_in, 16)
            steps.done(g.memset(bias_r[:], 0.0))
            steps.done(g.memset(bias_l[:], 0.0))
            steps.done(g.memset(bias_l[32:48], -1.0))
            g.tensor_copy(bias_r[0:16], const("onehot_1")[0:16].unsqueeze(2).broadcast_to([16, HEADS, T])).then_inc(zero_ready, 1)
            pool.wait_ge(zero_ready, 2)
            rsqrt(NORM["norm6"], "norm6")
            pool.wait_ge(read_dve, 2 + layers["o"][1].nth_read)
            pool.dma_start(fin_gain, W["final_norm_2"].rearrange("(a d) -> a d", a=1).partition_broadcast(P)).then_inc(fin_in, 16)
            rsqrt(NORM["norm7"], "norm7")
            pool.wait_ge(read_dve, 2 + layers["down1"][1].nth_read)
            pool.dma_start(emb[:], W["p_2"][1].rearrange("b (t p) d -> p (b t) d", p=P)).then_inc(emb_in, 16)
            rsqrt(NORM["norm8"], "norm8")
            rsqrt(NORM["fin1"], "fin1")

        @block.scalar
        def _(act):
            a = nc.scalar
            loads = [(cst[:], consts[:, 0:N_CONST]), (causal_in, consts[:, N_CONST:N_CONST + P])]
            for i, n in enumerate(GAINS):
                base, _, layer = n.partition(".")
                src = W[base]
                src = src[int(layer)] if layer else src
                if base == "da_head_norm":
                    src = src[0]
                elif len(src.shape) == 2:
                    src = src[0].rearrange("(a d) -> a d", d=P)
                else:
                    src = src.rearrange("(a d) -> a d", d=P)
                loads.append((rows_g[KD * i:KD * i + KD, :], src))
            loads.append((rows_w[0:TAPS, :], W["conv_w_dw_2"][0]))
            for k in range(2):
                loads.append((rows_p[0:16, k * P:(k + 1) * P], W["cmp_pos"][0, k].rearrange("(j h) d -> j (h d)", h=2)))
            loads.append((lam_in, W["da_lambda"].rearrange("a b c -> a (b c)").partition_broadcast(P)
                          .rearrange("q p (b c) -> q (p b) c", b=4)))
            for dst, src in loads:
                act.dma_start(dst, src).then_inc(const_in, 16)
            n_const = 16 * len(loads)

            def split(u, i=None, per=0):
                c, _, _ = units[u]
                k = 0 if i is None else i
                turn = per // RING
                act.wait_ge(unit_used, u + 1 + per * k)
                act.wait_ge(raw_a[u % RING], 16 * (u // RING + 1) + 16 * turn * k)
                if len(c.cols) == 2:
                    act.wait_ge(raw_b[u % RING], 16 * c.second[u] + 16 * turn * k)
                n = split_shape(u)
                a.activation(w_hi[:, u % RING, n], raw[:, u % RING, n], ACT.Copy).then_inc(hi_ready, 1)

            def split_next(c, i=None, per=0):
                end = c.u0 + len(c.units)
                for u in range(end - len(c.units) + AHEAD, min(end + AHEAD, len(units))):
                    split(u, i, per)

            def chunk_done(c, i=None, per=0):
                act.wait_ge(unit_used, RING + c.u0 + len(c.units) + (per * i if i is not None else 0))

            def hi_group(t, dst, scale=1.0, bank=None, i=None, per=0, ordered=True):
                k = 0 if i is None else per * i
                act.wait_ge(consts_ready, 1)
                act.wait_ge(tr_done, t + 1 + k)
                return a.activation(dst, bank, ACT.Copy, scale=scale)

            def hi_groups(name, dst, gain=None, groups=range(4)):
                for j in groups:
                    t = T_AT[name] + j
                    act.wait_ge(tr_done, t + 1)
                    bank = psT[:, j, :].rearrange("p (k t) -> p k t", k=2)
                    for k in range(2):
                        kt = 2 * j + k
                        sc_ = 1.0 if gain is None else gcol[:, GAIN[gain], kt:kt + 1]
                        ins = a.activation(dst[:, kt, :], bank[:, k, :], ACT.Copy, scale=sc_)
                    ins.then_inc(t_hi, 1)

            def norm(name, gain, h):
                n = NORM[name]
                if gain:
                    hi_groups(name, hT_hi, gain, range(2 * h, 2 * h + 2))
                if n or h:
                    act.wait_ge(sum_act, 2 * n + h)
                act.wait_ge(*half_ready(name, h))
                a.activation(xn[:, 0, CH:2 * CH], x[:, 1, h * CH:(h + 1) * CH], ACT.Square,
                             accum_out=sums[:, 2 * h + 1:2 * h + 2]).then_inc(sum_act, 1)
                if h == 1 and gain:
                    act.wait_ge(rstd_ready, n + 1)

            def residual(name, norm_name, gain):
                for h, c in enumerate(layers[name]):
                    split_next(c)
                    if h == 1:
                        norm(norm_name, gain, 0)
                norm(norm_name, gain, 1)

            def up(name, func, w):
                chunks = layers[name]
                n, loops = pairs(name, 1)
                groups = w // 256
                loops = (n - 2) // 2
                dst = gT_hi[:].rearrange("p k t -> p (k t)")

                def one(j, i=None):
                    c = chunks[j]
                    k = 0 if i is None else i
                    split_next(c, i, 4)
                    chunk_done(c, i, 4)
                    for t in range(TT):
                        ins = a.activation(s[:, c.index % 2, t, 0:w], ps[:, 2 * (c.index % 2) + t, 0:w], func,
                                           scale=rstd[:, t:t + 1])
                    ins.then_inc(act_part, 1)
                    if j > 0:
                        lag(j - 1, i)

                def lag(j, i=None):
                    for q in range(groups):
                        t = T_AT[name] + j * groups + q
                        at = (j * groups + q) * 512
                        if i is None:
                            d = dst[:, at:at + 512]
                        else:
                            d = dst[:, bass.ds(at + i * (2 * groups * 512), 512)]
                        hi_group(t, d, 1.0, psT[:, t % 2, :], i, 2 * groups).then_inc(t_hi, 1)

                one(0)
                with act.Fori(0, loops) as i:
                    one(1, i)
                    one(2, i)
                for j in range(1 + 2 * loops, n):
                    one(j)
                lag(n - 1)

            def attention(kind):
                for tok in range(TT):
                    w = P * (tok + 1)
                    for q in range(ATT_STEPS[kind]):
                        st = ATT[kind] + tok * ATT_STEPS[kind] + q
                        act.wait_ge(max_done, st + 1)
                        if st >= 2:
                            act.wait_ge(probs_tr, st - 1)
                        for b in range(2):
                            for m in range(2):
                                o = m * 2 + b if kind == "fox" else b * 2 + m
                                ins = a.activation(probs[:, st % 2, (2 * b + m) * T:(2 * b + m) * T + w],
                                                   ps[:, 2 * (st % 2) + b, m * w:m * w + w], ACT.Exp,
                                                   bias=negmax[:, st % 2, 2 * b + m:2 * b + m + 1],
                                                   accum_out=rowsum[:, st % 8, o:o + 1])
                        ins.then_inc(exp_done, 1)

            split(0)
            split(1)
            act.wait_ge(lam_sum, 1)
            a.activation(lam[:, 2:4], lam[:, 0:2], ACT.Exp).then_inc(lam_exp, 1)
            act.wait_ge(x_in, 16)
            act.wait_ge(consts_ready, 1)
            for h in range(2):
                norm("norm0", "ffn1_norm", h)
            up("ffn1_up", ACT.Silu, 256)
            residual("ffn1_down", "norm1", "mix_norm")
            with act.Fori(0, 4) as i:
                for c in layers["in_a"][0:2]:
                    split_next(c, i, 4)
            for c in layers["in_b"]:
                split_next(c)
            act.wait_ge(gl_ready, 1)
            a.activation(gates[:], gl[:], ACT.Sigmoid).then_inc(gates_ready, 1)
            for v, c in enumerate(layers["cmp"]):
                split_next(c)
                chunk_done(c)
                a.activation(g1[0:30, v, :], ps[0:30, 2 * (c.index % 2), 0:256], ACT.Gelu_apprx_tanh).then_inc(read_act, 1)
            act.wait_ge(cmp_sub, 1)
            a.activation(sc[:], sc[:], ACT.Exp).then_inc(cmp_exp, 1)
            attention("da")
            attention("ns")

            def gate_chunk(c, dst, i=None):
                chunk_done(c, i, 4)
                for t in range(TT):
                    ins = a.activation(dst(t), ps[:, 2 * (c.index % 2) + t, :], ACT.Sigmoid, scale=rstd[:, t:t + 1])
                ins.then_inc(read_act, 1)

            with act.Fori(0, 2) as i:
                for j, c in enumerate(layers["gates"][0:2]):
                    split_next(c, i, 4)
                    act.wait_ge(o_read, 8)
                    gate_chunk(c, lambda t, j=j, i=i: gatebuf[:].rearrange("p a b c -> p (a b c)")[
                        :, bass.ds((j * TT + t) * CH + i * (2 * TT * CH), CH)], i)
            hi_groups("y_da", yT_hi, "da_head_norm")
            for c in layers["proj_da"]:
                split_next(c)
            hi_groups("y_ns", hT_hi)
            for c in layers["proj_ns"]:
                split_next(c)
            hi_groups("m", hT_hi)
            residual("out", "norm2", "ffn2_norm")
            up("ffn2_up", ACT.Silu, 256)
            residual("ffn2_down", "fin0", None)
            for h in range(2):
                norm("norm3", "mix_norm_2.0", h)

            def diagonals(ct, n, ks):
                for k in ks:
                    ins = a.activation(diag_w[:, k, :], ident, ACT.Copy, scale=taps[:, ct, k:k + 1])
                ins.then_inc(diag_ready, 1)

            for j, c in enumerate(layers["pw1"]):
                split_next(c)
                act.wait_ge(read_dve, 2 + c.nth_read)
                for t in range(TT):
                    ins = a.activation(s[:, c.index % 2, t, 256:512], s[:, c.index % 2, t, 256:512], ACT.Sigmoid)
                ins.then_inc(act_part, 1)
                diagonals(PE_TILES[0], j, TAP_BATCHES[j])
            for b, taps_ in enumerate(TAP_BATCHES):
                if b < len(TAP_BATCHES) - 1:
                    act.wait_ge(diag_used, b + 1)
                else:
                    act.wait_ge(conv_pe, 1)
                diagonals(PE_TILES[1], b, taps_)
            for n, ct in enumerate(PE_TILES):
                act.wait_ge(conv_pe, n + 1)
                a.activation(conv[:, ct], ps[:, n, 0:T], ACT.Identity,
                             bias=gcol[:, GAIN["conv_b_dw_2"], ct:ct + 1]).then_inc(conv_act, 1)
            for q in range(KD // 2):
                act.wait_ge(centred, q + 1)
                a.activation(sq[:, 2 * q:2 * q + 2], conv[:, 2 * q:2 * q + 2], ACT.Square).then_inc(squared, 1)

            def silu(ct):
                if ct % 2 == 0:
                    act.wait_ge(normed, ct // 2 + 1)
                a.activation(conv[:, ct], conv[:, ct], ACT.Silu, scale=gcol[:, GAIN["conv_ln_g_2"], ct:ct + 1],
                             bias=gcol[:, GAIN["conv_ln_b_2"], ct:ct + 1]).then_inc(silu_done, 1)

            silu(0)
            for ct in range(KD):
                if ct + 1 < KD:
                    silu(ct + 1)
                act.wait_ge(silu_done, ct + 1)
                a.activation(hT_hi[:, ct, :], conv[:, ct], ACT.Copy).then_inc(cT_hi, 1)
            residual("pw2", "norm4", "ffn_norm_2.0")

            def ffn_ple(i, n_b, n_c, gain_c):
                up(f"up{i}", ACT.Relu, 512)
                residual(f"down{i}", n_b, f"ple_norm_2.{i}")
                act.wait_ge(tr_done, T_AT[f"emb{i}"] + 1)
                a.activation(eT_hi[:].rearrange("p k t -> p (k t)"), psT[:, 0, :], ACT.Copy).then_inc(t_hi, 1)
                for j, c in enumerate(layers[f"ple{i}"]):
                    split_next(c)
                    if j == 2:
                        norm(n_c, gain_c, 0)
                    if c.reader == "act":
                        gate_chunk(c, lambda t, j=j: s[:, j // 2, t, :])
                norm(n_c, gain_c, 1)

            ffn_ple(0, "norm5", "norm6", "kv_norm_2")
            for c in layers["kv"] + layers["f"]:
                split_next(c)
            act.wait_ge(f_abs, 1)
            a.activation(fz[:, 2], fz[:, 1], ACT.Exp).then_inc(f_exp, 1)
            act.wait_ge(f_exp, 1)
            a.activation(fz[:, 3], fz[:, 2], ACT.Ln, bias=1.0).then_inc(f_ln, 1)
            chunk_done(layers["f"][0])
            hi_groups("norm6q", hT_hi, "mix_norm_2.1")
            for c in layers["q"]:
                split_next(c)
            attention("fox")
            hi_groups("y_fox", hT_hi)
            residual("o", "norm7", "ffn_norm_2.1")
            ffn_ple(1, "norm8", "fin1", None)

        @block.vector
        def _(dve):
            v = nc.vector
            steps = Steps(dve, dve_step)

            def split(u, i=None, per=0):
                k = 0 if i is None else i
                dve.wait_ge(hi_ready, u + 1 + per * k)
                n = split_shape(u)
                v.tensor_tensor(w_lo[:, u % RING, n], raw[:, u % RING, n], w_hi[:, u % RING, n].bitcast(F32),
                                ALU.subtract).then_inc(lo_ready, 1)

            def split_next(c, i=None, per=0):
                end = c.u0 + len(c.units)
                for u in range(end - len(c.units) + AHEAD, min(end + AHEAD, len(units))):
                    split(u, i, per)

            def chunk_done(c, i=None, per=0):
                dve.wait_ge(unit_used, RING + c.u0 + len(c.units) + (per * i if i is not None else 0))

            def bank(c, t):
                return ps[:, 2 * (c.index % 2) + t, :]

            def lo_groups(name, hi, lo, gain=None, groups=range(4)):
                for j in groups:
                    t = T_AT[name] + j
                    dve.wait_ge(t_hi, t + 1)
                    bk = psT[:, j, :].rearrange("p (k t) -> p k t", k=2)
                    for k in range(2):
                        kt = 2 * j + k
                        g_ = 1.0 if gain is None else gcol[:, GAIN[gain], kt:kt + 1]
                        ins = v.scalar_tensor_tensor(out=lo[:, kt, :], in0=bk[:, k, :], scalar=g_,
                                                     in1=hi[:, kt, :].bitcast(F32), op0=ALU.mult, op1=ALU.subtract)
                    ins.then_inc(t_lo, 1)

            def norm(name, gain, h):
                n = NORM[name]
                if gain:
                    lo_groups(name, hT_hi, hT_lo, gain, range(2 * h, 2 * h + 2))
                if n or h:
                    dve.wait_ge(sum_dve, 2 * n + h)
                dve.wait_ge(*half_ready(name, h))
                v.tensor_tensor_reduce(out=xn[:, 0, 0:CH], in0=x[:, 0, h * CH:(h + 1) * CH],
                                       in1=x[:, 0, h * CH:(h + 1) * CH], scale=1.0, scalar=0.0, op0=ALU.mult,
                                       op1=ALU.add, accum_out=sums[:, 2 * h:2 * h + 1]).then_inc(sum_dve, 1)
                if h == 1:
                    dve.wait_ge(rstd_ready, n + 1)

            def final_norm(name, sem_, nth):
                dve.wait_ge(fin_in, 16 * nth)
                for h in range(2):
                    for t in range(TT):
                        xh = x[:, t, h * CH:(h + 1) * CH]
                        ins = v.scalar_tensor_tensor(out=xh, in0=xh, scalar=rstd[:, t:t + 1],
                                                     in1=fin_gain[:, h * CH:(h + 1) * CH], op0=ALU.mult, op1=ALU.mult)
                    ins.then_inc(sem_, 1)

            def up(name, w, off):
                chunks = layers[name]
                n = len(chunks)
                loops = (n - 2) // 2
                groups = w // 256
                lo = gT_lo[:].rearrange("p k t -> p (k t)")
                hi = gT_hi[:].rearrange("p k t -> p (k t)")
                part0 = ACT_PARTS[name]

                def one(j, i=None):
                    c = chunks[j]
                    k = 0 if i is None else 2 * i
                    split_next(c, i, 4)
                    dve.wait_ge(act_part, part0 + j + 1 + k)
                    for t in range(TT):
                        ins = v.scalar_tensor_tensor(out=s[:, c.index % 2, t, 0:w], in0=bank(c, t)[:, off:off + w],
                                                     scalar=rstd[:, t:t + 1], in1=s[:, c.index % 2, t, 0:w],
                                                     op0=ALU.mult, op1=ALU.mult)
                    ins.then_inc(read_dve, 1)
                    if j > 0:
                        lag(j - 1, i)

                def lag(j, i=None):
                    for q in range(groups):
                        t = T_AT[name] + j * groups + q
                        at = (j * groups + q) * 512
                        k = 0 if i is None else 2 * groups * i
                        sl = slice(at, at + 512) if i is None else bass.ds(at + i * (2 * groups * 512), 512)
                        dve.wait_ge(t_hi, t + 1 + k)
                        v.tensor_tensor(lo[:, sl], psT[:, t % 2, :], hi[:, sl].bitcast(F32),
                                        ALU.subtract).then_inc(t_lo, 1)

                one(0)
                with dve.Fori(0, loops) as i:
                    one(1, i)
                    one(2, i)
                for j in range(1 + 2 * loops, n):
                    one(j)
                lag(n - 1)

            def residual(name, scale, norm_name, gain):
                for h, c in enumerate(layers[name]):
                    split_next(c)
                    if h == 1:
                        norm(norm_name, gain, 0)
                    chunk_done(c)
                    for t in range(TT):
                        ins = v.scalar_tensor_tensor(out=x[:, t, h * CH:(h + 1) * CH], in0=bank(c, t), scalar=scale,
                                                     in1=x[:, t, h * CH:(h + 1) * CH], op0=ALU.mult, op1=ALU.add)
                    ins.then_inc(read_dve, 1)
                norm(norm_name, gain, 1)

            def rotary(src, dst, heads, t, cos, sin):
                tmp = s[:].rearrange("p a b c -> p (a b c)")[:, CH * t:CH * t + heads * 64].rearrange(
                    "p (h d) -> p h d", d=64)
                sv = src.rearrange("p (h d) -> p h d", d=64)
                dv = dst.rearrange("p (h d) -> p h d", d=64)
                v.tensor_tensor(dv, sv, cos[:, t, :].unsqueeze(1).broadcast_to([P, heads, 64]), ALU.mult)
                v.tensor_tensor(tmp[:, :, 0:32], sv[:, :, 32:64],
                                sin[:, t, 0:32].unsqueeze(1).broadcast_to([P, heads, 32]), ALU.mult)
                steps.done(v.tensor_tensor(tmp[:, :, 32:64], sv[:, :, 0:32],
                                           sin[:, t, 32:64].unsqueeze(1).broadcast_to([P, heads, 32]), ALU.mult))
                return v.tensor_tensor(dv, dv, tmp, ALU.add)

            def aux(name, j=0):
                n = A_AT[name] + j
                dve.wait_ge(aux_tr, n + 1)
                return psT[:, n % 4, :]

            def copied(ins):
                ins.then_inc(aux_cp, 1)

            def copy_groups(name, first, dst, scale):
                for j in range(4):
                    b = aux(name, first + j)
                    copied(v.tensor_scalar(dst[:, 2 * j:2 * j + 2, :], b.rearrange("p (k t) -> p k t", k=2), scale,
                                           None, ALU.mult))

            n_const = 16 * (len(GAINS) + 6)
            dve.wait_ge(const_in, n_const)
            v.tensor_copy(identb[:], ident)
            v.memset(causalb[:, 0:P], 0.0)
            v.tensor_copy(causalb[:, P:2 * P], causal_in)
            lp = lam_in.rearrange("p (a b) c -> p a b c", a=2)
            steps.done(v.tensor_tensor(lam_in[:, 0:4:2, :], lp[:, :, 0, :], lp[:, :, 1, :], ALU.mult))
            v.tensor_reduce(lam[:, 0:2], lam_in[:, 0:4:2, :], AX_X, ALU.add).then_inc(lam_sum, 1)
            b = aux("const", 0)
            copied(v.tensor_copy(gcol[:].rearrange("p g k -> p (g k)"), b[:, 0:KD * len(GAINS)]))
            for h in range(2):
                b = aux("const", 1 + h)
                copied(v.tensor_copy(taps[:, 4 * h:4 * h + 4, :],
                                     b[:, 0:4 * P].rearrange("p (k w) -> p k w", k=4)[:, :, 0:TAPS]))
            copied(v.tensor_copy(pos[:].rearrange("p k j -> p (k j)"), aux("const", 3)[:, 0:32]))
            dve.wait_ge(aux_cp, 4)
            g_da = gcol[:, GAIN["da_head_norm"], :]
            steps.done(v.tensor_scalar(g_da, g_da, 1.0 - LAM_INIT, None, ALU.mult))
            dve.wait_ge(lam_exp, 1)
            steps.done(v.tensor_tensor(lam[:, 5:6], lam[:, 3:4], lam[:, 2:3], ALU.subtract))
            v.tensor_scalar(lam[:, 4:5], lam[:, 5:6], -LAM_INIT, None, ALU.add).then_inc(consts_ready, 1)
            split(0)
            split(1)
            for h in range(2):
                norm("norm0", "ffn1_norm", h)
            up("ffn1_up", 256, 256)
            residual("ffn1_down", 0.5, "norm1", "mix_norm")
            for t in range(TT):
                v.tensor_scalar(cos_x[:, t, :], cos[:, t, :], rstd[:, t:t + 1], None, ALU.mult)
                ins = v.tensor_scalar(sin_x[:, t, :], sin[:, t, :], rstd[:, t:t + 1], None, ALU.mult)
            steps.done(ins)

            mix_flat = mixbuf[:].rearrange("p a b c -> p (a b c)")
            in_a, in_b = layers["in_a"], layers["in_b"]
            before = steps.n
            with dve.Fori(0, 2) as i:
                steps.loop = i * 4
                for j, c in enumerate(in_a[0:2]):
                    split_next(c, i, 4)
                    chunk_done(c, i, 4)
                    for t in range(TT):
                        ins = rotary(bank(c, t), mix_flat[:, bass.ds((j * TT + t) * CH + i * (2 * TT * CH), CH)], 8, t,
                                     cos_x, sin_x)
                    ins.then_inc(read_dve, 1)
            assert steps.n - before == 4
            steps.n, steps.loop = before + 8, 0
            for j, c in enumerate(in_a[4:8]):
                split_next(c)
                chunk_done(c)
                dst = (v_da, v_da, qa, qa)[j]
                lo_col = (j % 2) * CH
                for t in range(TT):
                    ins = v.tensor_scalar(dst[:, t, lo_col:lo_col + CH], bank(c, t), rstd[:, t:t + 1], None, ALU.mult)
                ins.then_inc(read_dve, 1)
                if j >= 2:
                    dve.wait_ge(read_dve, 2 + c.nth_read)
                    for t in range(TT):
                        ins = rotary(qa[:, t, lo_col:lo_col + CH], qr[:, t, lo_col:lo_col + CH], 8, t, cos, sin)
                    steps.done(ins)
            c = in_b[0]
            split_next(c)
            chunk_done(c)
            for t in range(TT):
                for q in range(2):
                    v.tensor_scalar(kvd[:, t, q], bank(c, t)[:, q * P:(q + 1) * P].rearrange("p (g d) -> p g d", g=2)
                                    .unsqueeze(2).broadcast_to([P, 2, 2, 64]), rstd[:, t:t + 1], None, ALU.mult)
                v.tensor_scalar(vs[:, t, :], bank(c, t)[:, 3 * P:4 * P], rstd[:, t:t + 1], None, ALU.mult)
                ins = rotary(bank(c, t)[:, 2 * P:3 * P], rot_tmp(t), 2, t, cos_x, sin_x)
                if t == TT - 1:
                    ins.then_inc(read_dve, 1)
                    dve.wait_ge(read_dve, 2 + c.nth_read)
                else:
                    steps.done(ins)
            for t in range(TT):
                steps.done(v.tensor_copy(kvd[:, t, 2], rot_tmp(t).rearrange("p (g d) -> p g d", g=2)
                                         .unsqueeze(2).broadcast_to([P, 2, 2, 64])))
            c = in_b[1]
            split_next(c)
            chunk_done(c)
            for t in range(TT):
                v.tensor_scalar(vw[:, t, :], bank(c, t)[:, P:2 * P], rstd[:, t:t + 1], None, ALU.mult)
                v.tensor_scalar(gl[:, t, :], bank(c, t)[:, 2 * P:2 * P + 48], rstd[:, t:t + 1], None, ALU.mult)
                ins = rotary(bank(c, t)[:, 0:P], rot_tmp(t), 2, t, cos_x, sin_x)
                if t == TT - 1:
                    ins.then_inc(read_dve, 1)
                    dve.wait_ge(read_dve, 2 + c.nth_read)
                else:
                    steps.done(ins)
            for t in range(TT):
                ins = v.tensor_copy(kvd[:, t, 3], rot_tmp(t).rearrange("p (g d) -> p g d", g=2)
                                    .unsqueeze(2).broadcast_to([P, 2, 2, 64]))
                if t == 0:
                    ins.then_inc(gl_ready, 1)
            ins.then_inc(kv_ready, 1)

            for k in range(2):
                b = aux("raw_cmp", k).rearrange("p (g t) -> p g t", g=2)
                for h in range(2):
                    ins = v.tensor_copy(cin[k][64 * h:64 * h + 64], b[64 * h:64 * h + 64, :, h:T:2])
                copied(ins)
            copied(v.tensor_copy(ksT[:].rearrange("p g t -> p (g t)"), aux("kk", 0)))
            copied(v.tensor_copy(kwT[:].rearrange("p g t -> p (g t)"), aux("kk", 1)))
            dve.wait_ge(aux_cp, A_AT["raw_cmp"] + 2)
            for k in range(2):
                for g_ in range(2):
                    src = cin[k][:, g_, :].rearrange("p (n j) -> p j n", j=8)
                    for jh in range(2):
                        ins = v.tensor_tensor(blk_full[:, k, 8 * jh:8 * jh + 8, 15 * g_:15 * g_ + 15],
                                              src[:, :, jh:jh + 15],
                                              pos[:, k, 8 * jh:8 * jh + 8].unsqueeze(2).broadcast_to([P, 8, 15]), ALU.add)
            steps.done(ins)
            steps.done(v.tensor_copy(blocks_hi[:], blk_full))
            v.tensor_tensor(blocks_lo[:], blk_full, blocks_hi[:].bitcast(F32), ALU.subtract).then_inc(blocks_ready, 1)
            copy_groups("q_cmp", 0, kT, QSCALE)
            for c in layers["cmp"]:
                split_next(c)
            b = aux("hidden_cmp")
            v.memset(g1k[:], 0.0)
            v.memset(g1v[:], 0.0)
            v.memset(kcT[:], 0.0)
            steps.done(v.memset(vcb[:], 0.0))
            bh = b[:, 0:128].rearrange("p (v k r) -> p v k r", v=2, k=2)[:, :, :, 0:30]
            for kt in range(2):
                v.tensor_copy(g1k[:, kt, :, 0:15], bh[:, 0, kt, :].rearrange("p (g n) -> p g n", g=2))
                for g_ in range(2):
                    ins = v.tensor_copy(g1v[:, kt, g_, :, 0:15],
                                        bh[:, 1, kt, 15 * g_:15 * g_ + 15].unsqueeze(1).broadcast_to([P, 4, 15]))
            copied(ins)
            b = aux("kc")[:, 0:32].rearrange("p (g n) -> p g n", g=2)
            for h in range(2):
                ins = v.tensor_copy(kcT[64 * h:64 * h + 64, :, h, :], b[64 * h:64 * h + 64])
            copied(ins)
            b = aux("vc")[:, 0:128].rearrange("p (g d) -> p g d", g=2)
            for j in range(4):
                ins = v.tensor_copy(vcb[32 * j:32 * j + 32, :, j, :], b[32 * j:32 * j + 32])
            copied(ins)
            b = aux("s_cmp")
            for t in range(TT):
                ins = v.tensor_tensor(sc[:, t], ps[:, 0, t * 256:(t + 1) * 256].rearrange("p (h n) -> p h n", h=HEADS),
                                      cmask[:, t, :].unsqueeze(1).broadcast_to([P, HEADS, 16]), ALU.add)
            copied(ins)
            dve.wait_ge(aux_cp, A_AT["s_cmp"] + 1)
            scf = sc.rearrange("p t h n -> p (t h) n")
            steps.done(v.tensor_reduce(cstat[:, 0, :], scf, AX_X, ALU.max))
            v.tensor_tensor(scf, scf, cstat[:, 0, :].unsqueeze(2).broadcast_to([P, 32, 16]), ALU.subtract).then_inc(cmp_sub, 1)
            v.memset(pc, 0.0)
            dve.wait_ge(cmp_exp, 1)
            steps.done(v.tensor_reduce(cstat[:, 0, :], scf, AX_X, ALU.add))
            steps.done(v.reciprocal(cstat[:, 1, :], cstat[:, 0, :]))
            dve.wait_ge(gates_ready, 1)
            steps.done(v.tensor_tensor(cstat[:, 2, :].rearrange("p (t h) -> p t h", t=TT),
                                       cstat[:, 1, :].rearrange("p (t h) -> p t h", t=TT),
                                       gates[:].rearrange("p t (h r) -> p t h r", r=3)[:, :, :, 0], ALU.mult))
            for t in range(TT):
                ins = v.tensor_tensor(sc[:, t], sc[:, t], cvalid[:, t, :].unsqueeze(1).broadcast_to([P, HEADS, 16]), ALU.mult)
            steps.done(ins)
            for t in range(TT):
                ins = v.tensor_tensor(pc[:, t, :, 0:16], sc[:, t], cstat[:, 2, t * HEADS:(t + 1) * HEADS].unsqueeze(2)
                                      .broadcast_to([P, HEADS, 16]), ALU.mult)
            ins.then_inc(cmp_p, 1)
            for j in range(2):
                copied(v.tensor_copy(pcT[:, j].rearrange("p q t -> p (q t)"), aux("p_cmp", j)))
            copy_groups("qk_da", 0, qaT, QSCALE)
            copy_groups("qk_da", 4, kT, 1.0)

            def attention(kind, o_out):
                n = ATT_STEPS[kind]
                total = TT * n

                def info(q):
                    tok = q // n
                    return ATT[kind] + q, tok, q % n, P * (tok + 1)

                def maxima(q):
                    st, tok, _, w = info(q)
                    dve.wait_ge(scores_done, st + 1)
                    v.tensor_reduce(negmax[:, st % 2, :], ps[:, 2 * (st % 2):2 * (st % 2) + 2, 0:2 * w]
                                    .rearrange("p b (m w) -> p b m w", m=2), AX_X, ALU.max,
                                    negate=True).then_inc(max_done, 1)

                def scale(q):
                    st, tok, h, w = info(q)
                    dve.wait_ge(exp_done, st + 1)
                    pr = probs[:, st % 2].rearrange("p (m w) -> p m w", m=4)
                    steps_r = v.reciprocal(rowinv[:, st % 8, :], rowsum[:, st % 8, :])
                    if kind == "fox":
                        steps_r.then_inc(probs_ready, 1)
                        return
                    steps.done(steps_r)
                    if kind == "da":
                        steps.done(v.scalar_tensor_tensor(out=weight[:, st % 2, 0:2], in0=rowinv[:, st % 8, 2:4],
                                                          scalar=lam[:, 4:5], in1=rowsum[:, st % 8, 0:2],
                                                          op0=ALU.mult, op1=ALU.mult))
                        for m in range(2):
                            ins = v.scalar_tensor_tensor(out=pr[:, m, 0:w], in0=pr[:, 2 + m, 0:w],
                                                         scalar=weight[:, st % 2, m:m + 1], in1=pr[:, m, 0:w],
                                                         op0=ALU.mult, op1=ALU.add)
                        ins.then_inc(probs_ready, 1)
                    else:
                        if q >= 2:
                            dve.wait_ge(probs_ready, st - 1)
                        v.tensor_tensor(weight[:, st % 2, :].rearrange("p (b m) -> p b m", b=2),
                                        rowinv[:, st % 8, :].rearrange("p (b m) -> p b m", b=2),
                                        gates[:, tok, 6 * h:6 * h + 6].rearrange("p (b r) -> p b r", b=2)[:, :, 1:3],
                                        ALU.mult).then_inc(weight_ready, 1)

                def copy_t(q):
                    st, tok, h, w = info(q)
                    blocks = (2 if kind == "da" else 4) * (tok + 1)
                    dve.wait_ge(probs_tr, st + 1)
                    if q >= 2:
                        dve.wait_ge(pv_done, st - 1)
                    v.tensor_copy(probsT[:, st % 2, 0:blocks * P],
                                  ps[:, 6:8, :].rearrange("p a b -> p (a b)")[:, 0:blocks * P]).then_inc(probsT_ready, 1)

                def read_o(tok, b):
                    st = ATT[kind] + tok * n + (b + 1) * n // 2
                    dve.wait_ge(pv_done, st)
                    o_out(tok, b, st % 8).then_inc(o_read, 1)

                for q in range(total + 4):
                    if q < total:
                        maxima(q)
                    if 1 <= q < total + 1:
                        scale(q - 1)
                    if 2 <= q < total + 2:
                        copy_t(q - 2)
                    done = q - 3
                    if done > 0 and done % (n // 2) == 0 and done <= total:
                        read_o((done - 1) // n, ((done - 1) % n) // (n // 2))

            y_da, y_ns = y_mix[:, 0], y_mix[:, 1]

            def o_da(tok, b, st):
                s0 = (tok * 4 + 2 * b) % 8
                return v.tensor_tensor(y_da[:, tok, b * CH:(b + 1) * CH].rearrange("p (s m e) -> p s m e", s=2, m=2),
                                       ps[:, 4 + b, :].rearrange("p (s m e) -> p s m e", s=2, m=2),
                                       rowinv[:, s0:s0 + 2, 0:2].unsqueeze(3).broadcast_to([P, 2, 2, P]), ALU.mult)

            def o_ns(tok, b, st):
                return v.tensor_copy(y_ns[:, tok, b * CH:(b + 1) * CH], ps[:, 4 + b, :])

            attention("da", o_da)
            copy_groups("q_ns", 0, qaT, QSCALE)
            attention("ns", o_ns)
            dve.wait_ge(o_read, 8)
            sqv = xn[:].rearrange("p t n -> p (t n)")
            yv = y_da.rearrange("p t n -> p (t n)")
            steps.done(v.tensor_tensor(sqv, yv, yv, ALU.mult))
            v.tensor_reduce(cstat[:, 0, 0:16], sqv.rearrange("p (h e) -> p h e", e=P), AX_X, ALU.add).then_inc(y_sum, 1)
            dve.wait_ge(y_rstd, 1)
            yh = yv.rearrange("p (h e) -> p h e", e=P)
            v.tensor_tensor(yh, yh, cstat[:, 2, 0:16].unsqueeze(2).broadcast_to([P, 16, P]), ALU.mult).then_inc(xn_ready, 2)

            with dve.Fori(0, 2) as i:
                for c in layers["gates"][0:2]:
                    split_next(c, i, 4)
            lo_groups("y_da", yT_hi, yT_lo, "da_head_norm")

            def merged(name, first, at):
                for n, c in enumerate(layers[name]):
                    split_next(c)
                    chunk_done(c)
                    for t in range(TT):
                        g_ = gatebuf[:, at + n, t, :]
                        d = m_buf[:, t, n * CH:(n + 1) * CH]
                        if first:
                            ins = v.tensor_tensor(d, bank(c, t), g_, ALU.mult)
                        else:
                            ins = v.tensor_tensor(g_, bank(c, t), g_, ALU.mult)
                    ins.then_inc(read_dve, 1)
                    if not first:
                        dve.wait_ge(read_dve, 2 + c.nth_read)
                        for t in range(TT):
                            d = m_buf[:, t, n * CH:(n + 1) * CH]
                            ins = v.tensor_tensor(d, d, gatebuf[:, at + n, t, :], ALU.add)
                        if n == 1:
                            ins.then_inc(xn_ready, 1)

            merged("proj_da", True, 0)
            lo_groups("y_ns", hT_hi, hT_lo)
            merged("proj_ns", False, 2)
            lo_groups("m", hT_hi, hT_lo)
            residual("out", 1.0, "norm2", "ffn2_norm")
            up("ffn2_up", 256, 256)
            residual("ffn2_down", 0.5, "fin0", None)
            final_norm("fin0", x_half, 1)

            for h in range(2):
                norm("norm3", "mix_norm_2.0", h)
            dve.wait_ge(conv_in, 32)
            dve.wait_ge(zero_ready, 1)
            bp = b_pw1[:].rearrange("p (h n) -> p h n", h=2)
            chunks = layers["pw1"]
            todo = [(ct, k) for ct in DVE_TILES[:2] for k in range(TAPS)]
            todo += [(ct, k) for k in range(TAPS) for ct in DVE_TILES[2:]]
            last_step = {}

            def convolve(n):
                for ct, k in todo[:n]:
                    if k:
                        dve.wait_ge(dve_step, last_step[ct])
                        ins = v.scalar_tensor_tensor(out=conv[:, ct], in0=ubuf[:, ct, k:k + T],
                                                     scalar=taps[:, ct, k:k + 1], in1=conv[:, ct],
                                                     op0=ALU.mult, op1=ALU.add)
                    else:
                        dve.wait_ge(aux_cp, A_AT["glu"] + ct // 2 + 1)
                        ins = v.tensor_scalar(conv[:, ct], ubuf[:, ct, 0:T], taps[:, ct, 0:1],
                                              gcol[:, GAIN["conv_b_dw_2"], ct:ct + 1], ALU.mult, ALU.add)
                    if k < TAPS - 1:
                        ins.then_inc(dve_step, 1)
                        steps.n += 1
                        last_step[ct] = steps.n
                    else:
                        ins.then_inc(conv_dve, 1)
                del todo[:n]

            for j, c in enumerate(chunks):
                split_next(c)
                chunk_done(c)
                for t in range(TT):
                    ins = v.scalar_tensor_tensor(out=s[:, c.index % 2, t, :].rearrange("p (h n) -> p h n", h=2),
                                                 in0=bank(c, t).rearrange("p (h n) -> p h n", h=2),
                                                 scalar=rstd[:, t:t + 1], in1=bp[:, :, 256 * j:256 * j + 256],
                                                 op0=ALU.mult, op1=ALU.add)
                ins.then_inc(read_dve, 1)
                dve.wait_ge(act_part, ACT_PARTS["pw1"] + j + 1)
                for t in range(TT):
                    ins = v.tensor_tensor(s[:, c.index % 2, t, 0:256], s[:, c.index % 2, t, 0:256],
                                          s[:, c.index % 2, t, 256:512], ALU.mult)
                ins.then_inc(g_ready, 1)
                if j:
                    convolve(9)
                copied(v.tensor_copy(ubuf[:, 2 * j:2 * j + 2, TAPS - 1:TAPS - 1 + T],
                                     aux("glu", j).rearrange("p (k t) -> p k t", k=2)))
                if j < 3:
                    convolve(9)
            convolve(len(todo))
            dve.wait_ge(mean_done, 1)
            for q in range(KD // 2):
                cp = conv[:, 2 * q:2 * q + 2]
                v.tensor_tensor(cp, cp, ps[:, 2, 0:T].unsqueeze(1).broadcast_to([P, 2, T]),
                                ALU.subtract).then_inc(centred, 1)
            for t in range(TT):
                ins = v.tensor_tensor(x[:, t, :], x[:, t, :], b_pw2[:], ALU.add)
            ins.then_inc(dve_step, 1)
            steps.n += 1
            dve.wait_ge(var_done, 1)
            v.tensor_scalar(stat[:, 0, :], ps[:, 3, 0:TT], EPS, None, ALU.add).then_inc(std_ready, 1)
            dve.wait_ge(std_spread, 1)
            dve.wait_ge(dve_step, steps.n)
            for q in range(KD // 2):
                cp = conv[:, 2 * q:2 * q + 2]
                v.tensor_tensor(cp, cp, ps[:, 2, 0:T].unsqueeze(1).broadcast_to([P, 2, T]), ALU.mult).then_inc(normed, 1)
            for ct in range(KD):
                dve.wait_ge(cT_hi, ct + 1)
                v.tensor_tensor(hT_lo[:, ct, :], conv[:, ct], hT_hi[:, ct, :].bitcast(F32), ALU.subtract).then_inc(cT_lo, 1)
            residual("pw2", 1.0, "norm4", "ffn_norm_2.0")

            def ffn_ple(i, n_b, n_c, gain_c):
                up(f"up{i}", 512, 0)
                residual(f"down{i}", 1.0, n_b, f"ple_norm_2.{i}")
                dve.wait_ge(t_hi, T_AT[f"emb{i}"] + 1)
                v.tensor_tensor(eT_lo[:].rearrange("p k t -> p (k t)"), psT[:, 0, :],
                                eT_hi[:].rearrange("p k t -> p (k t)").bitcast(F32), ALU.subtract).then_inc(t_lo, 1)
                for j, c in enumerate(layers[f"ple{i}"]):
                    split_next(c)
                    if j == 2:
                        norm(n_c, gain_c, 0)
                    if c.reader == "act":
                        continue
                    dve.wait_ge(read_act, 2 + layers[f"ple{i}"][j - 1].nth_read)
                    chunk_done(c)
                    n = j // 2
                    for t in range(TT):
                        ins = v.tensor_tensor(s[:, n, t, :], s[:, n, t, :], bank(c, t), ALU.mult)
                    ins.then_inc(read_dve, 1)
                    dve.wait_ge(read_dve, 2 + c.nth_read)
                    for t in range(TT):
                        d = x[:, t, n * CH:(n + 1) * CH]
                        ins = v.tensor_tensor(d, d, s[:, n, t, :], ALU.add)
                    ins.then_inc(x_half, 1)
                norm(n_c, gain_c, 1)

            ffn_ple(0, "norm5", "norm6", "kv_norm_2")
            for j, c in enumerate(layers["kv"]):
                split_next(c)
                chunk_done(c)
                dst = (kf, kf, vf, vf)[j]
                for t in range(TT):
                    ins = v.tensor_scalar(dst[:, t, (j % 2) * CH:(j % 2 + 1) * CH], bank(c, t), rstd[:, t:t + 1],
                                          None, ALU.mult)
                ins.then_inc(read_dve, 1)
            c = layers["f"][0]
            split_next(c)
            chunk_done(c)
            dve.wait_ge(bf_in, 16)
            for t in range(TT):
                ins = v.scalar_tensor_tensor(out=fz[:, 0, t], in0=bank(c, t)[:, 0:HEADS], scalar=rstd[:, t:t + 1],
                                             in1=b_f[:], op0=ALU.mult, op1=ALU.add)
            ins.then_inc(read_dve, 1)
            dve.wait_ge(read_dve, 2 + c.nth_read)
            steps.done(v.tensor_scalar(fz[:, 1], fz[:, 0], -1.0, None, ALU.mult))
            v.tensor_tensor(fz[:, 1], fz[:, 1], fz[:, 0], ALU.min).then_inc(f_abs, 1)
            steps.done(v.tensor_scalar(fz[:, 0], fz[:, 0], 0.0, None, ALU.min))
            lo_groups("norm6q", hT_hi, hT_lo, "mix_norm_2.1")
            dve.wait_ge(f_ln, 1)
            for d_ in range(3):
                ins = v.tensor_tensor(lfd[:, :, d_, :], fz[:, 0], fz[:, 3], ALU.subtract)
            ins.then_inc(lf_ready, 1)
            for n, c in enumerate(layers["q"]):
                split_next(c)
                if n == 1:
                    copied(v.tensor_copy(cum[:], aux("cum")[0:48, 0:T]))
                    copy_groups("k_fox", 0, kTf, 1.0)
                    dve.wait_ge(aux_cp, A_AT["cum"] + 1)
                    dve.wait_ge(zero_ready, 2)
                    v.tensor_copy(bias_l[0:16, :], cum[0:16, :])
                    for h in range(4):
                        v.tensor_tensor(bias_r[32:48, 4 * h:4 * h + 4], cum[32:48, :].unsqueeze(1).broadcast_to([16, 4, T]),
                                        const("onehot_c")[32:48, 4 * h:4 * h + 4].unsqueeze(2).broadcast_to([16, 4, T]),
                                        ALU.mult).then_inc(bias_rows, 1)
                chunk_done(c)
                for t in range(TT):
                    ins = v.tensor_scalar(qf[:, t, n * CH:(n + 1) * CH], bank(c, t), rstd[:, t:t + 1], None, ALU.mult)
                ins.then_inc(read_dve, 1)
            dve.wait_ge(read_dve, 2 + layers["q"][1].nth_read)
            v.tensor_copy(weight[:, 0, 1:2], qf[:, 0, 0:1]).then_inc(kv_ready, 1)
            copy_groups("q_fox", 0, qT, QSCALE)

            def o_fox(tok, b, st):
                s0 = (tok * 4 + 2 * b) % 8
                return v.tensor_tensor(qf[:, tok, b * CH:(b + 1) * CH].rearrange("p (h e) -> p h e", e=64),
                                       ps[:, 4 + b, :].rearrange("p (h e) -> p h e", e=64),
                                       rowinv[:, s0:s0 + 2, :].rearrange("p s m -> p (s m)").unsqueeze(2)
                                       .broadcast_to([P, 8, 64]), ALU.mult)

            attention("fox", o_fox)
            dve.wait_ge(o_read, 12)
            v.tensor_copy(weight[:, 0, 1:2], qf[:, 0, 0:1]).then_inc(xn_ready, 1)
            lo_groups("y_fox", hT_hi, hT_lo)
            residual("o", 1.0, "norm7", "ffn_norm_2.1")
            ffn_ple(1, "norm8", "fin1", None)
            final_norm("fin1", out_ready, 2)

        @block.tensor
        def _(pe):
            t_ = nc.tensor

            def products(c, lhs_hi, lhs_lo, i=None, per=0, need=None, rows=P, tiles=TT, before=None):
                k_ = 0 if i is None else per * i
                w = width(c)
                n_k = sum(c.units)
                k0 = 0
                for q, nk in enumerate(c.units):
                    u = c.u0 + q
                    if before and before[0] == q:
                        before[1]()
                    pe.wait_ge(lo_ready, RING + u + 1 + k_)
                    hi, lo = (unit_view(x_, u % RING, nk, w) for x_ in (w_hi, w_lo))
                    for k in range(nk):
                        kt = k0 + k
                        if need and kt % 2 == 0:
                            need(kt)
                        for t in range(tiles):
                            o = ps[0:rows, 2 * (c.index % 2) + t, 0:w]
                            ah, al = lhs_hi(kt, t), lhs_lo(kt, t)
                            t_.matmul(o, ah, hi[:, k, :], start=(kt == 0), stop=False)
                            t_.matmul(o, ah, lo[:, k, :], start=False, stop=False)
                            ins = t_.matmul(o, al, hi[:, k, :], start=False, stop=(kt == n_k - 1))
                    ins.then_inc(unit_used, 1)
                    k0 += nk

            def banks_free(c):
                if c.index >= 2:
                    b = order[c.index - 2]
                    pe.wait_ge({"dve": read_dve, "act": read_act}[b.reader], 2 + b.nth_read)

            def tokens(t, hi):
                return lambda kt, tok: t[:, kt, tok * P:(tok + 1) * P]

            h_hi, h_lo = tokens(hT_hi, 1), tokens(hT_lo, 0)
            g_hi, g_lo = tokens(gT_hi, 1), tokens(gT_lo, 0)
            y_hi, y_lo = tokens(yT_hi, 1), tokens(yT_lo, 0)

            def need_groups(name):
                return lambda kt: pe.wait_ge(t_lo, 2 + T_AT[name] + kt // 2 + 1)

            def transposes(name, src, src_count):
                if src_count:
                    pe.wait_ge(xn_ready, src_count)
                if T_AT[name]:
                    pe.wait_ge(t_lo, 2 + T_AT[name])
                for j in range(4):
                    for k in range(2):
                        for t in range(TT):
                            kt = 2 * j + k
                            ins = t_.transpose(psT[:, j, (k * TT + t) * P:(k * TT + t + 1) * P],
                                               src(t)[:, kt * P:(kt + 1) * P], ident)
                    ins.then_inc(tr_done, 1)

            def norm_t(name, h):
                if h == 0 and T_AT[name]:
                    pe.wait_ge(t_lo, 2 + T_AT[name])
                pe.wait_ge(*half_ready(name, h))
                for j in (2 * h, 2 * h + 1):
                    for k in range(2):
                        for t in range(TT):
                            kt = 2 * j + k
                            ins = t_.transpose(psT[:, j, (k * TT + t) * P:(k * TT + t + 1) * P],
                                               x[:, t, kt * P:(kt + 1) * P], ident)
                    ins.then_inc(tr_done, 1)

            def plain(name, lhs_hi, lhs_lo, need, norm_in=None, norm_out=None):
                for j, c in enumerate(layers[name]):
                    banks_free(c)
                    before = None
                    if j == 0 and norm_in:
                        before = (1, lambda: norm_t(norm_in, 1))
                    if j == len(layers[name]) - 1 and norm_out:
                        before = (len(c.units) - (1 if len(c.units) < 4 else 2), lambda: norm_t(norm_out, 0))
                    products(c, lhs_hi, lhs_lo, need=need if j == 0 else None, before=before)

            def paired(name, lhs_hi, lhs_lo, need=None, norm_in=None):
                chunks = layers[name]
                banks_free(chunks[0])
                if norm_in:
                    products(chunks[0], lhs_hi, lhs_lo, need=need, before=(1, lambda: norm_t(norm_in, 1)))
                    banks_free(chunks[1])
                    products(chunks[1], lhs_hi, lhs_lo)
                    chunks = chunks[2:]
                else:
                    banks_free(chunks[1])
                free = {"dve": read_dve, "act": read_act}[chunks[0].reader]
                with pe.Fori(0, len(chunks) // 2) as i:
                    for j, c in enumerate(chunks[0:2]):
                        pe.wait_ge(free, c.nth_read + i * 2)
                        products(c, lhs_hi, lhs_lo, i, 4)

            def up(name, w, norm_name):
                chunks = layers[name]
                n = len(chunks)
                loops = (n - 2) // 2
                groups = w // 256

                def tr(j, i=None):
                    c = chunks[j]
                    k_ = 0 if i is None else 2 * i
                    pe.wait_ge(read_dve, 2 + c.nth_read + k_)
                    for q in range(groups):
                        t0 = T_AT[name] + j * groups + q
                        pe.wait_ge(t_lo, t0 + 1 + k_ * groups)
                        for f in range(2):
                            for t in range(TT):
                                ins = t_.transpose(psT[:, t0 % 2, (f * TT + t) * P:(f * TT + t + 1) * P],
                                                   s[:, c.index % 2, t, (2 * q + f) * P:(2 * q + f + 1) * P], ident)
                        ins.then_inc(tr_done, 1)

                need = need_groups(norm_name)
                banks_free(chunks[0])
                products(chunks[0], h_hi, h_lo, need=need, before=(1, lambda: norm_t(norm_name, 1)))
                banks_free(chunks[1])

                def one(j, i=None):
                    c = chunks[j]
                    pe.wait_ge(read_dve, c.nth_read + (0 if i is None else 2 * i))
                    products(c, h_hi, h_lo, i, 4)
                    tr(j - 1, i)

                with pe.Fori(0, loops) as i:
                    one(1, i)
                    one(2, i)
                for j in range(1 + 2 * loops, n):
                    one(j)
                tr(n - 1)

            def down(name, up_name, norm_out):
                need = lambda kt: pe.wait_ge(t_lo, 2 + T_AT[up_name] + kt // 2 + 1)
                plain(name, g_hi, g_lo, need, norm_out=norm_out)

            def aux_bank(name, j=0):
                n = A_AT[name] + j
                if n >= 4:
                    pe.wait_ge(aux_cp, n - 3)
                return psT[:, n % 4, :]

            def aux_groups(name, first, src):
                for j in range(4):
                    b = aux_bank(name, first + j)
                    for k in range(2):
                        for t in range(TT):
                            ins = t_.transpose(b[:, (k * TT + t) * P:(k * TT + t + 1) * P], src(2 * j + k, t), ident)
                    ins.then_inc(aux_tr, 1)

            pe.wait_ge(pool_step, 1)
            pe.wait_ge(const_in, 16 * (len(GAINS) + 6))
            n_g = KD * len(GAINS)
            t_.transpose(aux_bank("const")[:, 0:n_g], rows_g[0:n_g, :], ident[0:n_g, 0:n_g]).then_inc(aux_tr, 1)
            for h in range(2):
                b = aux_bank("const", 1 + h)
                for k in range(4):
                    kt = 4 * h + k
                    ins = t_.transpose(b[:, k * P:k * P + TAPS], rows_w[0:TAPS, kt * P:(kt + 1) * P], ident[0:TAPS, 0:TAPS])
                ins.then_inc(aux_tr, 1)
            b = aux_bank("const", 3)
            for k in range(2):
                ins = t_.transpose(b[:, 16 * k:16 * k + 16], rows_p[0:16, k * P:(k + 1) * P], ident[0:16, 0:16])
            ins.then_inc(aux_tr, 1)
            pe.wait_ge(aux_cp, 4)

            norm_t("norm0", 0)
            up("ffn1_up", 256, "norm0")
            down("ffn1_down", "ffn1_up", "norm1")
            paired("in_a", h_hi, h_lo, need_groups("norm1"), "norm1")
            plain("in_b", h_hi, h_lo, None)

            pe.wait_ge(kv_ready, 1)
            for k in range(2):
                b = aux_bank("raw_cmp", k)
                for g_ in range(2):
                    for t in range(TT):
                        ins = t_.transpose(b[:, (g_ * TT + t) * P:(g_ * TT + t + 1) * P],
                                           kvd[:, t, k, g_].rearrange("p u d -> p (u d)"), ident)
                ins.then_inc(aux_tr, 1)
            for k in range(2):
                b = aux_bank("kk", k)
                for g_ in range(2):
                    for t in range(TT):
                        ins = t_.transpose(b[:, (g_ * TT + t) * P:(g_ * TT + t + 1) * P],
                                           kvd[:, t, 2 + k, g_].rearrange("p u d -> p (u d)"), ident)
                ins.then_inc(aux_tr, 1)
            aux_groups("q_cmp", 0, lambda kt, t: qa[:, t, kt * P:(kt + 1) * P])
            pe.wait_ge(blocks_ready, 1)
            for k, c in enumerate(layers["cmp"]):
                banks_free(c)
                products(c, lambda kt, t, k=k: blocks_hi[:, k, kt, :], lambda kt, t, k=k: blocks_lo[:, k, kt, :],
                         rows=30, tiles=1)
            pe.wait_ge(read_act, 2 + layers["cmp"][1].nth_read)
            b = aux_bank("hidden_cmp")
            for k in range(2):
                for kt in range(2):
                    ins = t_.transpose(b[:, (k * 2 + kt) * 32:(k * 2 + kt) * 32 + 30], g1[0:30, k, kt * P:(kt + 1) * P],
                                       ident[0:30, 0:30])
            ins.then_inc(aux_tr, 1)
            pe.wait_ge(aux_cp, A_AT["hidden_cmp"] + 1)
            pe.wait_ge(w2_in, 48)
            b = aux_bank("kc")
            for kt in range(2):
                ins = t_.matmul(b[:, 0:32], w2k[:, kt].rearrange("p u d -> p (u d)"),
                                g1k[:, kt].rearrange("p g n -> p (g n)"), start=(kt == 0), stop=(kt == 1))
            ins.then_inc(aux_tr, 1)
            b = aux_bank("vc")
            for g_ in range(2):
                for kt in range(2):
                    ins = t_.matmul(b[:, g_ * 64:(g_ + 1) * 64], g1v[:, kt, g_].rearrange("p u n -> p (u n)"),
                                    w2v[:, kt], start=(kt == 0), stop=(kt == 1))
            ins.then_inc(aux_tr, 1)
            pe.wait_ge(aux_cp, A_AT["vc"] + 1)
            pe.wait_ge(read_act, 2 + layers["cmp"][1].nth_read)
            for t in range(TT):
                for hp in range(8):
                    at = (t * 8 + hp) * 32
                    ins = t_.matmul(ps[:, 0, at:at + 32], kT[:, hp, t * P:(t + 1) * P],
                                    kcT[:, hp // 4].rearrange("p u n -> p (u n)"), start=True, stop=True)
            ins.then_inc(aux_tr, 1)
            pe.wait_ge(cmp_p, 1)
            for t in range(TT):
                b = aux_bank("p_cmp", t)
                for q in range(4):
                    ins = t_.transpose(b[:, q * P:(q + 1) * P], pc[:, t, 4 * q:4 * q + 4, :].rearrange("p h n -> p (h n)"),
                                       ident)
                ins.then_inc(aux_tr, 1)

            aux_groups("qk_da", 0, lambda kt, t: mixbuf[:, kt // 4, t, (kt % 4) * P:(kt % 4 + 1) * P])
            aux_groups("qk_da", 4, lambda kt, t: mixbuf[:, 2 + kt // 4, t, (kt % 4) * P:(kt % 4 + 1) * P])

            def attention(kind, q_op, k_op, v_op, o_at):
                n = ATT_STEPS[kind]
                total = TT * n

                def scores(q):
                    st, tok, h = ATT[kind] + q, q // n, q % n
                    w = P * (tok + 1)
                    if kind == "fox" and q < n:
                        pe.wait_ge(bias_rows, h + 1)
                    if q >= 2:
                        pe.wait_ge(exp_done, st - 1)
                    for b in range(2):
                        for m in range(2):
                            o = ps[:, 2 * (st % 2) + b, m * w:(m + 1) * w]
                            first = True
                            if kind == "fox":
                                t_.matmul(o, bias_l[:, tok * P:(tok + 1) * P], bias_r[:, 4 * h + 2 * m + b, 0:w],
                                          start=True, stop=False)
                                first = False
                            t_.matmul(o, q_op(h, b, m, tok), k_op(h, b, m, w), start=first, stop=False)
                            ins = t_.matmul(o, identb[:], causalb[:, 2 * P - w:2 * P], start=False, stop=True)
                    ins.then_inc(scores_done, 1)

                def turn(q):
                    st, tok = ATT[kind] + q, q // n
                    pe.wait_ge(probs_ready, st + 1)
                    if q >= 1:
                        pe.wait_ge(probsT_ready, st)
                    maps = 2 if kind == "da" else 4
                    for m in range(maps):
                        for kb in range(tok + 1):
                            r = m * (tok + 1) + kb
                            o = ps[:, 6 + r // 4, (r % 4) * P:(r % 4 + 1) * P]
                            pr = probs[:, st % 2, m * T + kb * P:m * T + (kb + 1) * P]
                            if kind == "ns":
                                ins = t_.matmul(o, pr, diag[:, st % 2, m, :], start=True, stop=True)
                            else:
                                ins = t_.transpose(o, pr, ident)
                    ins.then_inc(probs_tr, 1)

                def pv(q):
                    st, tok, h = ATT[kind] + q, q // n, q % n
                    pe.wait_ge(probsT_ready, st + 1)
                    bank = h // (n // 2)
                    fresh = h % (n // 2) == 0
                    if fresh and (kind != "da" or tok > 0):
                        reads = {"da": 0, "ns": 4, "fox": 8}[kind] + 2 * tok + bank
                        pe.wait_ge(o_read, reads - 1)
                    if fresh and kind == "ns":
                        for quad in range(2):
                            t_.matmul(ps[:, 4 + bank, quad * 256:(quad + 1) * 256], pcT[:, tok, 2 * bank + quad, :],
                                      vcb[:, bank].rearrange("p j d -> p (j d)"), start=(quad == 0), stop=False,
                                      skip_group_check=True)
                        fresh = False
                    maps = 2 if kind == "da" else 4
                    for m in range(maps):
                        for kb in range(tok + 1):
                            r = m * (tok + 1) + kb
                            rhs = v_op(h, m, kb)
                            at = o_at(h, m)
                            last = h % (n // 2) == n // 2 - 1 and m == maps - 1 and kb == tok
                            ins = t_.matmul(ps[:, 4 + bank, at:at + rhs.shape[-1]], probsT[:, st % 2, r * P:(r + 1) * P],
                                            rhs, start=fresh, stop=last, skip_group_check=True)
                            fresh = False
                    ins.then_inc(pv_done, 1)

                for q in range(total + 3):
                    if q < total:
                        scores(q)
                    if 2 <= q < total + 2:
                        turn(q - 2)
                    if q >= 3:
                        pv(q - 3)

            pe.wait_ge(aux_cp, A_AT["qk_da"] + 8)
            attention("da", lambda h, b, m, tok: qaT[64 * b:64 * b + 64, 2 * h + m, tok * P:(tok + 1) * P],
                      lambda h, b, m, w: kT[64 * b:64 * b + 64, 2 * h + m, 0:w],
                      lambda h, m, kb: v_da[:, kb, (2 * h + m) * P:(2 * h + m + 1) * P],
                      lambda h, m: ((2 * h + m) % 4) * P)
            pe.wait_ge(o_read, 4)
            aux_groups("q_ns", 0, lambda kt, t: qr[:, t, kt * P:(kt + 1) * P])
            pe.wait_ge(aux_cp, A_AT["q_ns"] + 4)
            attention("ns", lambda h, b, m, tok: qaT[64 * b:64 * b + 64, h, tok * P:(tok + 1) * P],
                      lambda h, b, m, w: (ksT, kwT)[m][64 * b:64 * b + 64, h // 4, 0:w],
                      lambda h, m, kb: (vs, vw)[m % 2][:, kb, 64 * (h // 4):64 * (h // 4) + 64],
                      lambda h, m: ((2 * h + m // 2) % 8) * 64)

            pe.wait_ge(exp_done, ATT["ns"] + 16)
            paired("gates", h_hi, h_lo)
            transposes("y_da", lambda t: y_mix[:, 0, t, :], SRC["y_da"])
            plain("proj_da", y_hi, y_lo, need_groups("y_da"))
            transposes("y_ns", lambda t: y_mix[:, 1, t, :], SRC["y_ns"])
            plain("proj_ns", h_hi, h_lo, need_groups("y_ns"))
            transposes("m", lambda t: m_buf[:, t, :], SRC["m"])
            plain("out", h_hi, h_lo, need_groups("m"), norm_out="norm2")
            up("ffn2_up", 256, "norm2")
            down("ffn2_down", "ffn2_up", None)

            norm_t("norm3", 0)
            chunks = layers["pw1"]

            def turn_glu(j):
                c = chunks[j]
                pe.wait_ge(g_ready, j + 1)
                b = aux_bank("glu", j)
                for f in range(2):
                    for t in range(TT):
                        ins = t_.transpose(b[:, (f * TT + t) * P:(f * TT + t + 1) * P],
                                           s[:, c.index % 2, t, f * P:(f + 1) * P], ident)
                ins.then_inc(aux_tr, 1)

            for j, c in enumerate(chunks):
                banks_free(c)
                first = (lambda: norm_t("norm3", 1)) if j == 0 else (lambda: turn_glu(j - 1))
                products(c, h_hi, h_lo, need=need_groups("norm3") if j == 0 else None, before=(1, first))
            turn_glu(3)
            pe.wait_ge(zero_ready, 1)
            for n, ct in enumerate(PE_TILES):
                pe.wait_ge(aux_cp, A_AT["glu"] + ct // 2 + 1)
                for b, ks in enumerate(TAP_BATCHES):
                    pe.wait_ge(diag_ready, n * len(TAP_BATCHES) + b + 1)
                    for k in ks:
                        ins = t_.matmul(ps[:, n, 0:T], diag_w[:, k, :], ubuf[:, ct, k:k + T], start=(k == 0),
                                        stop=(k == TAPS - 1))
                    if b < len(TAP_BATCHES) - 1:
                        ins.then_inc(diag_used, 1)
                ins.then_inc(conv_pe, 1)
            ready = [(conv_dve, 1, 0), (conv_dve, 2, 2), (conv_pool, 1, 1), (conv_pool, 2, 3), (conv_act, 1, 6),
                     (conv_act, 2, 7), (conv_dve, 3, 4), (conv_dve, 4, 5)]
            for n, (sem_, count, ct) in enumerate(ready):
                pe.wait_ge(sem_, count)
                ins = t_.matmul(ps[:, 2, 0:T], const("inv_d"), conv[:, ct], start=(n == 0), stop=(n == KD - 1))
            ins.then_inc(mean_done, 1)
            for q in range(KD // 2):
                pe.wait_ge(squared, q + 1)
                for ct in (2 * q, 2 * q + 1):
                    for t in range(TT):
                        ins = t_.matmul(ps[:, 3, t:t + 1], sq[:, ct, t * P:(t + 1) * P], const("inv_d")[:, 0:1],
                                        start=(ct == 0 and t == 0), stop=(ct == KD - 1 and t == TT - 1),
                                        skip_group_check=True)
            ins.then_inc(var_done, 1)
            pe.wait_ge(std_ready, 2)
            for t in range(TT):
                ins = t_.matmul(ps[:, 2, t * P:(t + 1) * P], tri[:, 2 * P:3 * P], diag_w[:, t, :], start=True, stop=True)
            ins.then_inc(std_spread, 1)
            plain("pw2", h_hi, h_lo, lambda kt: pe.wait_ge(cT_lo, kt + 2), norm_out="norm4")

            def ffn_ple(i, n_a, n_b, n_c):
                up(f"up{i}", 512, n_a)
                down(f"down{i}", f"up{i}", n_b)
                t0 = T_AT[f"emb{i}"]

                def turn_embedding():
                    pe.wait_ge(emb_in, 16 * (i + 1))
                    pe.wait_ge(t_lo, 2 + t0)
                    for k in range(2):
                        for t in range(TT):
                            ins = t_.transpose(psT[:, 0, (k * TT + t) * P:(k * TT + t + 1) * P],
                                               emb[:, t, k * P:(k + 1) * P], ident)
                    ins.then_inc(tr_done, 1)

                e_hi, e_lo = tokens(eT_hi, 1), tokens(eT_lo, 0)
                for j, c in enumerate(layers[f"ple{i}"]):
                    banks_free(c)
                    if c.reader == "act":
                        if j == 0:
                            before = (1, lambda: norm_t(n_b, 1))
                        else:
                            before = (1, lambda: norm_t(n_c, 0)) if n_c else None
                        products(c, h_hi, h_lo, need=need_groups(n_b) if j == 0 else None, before=before)
                        if j == 0:
                            turn_embedding()
                    else:
                        products(c, e_hi, e_lo, need=lambda kt: pe.wait_ge(t_lo, 2 + t0 + 1))

            ffn_ple(0, "norm4", "norm5", "norm6")
            plain("kv", h_hi, h_lo, need_groups("norm6"), norm_in="norm6")
            plain("f", h_hi, h_lo, None)
            transposes("norm6q", lambda t: x[:, t, :], 0)

            def cumulate_and_turn_k():
                pe.wait_ge(lf_ready, 1)
                pe.wait_ge(t_lo, 2 + T_AT["norm6q"] + 4)
                b = aux_bank("cum")
                t_.matmul(b[0:48, 0:T], lfd[:, 0].rearrange("p u h -> p (u h)"), tri[:, P:3 * P], start=True, stop=False)
                t_.matmul(b[0:48, 0:T], lfd[:, 1].rearrange("p u h -> p (u h)"), tri[:, 0:2 * P], start=False,
                          stop=True).then_inc(aux_tr, 1)
                pe.wait_ge(read_dve, 2 + layers["kv"][1].nth_read)
                aux_groups("k_fox", 0, lambda kt, t: kf[:, t, kt * P:(kt + 1) * P])

            for j, c in enumerate(layers["q"]):
                banks_free(c)
                products(c, h_hi, h_lo, need=need_groups("norm6q") if j == 0 else None,
                         before=(0, cumulate_and_turn_k) if j == 1 else None)
            pe.wait_ge(kv_ready, 2)
            aux_groups("q_fox", 0, lambda kt, t: qf[:, t, kt * P:(kt + 1) * P])
            pe.wait_ge(aux_cp, A_AT["q_fox"] + 4)
            attention("fox", lambda h, b, m, tok: qT[64 * b:64 * b + 64, 2 * h + m, tok * P:(tok + 1) * P],
                      lambda h, b, m, w: kTf[64 * b:64 * b + 64, 2 * h + m, 0:w],
                      lambda h, m, kb: vf[:, kb, (4 * h + 2 * (m % 2) + m // 2) * 64:(4 * h + 2 * (m % 2) + m // 2 + 1) * 64],
                      lambda h, m: ((4 * h + 2 * (m % 2) + m // 2) % 8) * 64)
            transposes("y_fox", lambda t: qf[:, t, :], SRC["y_fox"])
            plain("o", h_hi, h_lo, need_groups("y_fox"), norm_out="norm7")
            ffn_ple(1, "norm7", "norm8", None)


_INS = ["x", "ffn1_norm", "ffn1_w1", "ffn1_w3", "ffn1_w2", "mix_norm", "w_in", "da_lambda", "da_head_norm",
        "cmp_pos", "cmp_w1", "cmp_w2", "w_proj_da", "w_proj_nsa", "w_out", "ffn2_norm", "ffn2_w1", "ffn2_w3",
        "ffn2_w2", "final_norm", "p_2", "mix_norm_2", "conv_w_pw1_2", "conv_b_pw1_2", "conv_w_dw_2", "conv_b_dw_2",
        "conv_ln_g_2", "conv_ln_b_2", "conv_w_pw2_2", "conv_b_pw2_2", "kv_norm_2", "w_kvf_2", "b_f_2",
        "attn_w_q_2", "attn_w_o_2", "ffn_norm_2", "ffn_w1_2", "ffn_w2_2", "ple_norm_2", "ple_w_gate_2",
        "ple_w_proj_2", "final_norm_2"]


def kernel(**inputs):
    import numpy as _np
    import concourse.bacc as _bacc
    from concourse import mybir as _mybir
    from concourse.bass_utils import run_bass_kernel_spmd as _run

    nc = _bacc.Bacc("TRN2", target_bir_lowering=False, num_devices=1)
    arrays, args = {}, {}
    for name in _INS:
        a = _np.ascontiguousarray(inputs[name])
        arrays[f"in_{name}_dram"] = a
        args[name] = nc.dram_tensor(f"in_{name}_dram", a.shape, _mybir.dt.from_np(a.dtype), kind="ExternalInput").ap()
    table = constants()[0]
    arrays["in_constants_dram"] = table
    consts = nc.dram_tensor("in_constants_dram", table.shape, _mybir.dt.from_np(table.dtype), kind="ExternalInput").ap()
    out = nc.dram_tensor("out_0_dram", (1, T, D), F32, kind="ExternalOutput").ap()
    block_kernel(nc, args, consts, out)
    r = _run(nc, [arrays], core_ids=[0])
    return r.results[0]["out_0_dram"]
```

```python
from contextlib import ExitStack

import numpy as np
import concourse.bass as bass
from concourse import mybir

F32 = mybir.dt.float32
F32R = mybir.dt.float32r
BF16 = mybir.dt.bfloat16
ALU = mybir.AluOpType
ACT = mybir.ActivationFunctionType
AX_X = mybir.AxisListType.X

P = 128
T = 256
TT = T // P
D = 1024
KD = D // P
F1 = 2816
F2 = 4096
CH = 512
RING = 4
UNIT = 4 * CH
AHEAD = 2
EPS = 1e-6
NEG = -1e30
N_CMP = 15
TAPS = 31
LAM_INIT = 0.2
QSCALE = 0.125
HEADS = 16

IN_KV = 4 * D
IN_KW = IN_KV + CH
KW_W = 256 + 48
IN_GATES = IN_KW + KW_W

GAINS = ["ffn1_norm", "mix_norm", "ffn2_norm", "mix_norm_2.0", "mix_norm_2.1", "kv_norm_2", "ffn_norm_2.0",
         "ffn_norm_2.1", "ple_norm_2.0", "ple_norm_2.1", "conv_ln_g_2", "conv_ln_b_2", "conv_b_dw_2", "da_head_norm"]
GAIN = {n: i for i, n in enumerate(GAINS)}


def constants():
    f = np.float32
    parts, at, off = [], {}, 0

    def put(name, a):
        nonlocal off
        a = np.asarray(a, f).reshape(P, -1)
        at[name] = (off, a.shape[1])
        off += a.shape[1]
        parts.append(a)

    i = np.arange(P)
    put("ident", np.eye(P))
    tri = (i[:, None] <= i[None, :])
    put("inv_d", np.full((P, P), 1.0 / D))
    put("tri", np.concatenate([np.zeros((P, P)), tri, np.ones((P, P))], 1))
    inv = (1.0 / (f(10000.0) ** (np.arange(0, 64, 2, dtype=f) / f(64)))).astype(f)
    pos = (i[:, None] + P * np.arange(TT)[None, :]).astype(f)
    ang = (pos[:, :, None] * inv).astype(f)
    put("cos", np.concatenate([np.cos(ang), np.cos(ang)], 2))
    put("sin", np.concatenate([-np.sin(ang), np.sin(ang)], 2))
    n = np.arange(16)
    valid = (n[None, None, :] * 16 + 31 <= pos[:, :, None]) & (n < N_CMP)
    put("cmask", np.where(valid, 0.0, NEG))
    put("cvalid", valid)
    put("onehot_c", (i[:, None] - 32 == n[None, :]))
    put("onehot_1", (i[:, None] == n[None, :]))
    put("causal", np.where(i[None, :] <= i[:, None], 0.0, NEG))
    return np.concatenate(parts, 1), at


CONST_AT = constants()[1]
N_CONST = CONST_AT["causal"][0]


class Chunk:

    def __init__(self, cols, width, units, reader="dve"):
        self.cols, self.width, self.units, self.reader = cols, width, units, reader
        self.second = {}


def plan(W):
    def kview(w):
        return w.rearrange("(kt p) n -> p kt n", p=P)

    def layer(name, chunks):
        for c in chunks:
            c.index = len(order)
            order.append(c)
            c.u0 = len(units)
            k = 0
            for nk in c.units:
                units.append((c, k, nk))
                k += nk
        layers[name] = chunks

    def plain(w, n, k_units, width=CH, start=0, reader="dve"):
        v = kview(w)
        return [Chunk([(v, start + i * width)], width, k_units, reader) for i in range(n)]

    def dual(a, b, n, b0=0):
        return [Chunk([(kview(a), i * 256), (kview(b), b0 + i * 256)], 256, [4, 4]) for i in range(n)]

    layers, order, units = {}, [], []
    kd, kf1, kf2 = [4, 4], [4] * 5 + [2], [4] * 8
    layer("ffn1_up", dual(W["ffn1_w1"][0], W["ffn1_w3"][0], F1 // 256))
    layer("ffn1_down", plain(W["ffn1_w2"][0], 2, kf1))
    w_in = W["w_in"][0]
    layer("in_kv", plain(w_in, 1, kd, CH, IN_KV) + plain(w_in, 1, kd, KW_W, IN_KW))
    layer("in_q_ns", plain(w_in, 2, kd, CH, 3 * D))
    layer("in_v0", plain(w_in, 1, kd, CH, 2 * D, "act"))
    layer("cmp", [plain(W["cmp_w1"][0, i], 1, [8, 8], 256, 0, "act")[0] for i in range(2)])
    layer("in_v1", plain(w_in, 1, kd, CH, 2 * D + CH, "act"))
    layer("in_qk", plain(w_in, 4, kd))
    layer("gates", plain(w_in, 4, kd, CH, IN_GATES, "act"))
    layer("proj_da", plain(W["w_proj_da"][0], 2, kd))
    layer("proj_ns", plain(W["w_proj_nsa"][0], 2, kd))
    layer("out", plain(W["w_out"][0], 2, kd))
    layer("ffn2_up", dual(W["ffn2_w1"][0], W["ffn2_w3"][0], F1 // 256))
    layer("ffn2_down", plain(W["ffn2_w2"][0], 2, kf1))
    pw1 = W["conv_w_pw1_2"][0]
    layer("pw1", dual(pw1, pw1, 4, D))
    layer("pw2", plain(W["conv_w_pw2_2"][0], 2, kd))
    for i in range(2):
        layer(f"up{i}", plain(W["ffn_w1_2"][i], F2 // CH, kd))
        layer(f"down{i}", plain(W["ffn_w2_2"][i], 2, kf2))
        gate = plain(W["ple_w_gate_2"][i], 2, kd, reader="act")
        proj = plain(W["ple_w_proj_2"][i], 2, [2])
        layer(f"ple{i}", [gate[0], proj[0], gate[1], proj[1]])
        if i == 0:
            layer("kv", plain(W["w_kvf_2"], 4, kd))
            layer("f", plain(W["w_kvf_2"], 1, [8], HEADS, 2 * D))
            layer("q", plain(W["attn_w_q_2"][0], 2, kd))
            layer("o", plain(W["attn_w_o_2"][0], 2, kd))
    on_slot = [0] * RING
    for u, (c, _, _) in enumerate(units):
        if len(c.cols) == 2:
            on_slot[u % RING] += 1
        c.second[u] = on_slot[u % RING]
    read = {"dve": 0, "act": 0}
    for c in order:
        read[c.reader] += 1
        c.nth_read = read[c.reader]
    return layers, order, units


T_GROUPS = [("norm0", 4), ("ffn1_up", 11), ("norm1", 4), ("y_da", 4), ("y_ns", 4), ("m", 4), ("norm2", 4),
            ("ffn2_up", 11), ("norm3", 4), ("norm4", 4), ("up0", 16), ("norm5", 4), ("emb0", 1), ("norm6", 4),
            ("norm6q", 4), ("y_fox", 4), ("norm7", 4), ("up1", 16), ("norm8", 4), ("emb1", 1)]
T_AT = {}
_n = 0
for _name, _k in T_GROUPS:
    T_AT[_name] = _n
    _n += _k

A_GROUPS = [("gain0", 1), ("const", 4), ("raw_cmp", 2), ("kk", 2), ("q_cmp", 4), ("hidden_cmp", 1), ("kc", 1), ("vc", 1), ("s_cmp", 1),
            ("p_cmp", 2), ("qk_da", 8), ("q_ns", 4), ("glu", 4), ("cum", 1), ("k_fox", 4), ("q_fox", 4)]
A_AT = {}
_n = 0
for _name, _k in A_GROUPS:
    A_AT[_name] = _n
    _n += _k


ACT_PARTS = {"ffn1_up": 0, "ffn2_up": 11, "pw1": 22, "up0": 26, "up1": 34}


class Steps:

    def __init__(self, eng, sem):
        self.eng, self.sem, self.n = eng, sem, 0

    def done(self, ins):
        ins.then_inc(self.sem, 1)
        self.n += 1
        self.eng.wait_ge(self.sem, self.n)


def block_kernel(nc, W, consts, out):
    layers, order, units = plan(W)
    with ExitStack() as ctx:
        sb = lambda n, s, d=F32: ctx.enter_context(nc.sbuf_tensor(n, s, d))
        sem = lambda n: ctx.enter_context(nc.semaphore(n))

        def scoped(*specs):
            with ExitStack() as c:
                return [c.enter_context(nc.sbuf_tensor(n, sh, d)) for n, sh, d in specs]

        raw = sb("raw", [P, RING, UNIT])
        w_hi = sb("w_hi", [P, RING, UNIT], F32R)
        w_lo = sb("w_lo", [P, RING, UNIT], F32R)
        x = sb("x", [P, TT, D])
        hT_hi = sb("hT_hi", [P, KD, T], F32R)
        hT_lo = sb("hT_lo", [P, KD, T], F32R)
        blocks_hi, blocks_lo = scoped(("blocks_hi", [P, 2, 16, 30], F32R), ("blocks_lo", [P, 2, 16, 30], F32R))
        xn = sb("xn", [P, TT, D])
        s = sb("s", [P, 2, TT, CH])
        cst = sb("cst", [P, N_CONST])
        identb = sb("identb", [P, P], BF16)
        causalb = sb("causalb", [P, 2 * P], BF16)
        gcol = sb("gcol", [P, len(GAINS), KD])
        taps = sb("taps", [P, KD, TAPS])
        sums = sb("sums", [P, 4])
        mean = sb("mean", [P, 4])
        rstd = sb("rstd", [P, 4])
        half = sb("half", [P, 32])
        pos = sb("pos", [P, 2, 16])
        lam = sb("lam", [P, 8])
        negmax = sb("negmax", [P, 2, 4])
        rowsum = sb("rowsum", [P, 8, 4])
        rowinv = sb("rowinv", [P, 8, 4])
        weight = sb("weight", [P, 2, 4])

        gT_hi, gT_lo = scoped(("gT_hi", [P, F2 // P, T], F32R), ("gT_lo", [P, F2 // P, T], F32R))
        with ExitStack() as mix:
            msb = lambda n, sh, d=F32: mix.enter_context(nc.sbuf_tensor(n, sh, d))
            mixbuf = msb("mixbuf", [P, 4, TT, CH])
            yT_hi, yT_lo, gatebuf, m_buf = scoped(("yT_hi", [P, KD, T], F32R), ("yT_lo", [P, KD, T], F32R),
                                                  ("gatebuf", [P, 4, TT, CH], F32), ("m_buf", [P, TT, D], F32))
            v_da = msb("v_da", [P, TT, D])
            qa = msb("qa", [P, TT, D])
            qr = msb("qr", [P, TT, D])
            kT = msb("kT", [P, KD, T])
            ksT = msb("ksT", [P, 2, T])
            kwT = msb("kwT", [P, 2, T])
            vs = msb("vs", [P, TT, P])
            vw = msb("vw", [P, TT, P])
            gl = msb("gl", [P, TT, 48])
            gates = msb("gates", [P, TT, 48])
            w2k = msb("w2k", [P, 2, 2, 64])
            w2v = msb("w2v", [P, 2, 64])
            kcT = msb("kcT", [P, 2, 2, 16])
            vcb = msb("vcb", [P, 2, 4, 64])
            g1k = msb("g1k", [P, 2, 2, 16])
            g1v = msb("g1v", [P, 2, 2, 4, 32])
            cstat = msb("cstat", [P, 3, TT * HEADS])
            pcT = msb("pcT", [P, TT, 4, P])
        ubuf, conv, sq, b_pw1, stat, b_pw2, diag_w = scoped(
            ("ubuf", [P, KD, TAPS - 1 + T], F32), ("conv", [P, KD, T], F32), ("sq", [P, KD, T], F32),
            ("b_pw1", [P, 2 * D], F32), ("stat", [P, 2, TT], F32), ("b_pw2", [P, D], F32),
            ("diag_w", [P, TAPS, P], F32))
        qf, kf, vf, qT, kTf, bias_r, bias_l, cum, fz, lfd, b_f = scoped(
            ("qf", [P, TT, D], F32), ("kf", [P, TT, D], F32), ("vf", [P, TT, D], F32), ("qT", [P, KD, T], F32),
            ("kTf", [P, KD, T], F32), ("bias_r", [P, HEADS, T], F32), ("bias_l", [P, T], F32), ("cum", [48, T], F32),
            ("fz", [P, 4, TT, HEADS], F32), ("lfd", [P, TT, 3, HEADS], F32), ("b_f", [P, HEADS], F32))
        emb, eT_hi, eT_lo = scoped(("emb", [P, TT, 256], F32), ("eT_hi", [P, 2, T], F32R), ("eT_lo", [P, 2, T], F32R))
        qaT = qa[:].rearrange("p a b -> p (a b)").rearrange("p (k t) -> p k t", t=T)
        diag = kT[:].rearrange("p a b -> p (a b)").rearrange("p (i m q) -> p i m q", i=4, m=4)
        y_mix = mixbuf[:].rearrange("p a b c -> p (a b c)").rearrange("p (i t n) -> p i t n", i=2, t=TT)
        scratch = mixbuf[:].rearrange("p a b c -> p (a b c)")[:, 2 * D:4 * D]
        blk_full = scratch[:, 0:960].rearrange("p (v j r) -> p v j r", v=2, j=16)
        g1 = scratch[:, 1024:1536].rearrange("p (v n) -> p v n", v=2)
        sc = scratch[:, 0:512].rearrange("p (t h n) -> p t h n", t=TT, h=HEADS)
        pc = xn[:].rearrange("p a b -> p (a b)")[:, 0:1024].rearrange("p (t h n) -> p t h n", t=TT, h=HEADS)
        kvd = xn[:].rearrange("p t (v g u d) -> p t v g u d", v=4, g=2, u=2)
        probs = s[:].rearrange("p a b c -> p a (b c)")
        probsT = xn
        rows_f = s[:].rearrange("p a b c -> p (a b c)")[:, 0:P]
        _, const_rows = scoped(("before_const_rows", [P, (F2 + F1) // P * T], F32), ("const_rows", [P, 2 * D], F32))
        rows_w = const_rows[:, 0:1024]
        rows_g = const_rows[:, 1024:1152]
        rows_p = const_rows[:, 1152:1408]
        causal_in = const_rows[:, 1408:1536]
        lam_in = const_rows[:, 1536:1792].rearrange("p (a d) -> p a d", a=4)
        cin = [scratch[:, 1536 + 256 * k:1792 + 256 * k].rearrange("p (g m) -> p g m", g=2)
               for k in range(2)]
        fin_gain = xn[:, 1, :]
        cos_x = s[:].rearrange("p a b c -> p (a b c)")[:, 1024:1152].rearrange("p (t d) -> p t d", t=TT)
        sin_x = s[:].rearrange("p a b c -> p (a b c)")[:, 1152:1280].rearrange("p (t d) -> p t d", t=TT)
        ps = ctx.enter_context(nc.psum_tensor("ps", [P, 8, CH], F32))
        psT = ps[:, 4:8, :]

        def rot_tmp(t):
            return s[:].rearrange("p a b c -> p (a b c)")[:, 1536 + P * t:1536 + P * (t + 1)]

        def const(name):
            o, w = CONST_AT[name]
            return cst[:, o:o + w]

        ident = const("ident")
        tri = const("tri")
        cos = const("cos").rearrange("p (t d) -> p t d", t=TT)
        sin = const("sin").rearrange("p (t d) -> p t d", t=TT)
        cmask = const("cmask").rearrange("p (t n) -> p t n", t=TT)
        cvalid = const("cvalid").rearrange("p (t n) -> p t n", t=TT)

        raw_a = [sem(f"raw_a{i}") for i in range(RING)]
        raw_b = [sem(f"raw_b{i}") for i in range(RING)]
        hi_ready = sem("hi_ready")
        lo_ready = sem("lo_ready")
        unit_used = sem("unit_used")
        read_dve = sem("read_dve")
        read_act = sem("read_act")
        act_part = sem("act_part")
        g_ready = sem("g_ready")
        tr_done = sem("tr_done")
        t_hi = sem("t_hi")
        t_lo = sem("t_lo")
        aux_tr = sem("aux_tr")
        aux_cp = sem("aux_cp")
        dve_step = sem("dve_step")
        pool_step = sem("pool_step")
        x_in = sem("x_in")
        x_in1 = sem("x_in1")
        const_first = sem("const_first")
        const_in = sem("const_in")
        consts_ready = sem("consts_ready")
        x_half = sem("x_half")
        sum_dve = sem("sum_dve")
        sum_act = sem("sum_act")
        rstd_ready = sem("rstd_ready")
        xn_ready = sem("xn_ready")
        lam_sum = sem("lam_sum")
        lam_exp = sem("lam_exp")
        kv_ready = sem("kv_ready")
        blocks_ready = sem("blocks_ready")
        w2_in = sem("w2_in")
        cmp_sub = sem("cmp_sub")
        cmp_exp = sem("cmp_exp")
        cmp_p = sem("cmp_p")
        gl_ready = sem("gl_ready")
        gates_ready = sem("gates_ready")
        scores_done = sem("scores_done")
        max_done = sem("max_done")
        exp_done = sem("exp_done")
        probs_ready = sem("probs_ready")
        probs_tr = sem("probs_tr")
        probsT_ready = sem("probsT_ready")
        weight_ready = sem("weight_ready")
        pv_done = sem("pv_done")
        o_read = sem("o_read")
        y_sum = sem("y_sum")
        y_rstd = sem("y_rstd")
        conv_in = sem("conv_in")
        diag_ready = sem("diag_ready")
        diag_used = sem("diag_used")
        conv_pe = sem("conv_pe")
        conv_act = sem("conv_act")
        conv_dve = sem("conv_dve")
        conv_pool = sem("conv_pool")
        mean_done = sem("mean_done")
        centred = sem("centred")
        squared = sem("squared")
        var_done = sem("var_done")
        std_ready = sem("std_ready")
        std_spread = sem("std_spread")
        normed = sem("normed")
        silu_done = sem("silu_done")
        cT_hi = sem("cT_hi")
        cT_lo = sem("cT_lo")
        emb_in = sem("emb_in")
        bf_in = sem("bf_in")
        f_abs = sem("f_abs")
        f_exp = sem("f_exp")
        f_ln = sem("f_ln")
        lf_ready = sem("lf_ready")
        zero_ready = sem("zero_ready")
        bias_rows = sem("bias_rows")
        fin_in = sem("fin_in")
        out_ready = sem("out_ready")
        out_done = sem("out_done")

        def unit_view(t, u_slot, nk, w):
            return t[:, u_slot, 0:nk * w].rearrange("p (k w) -> p k w", w=w)

        def width(c):
            return c.width * len(c.cols)

        def pairs(name, lag):
            n = len(layers[name])
            loops = (n - lag) // 2
            return n, loops

        block = ctx.enter_context(nc.Block())

        @block.sync
        def _(sp):
            xv = W["x"].rearrange("b (t p) d -> p (b t) d", p=P)
            sp.dma_start(x[:, :, 0:CH], xv[:, :, 0:CH]).then_inc(x_in, 16)

            def load(u, i=None, step=0, per=0, turns=0):
                c, k0, nk = units[u]
                shift = 0 if i is None else i
                if u >= RING or i is not None:
                    sp.wait_ge(lo_ready, u + 1 + per * shift)
                for q, (v, col) in enumerate(c.cols):
                    dst = raw[:, u % RING, 0:nk * width(c)].rearrange("p (k h w) -> p k h w", k=nk, w=c.width)[:, :, q, :]
                    cols = slice(col, col + c.width) if i is None else bass.ds(col + step * i, c.width)
                    sp.dma_start(dst, v[:, k0:k0 + nk, cols]).then_inc((raw_a, raw_b)[q][u % RING], 16)

            for name, chunks in layers.items():
                n, loops = pairs(name, 0)
                if n >= 4 and not name.startswith("ple"):
                    with sp.Fori(0, loops) as i:
                        for c in chunks[0:2]:
                            for u in range(c.u0, c.u0 + 2):
                                load(u, i, 2 * c.width, 4)
                    rest = chunks[2 * loops:]
                else:
                    rest = chunks
                for c in rest:
                    for u in range(c.u0, c.u0 + len(c.units)):
                        load(u)
            for h in range(2):
                sp.wait_ge(out_ready, h + 1)
                sp.dma_start(out.rearrange("b (t p) d -> p (b t) d", p=P)[:, :, h * CH:(h + 1) * CH],
                             x[:, :, h * CH:(h + 1) * CH]).then_inc(out_done, 16)
            sp.wait_ge(out_done, 32)

        def split_shape(u):
            c, _, nk = units[u]
            return slice(0, nk * width(c))

        NORM = {n: i for i, n in enumerate(["norm0", "norm1", "norm2", "fin0", "norm3", "norm4", "norm5", "norm6",
                                            "norm7", "norm8", "fin1"])}
        SRC = {n: i + 1 for i, n in enumerate(["y_da", "y_ns", "m", "m second half", "y_fox"])}

        def half_ready(name, h):
            after = {"norm1": "ffn1_down", "norm2": "out", "fin0": "ffn2_down", "norm4": "pw2", "norm5": "down0",
                     "norm7": "o", "norm8": "down1"}
            if name == "norm0":
                return (x_in, x_in1)[h], 16
            if name in after:
                return read_dve, 2 + layers[after[name]][h].nth_read
            return x_half, {"norm3": 0, "norm6": 2, "fin1": 4}[name] + h + 1
        ATT = {"da": 0, "ns": 8, "fox": 24}
        ATT_STEPS = {"da": 4, "ns": 8, "fox": 4}
        DVE_TILES = [0, 2, 4, 5]
        POOL_TILES = [1]
        PE_TILES = [3, 6, 7]
        CONV_BANKS = [0, 1, 3]
        TAP_BATCHES = [range(k, min(k + 8, TAPS)) for k in range(0, TAPS, 8)]

        @block.gpsimd
        def _(pool):
            g = nc.gpsimd
            steps = Steps(pool, pool_step)
            for k in range(RING):
                g.memset(half[:, k:k + 1], -0.5).then_inc(lo_ready, 1)
            for k in range(RING):
                g.memset(half[:, RING + k:RING + k + 1], -0.5).then_inc(unit_used, 1)
            for k in range(2):
                g.memset(half[:, 8 + k:9 + k], -0.5).then_inc(read_dve, 1)
                g.memset(half[:, 10 + k:11 + k], -0.5).then_inc(read_act, 1)
                g.memset(half[:, 12 + k:13 + k], -0.5).then_inc(t_lo, 1)
            steps.done(g.memset(half[:, 14:32], -0.5))

            def rsqrt(n, name):
                pool.wait_ge(sum_dve, 2 * n + 2)
                pool.wait_ge(sum_act, 2 * n + 2)
                steps.done(g.tensor_tensor(out=mean[:, 2:4], in0=sums[:, 0:2], in1=sums[:, 2:4], op=ALU.add))
                steps.done(g.tensor_scalar(mean[:, 0:2], mean[:, 2:4], 1.0 / D, EPS, ALU.mult, ALU.add))
                g.tensor_tensor(out=rstd[:, 0:2], in0=mean[:, 0:2], in1=half[:, 0:2], op=ALU.pow).then_inc(rstd_ready, 1)

            rsqrt(NORM["norm0"], "norm0")
            loads = [(causal_in, consts[:, N_CONST:N_CONST + P])]
            for i, n in enumerate(GAINS):
                base, _, layer = n.partition(".")
                src = W[base]
                src = src[int(layer)] if layer else src
                if base == "da_head_norm":
                    src = src[0]
                elif len(src.shape) == 2:
                    src = src[0].rearrange("(a d) -> a d", d=P)
                else:
                    src = src.rearrange("(a d) -> a d", d=P)
                loads.append((rows_g[KD * i:KD * i + KD, :], src))
            loads.append((rows_w[0:TAPS, :], W["conv_w_dw_2"][0]))
            for k in range(2):
                loads.append((rows_p[0:16, k * P:(k + 1) * P], W["cmp_pos"][0, k].rearrange("(j h) d -> j (h d)", h=2)))
            loads.append((lam_in, W["da_lambda"].rearrange("a b c -> a (b c)").partition_broadcast(P)
                          .rearrange("q p (b c) -> q (p b) c", b=4)))
            for dst, src in loads:
                pool.dma_start(dst, src).then_inc(const_in, 16)
            pool.wait_ge(read_dve, 2 + layers["ffn1_down"][1].nth_read)
            w2 = W["cmp_w2"][0]
            for d_ in range(2):
                pool.dma_start(w2k[:, :, d_, :], w2[0].rearrange("(k p) d -> p k d", p=P)).then_inc(w2_in, 16)
            pool.dma_start(w2v[:], w2[1].rearrange("(k p) d -> p k d", p=P)).then_inc(w2_in, 16)
            rsqrt(NORM["norm1"], "norm1")
            n = TT * ATT_STEPS["ns"]
            for q in range(n):
                st = ATT["ns"] + q
                pool.wait_ge(weight_ready, q + 1)
                if q >= 2:
                    pool.wait_ge(probs_tr, st - 1)
                g.tensor_tensor(out=diag[:, st % 2], in0=ident.unsqueeze(1).broadcast_to([P, 4, P]),
                                in1=weight[:, st % 2, :].unsqueeze(2).broadcast_to([P, 4, P]),
                                op=ALU.mult).then_inc(probs_ready, 1)
            pool.wait_ge(y_sum, 1)
            steps.done(g.tensor_scalar(cstat[:, 1, 0:16], cstat[:, 0, 0:16], 1.0 / P, EPS, ALU.mult, ALU.add))
            g.tensor_tensor(out=cstat[:, 2, 0:16], in0=cstat[:, 1, 0:16], in1=half[:, 0:16], op=ALU.pow).then_inc(y_rstd, 1)
            rsqrt(NORM["norm2"], "norm2")
            pool.wait_ge(read_dve, 2 + layers["out"][1].nth_read)
            pool.dma_start(fin_gain, W["final_norm"].rearrange("(a d) -> a d", a=1).partition_broadcast(P)).then_inc(fin_in, 16)
            rsqrt(NORM["fin0"], "fin0")
            pool.wait_ge(read_dve, 2 + layers["ffn2_down"][1].nth_read)
            pool.dma_start(b_pw1[:], W["conv_b_pw1_2"].partition_broadcast(P)).then_inc(conv_in, 16)
            pool.dma_start(b_pw2[:], W["conv_b_pw2_2"].partition_broadcast(P)).then_inc(conv_in, 16)
            g.memset(ubuf[:, :, 0:TAPS - 1], 0.0).then_inc(zero_ready, 1)
            rsqrt(NORM["norm3"], "norm3")
            for ct in POOL_TILES:
                pool.wait_ge(aux_cp, A_AT["glu"] + ct // 2 + 1)
                steps.done(g.tensor_scalar(conv[:, ct], ubuf[:, ct, 0:T], taps[:, ct, 0:1],
                                           gcol[:, GAIN["conv_b_dw_2"], ct:ct + 1], ALU.mult, ALU.add))
                for k in range(1, TAPS):
                    steps.done(g.tensor_scalar(sq[:, ct], ubuf[:, ct, k:k + T], taps[:, ct, k:k + 1], 0.0,
                                               ALU.mult, ALU.add))
                    last = g.tensor_tensor(out=conv[:, ct], in0=conv[:, ct], in1=sq[:, ct], op=ALU.add)
                    if k < TAPS - 1:
                        steps.done(last)
                last.then_inc(conv_pool, 1)
            pool.wait_ge(std_ready, 1)
            steps.done(g.tensor_tensor(out=stat[:, 1, :], in0=stat[:, 0, :], in1=half[:, 0:2], op=ALU.pow))
            g.tensor_tensor(out=diag_w[:, 0:2, :], in0=ident.unsqueeze(1).broadcast_to([P, TT, P]),
                            in1=stat[:, 1, :].unsqueeze(2).broadcast_to([P, TT, P]), op=ALU.mult).then_inc(std_ready, 1)
            rsqrt(NORM["norm4"], "norm4")
            pool.wait_ge(read_dve, 2 + layers["down0"][1].nth_read)
            pool.dma_start(emb[:], W["p_2"][0].rearrange("b (t p) d -> p (b t) d", p=P)).then_inc(emb_in, 16)
            rsqrt(NORM["norm5"], "norm5")
            pool.wait_ge(x_half, 4)
            pool.dma_start(b_f[:], W["b_f_2"].rearrange("(a d) -> a d", a=1).partition_broadcast(P)).then_inc(bf_in, 16)
            rsqrt(NORM["norm6"], "norm6")
            steps.done(g.memset(bias_r[:], 0.0))
            steps.done(g.memset(bias_l[:], 0.0))
            steps.done(g.memset(bias_l[32:48], -1.0))
            g.tensor_copy(bias_r[0:16], const("onehot_1")[0:16].unsqueeze(2).broadcast_to([16, HEADS, T])).then_inc(zero_ready, 1)
            pool.wait_ge(zero_ready, 2)
            pool.wait_ge(read_dve, 2 + layers["o"][1].nth_read)
            pool.dma_start(fin_gain, W["final_norm_2"].rearrange("(a d) -> a d", a=1).partition_broadcast(P)).then_inc(fin_in, 16)
            rsqrt(NORM["norm7"], "norm7")
            pool.wait_ge(read_dve, 2 + layers["down1"][1].nth_read)
            pool.dma_start(emb[:], W["p_2"][1].rearrange("b (t p) d -> p (b t) d", p=P)).then_inc(emb_in, 16)
            rsqrt(NORM["norm8"], "norm8")
            rsqrt(NORM["fin1"], "fin1")

        @block.scalar
        def _(act):
            a = nc.scalar
            act.dma_start(cst[:], consts[:, 0:N_CONST]).then_inc(const_first, 16)
            act.dma_start(rows_f[0:KD, :], W["ffn1_norm"][0].rearrange("(a d) -> a d", d=P)).then_inc(const_first, 16)
            act.dma_start(x[:, :, CH:D], W["x"].rearrange("b (t p) d -> p (b t) d", p=P)[:, :, CH:D]).then_inc(x_in1, 16)

            def split(u, i=None, per=0):
                c, _, _ = units[u]
                k = 0 if i is None else i
                turn = per // RING
                act.wait_ge(unit_used, u + 1 + per * k)
                act.wait_ge(raw_a[u % RING], 16 * (u // RING + 1) + 16 * turn * k)
                if len(c.cols) == 2:
                    act.wait_ge(raw_b[u % RING], 16 * c.second[u] + 16 * turn * k)
                n = split_shape(u)
                a.activation(w_hi[:, u % RING, n], raw[:, u % RING, n], ACT.Copy).then_inc(hi_ready, 1)

            def split_next(c, i=None, per=0):
                end = c.u0 + len(c.units)
                for u in range(end - len(c.units) + AHEAD, min(end + AHEAD, len(units))):
                    split(u, i, per)

            def chunk_done(c, i=None, per=0):
                act.wait_ge(unit_used, RING + c.u0 + len(c.units) + (per * i if i is not None else 0))

            def hi_group(t, dst, scale=1.0, bank=None, i=None, per=0, ordered=True):
                k = 0 if i is None else per * i
                act.wait_ge(tr_done, t + 1 + k)
                return a.activation(dst, bank, ACT.Copy, scale=scale)

            def hi_groups(name, dst, gain=None, groups=range(4)):
                for j in groups:
                    t = T_AT[name] + j
                    act.wait_ge(tr_done, t + 1)
                    bank = psT[:, j, :].rearrange("p (k t) -> p k t", k=2)
                    for k in range(2):
                        kt = 2 * j + k
                        sc_ = 1.0 if gain is None else gcol[:, GAIN[gain], kt:kt + 1]
                        ins = a.activation(dst[:, kt, :], bank[:, k, :], ACT.Copy, scale=sc_)
                    ins.then_inc(t_hi, 1)

            def rstd_of(name):
                act.wait_ge(rstd_ready, NORM[name] + 1)

            def norm(name, gain, h):
                n = NORM[name]
                if gain:
                    hi_groups(name, hT_hi, gain, range(2 * h, 2 * h + 2))
                if n or h:
                    act.wait_ge(sum_act, 2 * n + h)
                act.wait_ge(*half_ready(name, h))
                a.activation(xn[:, 0, CH:2 * CH], x[:, 1, h * CH:(h + 1) * CH], ACT.Square,
                             accum_out=sums[:, 2 * h + 1:2 * h + 2]).then_inc(sum_act, 1)

            def residual(name, norm_name, gain, between=None):
                for h, c in enumerate(layers[name]):
                    split_next(c)
                    if h == 0 and between:
                        between()
                    if h == 1:
                        norm(norm_name, gain, 0)
                norm(norm_name, gain, 1)

            def up(name, func, w, norm_name):
                chunks = layers[name]
                n, loops = pairs(name, 1)
                groups = w // 256
                loops = (n - 2) // 2
                dst = gT_hi[:].rearrange("p k t -> p (k t)")

                def one(j, i=None):
                    c = chunks[j]
                    k = 0 if i is None else i
                    split_next(c, i, 4)
                    if j == 0:
                        rstd_of(norm_name)
                    chunk_done(c, i, 4)
                    for t in range(TT):
                        ins = a.activation(s[:, c.index % 2, t, 0:w], ps[:, 2 * (c.index % 2) + t, 0:w], func,
                                           scale=rstd[:, t:t + 1])
                    ins.then_inc(act_part, 1)
                    if j > 0:
                        lag(j - 1, i)

                def lag(j, i=None):
                    for q in range(groups):
                        t = T_AT[name] + j * groups + q
                        at = (j * groups + q) * 512
                        if i is None:
                            d = dst[:, at:at + 512]
                        else:
                            d = dst[:, bass.ds(at + i * (2 * groups * 512), 512)]
                        hi_group(t, d, 1.0, psT[:, t % 2, :], i, 2 * groups).then_inc(t_hi, 1)

                one(0)
                with act.Fori(0, loops) as i:
                    one(1, i)
                    one(2, i)
                for j in range(1 + 2 * loops, n):
                    one(j)
                lag(n - 1)

            def attention(kind):
                for tok in range(TT):
                    w = P * (tok + 1)
                    for q in range(ATT_STEPS[kind]):
                        st = ATT[kind] + tok * ATT_STEPS[kind] + q
                        act.wait_ge(max_done, st + 1)
                        if st >= 2:
                            act.wait_ge(probs_tr, st - 1)
                        for b in range(2):
                            for m in range(2):
                                o = m * 2 + b if kind == "fox" else b * 2 + m
                                ins = a.activation(probs[:, st % 2, (2 * b + m) * T:(2 * b + m) * T + w],
                                                   ps[:, 2 * (st % 2) + b, m * w:m * w + w], ACT.Exp,
                                                   bias=negmax[:, st % 2, 2 * b + m:2 * b + m + 1],
                                                   accum_out=rowsum[:, st % 8, o:o + 1])
                        ins.then_inc(exp_done, 1)

            act.wait_ge(aux_cp, 1)
            for h in range(2):
                norm("norm0", "ffn1_norm", h)
                split(h)
            up("ffn1_up", ACT.Silu, 256, "norm0")

            def lambda_exp():
                act.wait_ge(lam_sum, 1)
                a.activation(lam[:, 2:4], lam[:, 0:2], ACT.Exp).then_inc(lam_exp, 1)
                act.wait_ge(consts_ready, 1)

            residual("ffn1_down", "norm1", "mix_norm", lambda_exp)

            def read_v(h):
                c = layers[f"in_v{h}"][0]
                split_next(c)
                chunk_done(c)
                for t in range(TT):
                    ins = a.activation(v_da[:, t, h * CH:(h + 1) * CH], ps[:, 2 * (c.index % 2) + t, :], ACT.Copy,
                                       scale=rstd[:, t:t + 1])
                ins.then_inc(read_act, 1)

            for c in layers["in_kv"] + layers["in_q_ns"]:
                split_next(c)
            rstd_of("norm1")
            act.wait_ge(gl_ready, 1)
            a.activation(gates[:], gl[:], ACT.Sigmoid).then_inc(gates_ready, 1)
            read_v(0)
            for v, c in enumerate(layers["cmp"]):
                split_next(c)
                chunk_done(c)
                a.activation(g1[0:30, v, :], ps[0:30, 2 * (c.index % 2), 0:256], ACT.Gelu_apprx_tanh).then_inc(read_act, 1)
            read_v(1)
            for j, c in enumerate(layers["in_qk"]):
                split_next(c)
                if j == 1:
                    act.wait_ge(cmp_sub, 1)
                    a.activation(sc[:], sc[:], ACT.Exp).then_inc(cmp_exp, 1)
            attention("da")
            attention("ns")

            def gate_chunk(c, dst):
                chunk_done(c)
                for t in range(TT):
                    ins = a.activation(dst(t), ps[:, 2 * (c.index % 2) + t, :], ACT.Sigmoid, scale=rstd[:, t:t + 1])
                ins.then_inc(read_act, 1)

            for j, c in enumerate(layers["gates"]):
                split_next(c)
                if j == 0:
                    act.wait_ge(o_read, 8)
                if j == 3:
                    hi_groups("y_da", yT_hi, "da_head_norm")
                gate_chunk(c, lambda t, j=j: gatebuf[:, j, t, :])
            for j, c in enumerate(layers["proj_da"]):
                split_next(c)
                if j == 1:
                    hi_groups("y_ns", hT_hi)
            for j, c in enumerate(layers["proj_ns"]):
                split_next(c)
                if j == 1:
                    hi_groups("m", hT_hi, groups=range(2))
            hi_groups("m", hT_hi, groups=range(2, 4))
            residual("out", "norm2", "ffn2_norm")
            up("ffn2_up", ACT.Silu, 256, "norm2")
            residual("ffn2_down", "fin0", None)
            for h in range(2):
                norm("norm3", "mix_norm_2.0", h)

            def diagonals(ct, n, ks):
                for k in ks:
                    ins = a.activation(diag_w[:, k, :], ident, ACT.Copy, scale=taps[:, ct, k:k + 1])
                ins.then_inc(diag_ready, 1)

            for j, c in enumerate(layers["pw1"]):
                split_next(c)
                act.wait_ge(read_dve, 2 + c.nth_read)
                for t in range(TT):
                    ins = a.activation(s[:, c.index % 2, t, 256:512], s[:, c.index % 2, t, 256:512], ACT.Sigmoid)
                ins.then_inc(act_part, 1)
                diagonals(PE_TILES[0], j, TAP_BATCHES[j])
            for n in range(1, len(PE_TILES)):
                for b, taps_ in enumerate(TAP_BATCHES):
                    if b < len(TAP_BATCHES) - 1:
                        act.wait_ge(diag_used, (n - 1) * (len(TAP_BATCHES) - 1) + b + 1)
                    else:
                        act.wait_ge(conv_pe, n)
                    diagonals(PE_TILES[n], b, taps_)
            for n, ct in enumerate(PE_TILES):
                act.wait_ge(conv_pe, n + 1)
                a.activation(conv[:, ct], ps[:, CONV_BANKS[n], 0:T], ACT.Identity,
                             bias=gcol[:, GAIN["conv_b_dw_2"], ct:ct + 1]).then_inc(conv_act, 1)
            for q in range(KD // 2):
                act.wait_ge(centred, q + 1)
                a.activation(sq[:, 2 * q:2 * q + 2], conv[:, 2 * q:2 * q + 2], ACT.Square).then_inc(squared, 1)

            def silu(ct):
                if ct % 2 == 0:
                    act.wait_ge(normed, ct // 2 + 1)
                a.activation(conv[:, ct], conv[:, ct], ACT.Silu, scale=gcol[:, GAIN["conv_ln_g_2"], ct:ct + 1],
                             bias=gcol[:, GAIN["conv_ln_b_2"], ct:ct + 1]).then_inc(silu_done, 1)

            silu(0)
            for ct in range(KD):
                if ct + 1 < KD:
                    silu(ct + 1)
                act.wait_ge(silu_done, ct + 1)
                a.activation(hT_hi[:, ct, :], conv[:, ct], ACT.Copy).then_inc(cT_hi, 1)
            residual("pw2", "norm4", "ffn_norm_2.0")

            def ffn_ple(i, n_a, n_b, n_c, gain_c):
                up(f"up{i}", ACT.Relu, 512, n_a)
                residual(f"down{i}", n_b, f"ple_norm_2.{i}")
                act.wait_ge(tr_done, T_AT[f"emb{i}"] + 1)
                a.activation(eT_hi[:].rearrange("p k t -> p (k t)"), psT[:, 0, :], ACT.Copy).then_inc(t_hi, 1)
                for j, c in enumerate(layers[f"ple{i}"]):
                    split_next(c)
                    if j == 0:
                        rstd_of(n_b)
                    if j == 2:
                        norm(n_c, gain_c, 0)
                    if c.reader == "act":
                        gate_chunk(c, lambda t, j=j: s[:, j // 2, t, :])
                norm(n_c, gain_c, 1)

            ffn_ple(0, "norm4", "norm5", "norm6", "kv_norm_2")
            for c in layers["kv"] + layers["f"]:
                split_next(c)
            act.wait_ge(f_abs, 1)
            a.activation(fz[:, 2], fz[:, 1], ACT.Exp).then_inc(f_exp, 1)
            act.wait_ge(f_exp, 1)
            a.activation(fz[:, 3], fz[:, 2], ACT.Ln, bias=1.0).then_inc(f_ln, 1)
            chunk_done(layers["f"][0])
            hi_groups("norm6q", hT_hi, "mix_norm_2.1")
            for c in layers["q"]:
                split_next(c)
            attention("fox")
            hi_groups("y_fox", hT_hi)
            residual("o", "norm7", "ffn_norm_2.1")
            ffn_ple(1, "norm7", "norm8", "fin1", None)

        @block.vector
        def _(dve):
            v = nc.vector
            steps = Steps(dve, dve_step)

            def split(u, i=None, per=0):
                k = 0 if i is None else i
                dve.wait_ge(hi_ready, u + 1 + per * k)
                n = split_shape(u)
                v.tensor_tensor(w_lo[:, u % RING, n], raw[:, u % RING, n], w_hi[:, u % RING, n].bitcast(F32),
                                ALU.subtract).then_inc(lo_ready, 1)

            def split_next(c, i=None, per=0):
                end = c.u0 + len(c.units)
                for u in range(end - len(c.units) + AHEAD, min(end + AHEAD, len(units))):
                    split(u, i, per)

            def chunk_done(c, i=None, per=0):
                dve.wait_ge(unit_used, RING + c.u0 + len(c.units) + (per * i if i is not None else 0))

            def bank(c, t):
                return ps[:, 2 * (c.index % 2) + t, :]

            def lo_groups(name, hi, lo, gain=None, groups=range(4)):
                for j in groups:
                    t = T_AT[name] + j
                    dve.wait_ge(t_hi, t + 1)
                    bk = psT[:, j, :].rearrange("p (k t) -> p k t", k=2)
                    for k in range(2):
                        kt = 2 * j + k
                        g_ = 1.0 if gain is None else gcol[:, GAIN[gain], kt:kt + 1]
                        ins = v.scalar_tensor_tensor(out=lo[:, kt, :], in0=bk[:, k, :], scalar=g_,
                                                     in1=hi[:, kt, :].bitcast(F32), op0=ALU.mult, op1=ALU.subtract)
                    ins.then_inc(t_lo, 1)

            def rstd_of(name):
                dve.wait_ge(rstd_ready, NORM[name] + 1)

            def norm(name, gain, h):
                n = NORM[name]
                if gain:
                    lo_groups(name, hT_hi, hT_lo, gain, range(2 * h, 2 * h + 2))
                if n or h:
                    dve.wait_ge(sum_dve, 2 * n + h)
                dve.wait_ge(*half_ready(name, h))
                v.tensor_tensor_reduce(out=xn[:, 0, 0:CH], in0=x[:, 0, h * CH:(h + 1) * CH],
                                       in1=x[:, 0, h * CH:(h + 1) * CH], scale=1.0, scalar=0.0, op0=ALU.mult,
                                       op1=ALU.add, accum_out=sums[:, 2 * h:2 * h + 1]).then_inc(sum_dve, 1)
                if h == 1 and not gain:
                    rstd_of(name)

            def final_norm(name, sem_, nth):
                dve.wait_ge(fin_in, 16 * nth)
                for h in range(2):
                    for t in range(TT):
                        xh = x[:, t, h * CH:(h + 1) * CH]
                        ins = v.scalar_tensor_tensor(out=xh, in0=xh, scalar=rstd[:, t:t + 1],
                                                     in1=fin_gain[:, h * CH:(h + 1) * CH], op0=ALU.mult, op1=ALU.mult)
                    ins.then_inc(sem_, 1)

            def up(name, w, off, norm_name):
                chunks = layers[name]
                n = len(chunks)
                loops = (n - 2) // 2
                groups = w // 256
                lo = gT_lo[:].rearrange("p k t -> p (k t)")
                hi = gT_hi[:].rearrange("p k t -> p (k t)")
                part0 = ACT_PARTS[name]

                def one(j, i=None):
                    c = chunks[j]
                    k = 0 if i is None else 2 * i
                    split_next(c, i, 4)
                    if j == 0:
                        rstd_of(norm_name)
                    dve.wait_ge(act_part, part0 + j + 1 + k)
                    for t in range(TT):
                        ins = v.scalar_tensor_tensor(out=s[:, c.index % 2, t, 0:w], in0=bank(c, t)[:, off:off + w],
                                                     scalar=rstd[:, t:t + 1], in1=s[:, c.index % 2, t, 0:w],
                                                     op0=ALU.mult, op1=ALU.mult)
                    ins.then_inc(read_dve, 1)
                    if j > 0:
                        lag(j - 1, i)

                def lag(j, i=None):
                    for q in range(groups):
                        t = T_AT[name] + j * groups + q
                        at = (j * groups + q) * 512
                        k = 0 if i is None else 2 * groups * i
                        sl = slice(at, at + 512) if i is None else bass.ds(at + i * (2 * groups * 512), 512)
                        dve.wait_ge(t_hi, t + 1 + k)
                        v.tensor_tensor(lo[:, sl], psT[:, t % 2, :], hi[:, sl].bitcast(F32),
                                        ALU.subtract).then_inc(t_lo, 1)

                one(0)
                with dve.Fori(0, loops) as i:
                    one(1, i)
                    one(2, i)
                for j in range(1 + 2 * loops, n):
                    one(j)
                lag(n - 1)

            def residual(name, scale, norm_name, gain, between=None):
                for h, c in enumerate(layers[name]):
                    split_next(c)
                    if h == 0 and between:
                        between()
                    if h == 1:
                        norm(norm_name, gain, 0)
                    chunk_done(c)
                    for t in range(TT):
                        ins = v.scalar_tensor_tensor(out=x[:, t, h * CH:(h + 1) * CH], in0=bank(c, t), scalar=scale,
                                                     in1=x[:, t, h * CH:(h + 1) * CH], op0=ALU.mult, op1=ALU.add)
                    ins.then_inc(read_dve, 1)
                norm(norm_name, gain, 1)

            def rotary(src, dst, heads, t, cos, sin):
                tmp = s[:].rearrange("p a b c -> p (a b c)")[:, CH * t:CH * t + heads * 64].rearrange(
                    "p (h d) -> p h d", d=64)
                sv = src.rearrange("p (h d) -> p h d", d=64)
                dv = dst.rearrange("p (h d) -> p h d", d=64)
                v.tensor_tensor(dv, sv, cos[:, t, :].unsqueeze(1).broadcast_to([P, heads, 64]), ALU.mult)
                v.tensor_tensor(tmp[:, :, 0:32], sv[:, :, 32:64],
                                sin[:, t, 0:32].unsqueeze(1).broadcast_to([P, heads, 32]), ALU.mult)
                steps.done(v.tensor_tensor(tmp[:, :, 32:64], sv[:, :, 0:32],
                                           sin[:, t, 32:64].unsqueeze(1).broadcast_to([P, heads, 32]), ALU.mult))
                return v.tensor_tensor(dv, dv, tmp, ALU.add)

            def aux(name, j=0):
                n = A_AT[name] + j
                dve.wait_ge(aux_tr, n + 1)
                return psT[:, n % 4, :]

            def copied(ins):
                ins.then_inc(aux_cp, 1)

            def copy_groups(name, first, dst, scale, groups=range(4)):
                for j in groups:
                    b = aux(name, first + j)
                    copied(v.tensor_scalar(dst[:, 2 * j:2 * j + 2, :], b.rearrange("p (k t) -> p k t", k=2), scale,
                                           None, ALU.mult))

            copied(v.tensor_copy(gcol[:, 0, :], aux("gain0")[:, 0:KD]))
            dve.wait_ge(aux_cp, 1)
            for h in range(2):
                norm("norm0", "ffn1_norm", h)
                split(h)
            up("ffn1_up", 256, 256, "norm0")

            def constants_in():
                dve.wait_ge(const_in, 16 * (len(GAINS) + 5))
                v.tensor_copy(identb[:], ident)
                v.memset(causalb[:, 0:P], 0.0)
                v.tensor_copy(causalb[:, P:2 * P], causal_in)
                lp = lam_in.rearrange("p (a b) c -> p a b c", a=2)
                steps.done(v.tensor_tensor(lam_in[:, 0:4:2, :], lp[:, :, 0, :], lp[:, :, 1, :], ALU.mult))
                v.tensor_reduce(lam[:, 0:2], lam_in[:, 0:4:2, :], AX_X, ALU.add).then_inc(lam_sum, 1)
                copied(v.tensor_copy(gcol[:, 1:, :].rearrange("p g k -> p (g k)"), aux("const", 0)[:, KD:KD * len(GAINS)]))
                for h in range(2):
                    b = aux("const", 1 + h)
                    copied(v.tensor_copy(taps[:, 4 * h:4 * h + 4, :],
                                         b[:, 0:4 * P].rearrange("p (k w) -> p k w", k=4)[:, :, 0:TAPS]))
                copied(v.tensor_copy(pos[:].rearrange("p k j -> p (k j)"), aux("const", 3)[:, 0:32]))
                dve.wait_ge(aux_cp, A_AT["const"] + 4)
                g_da = gcol[:, GAIN["da_head_norm"], :]
                steps.done(v.tensor_scalar(g_da, g_da, 1.0 - LAM_INIT, None, ALU.mult))
                dve.wait_ge(lam_exp, 1)
                steps.done(v.tensor_tensor(lam[:, 5:6], lam[:, 3:4], lam[:, 2:3], ALU.subtract))
                v.tensor_scalar(lam[:, 4:5], lam[:, 5:6], -LAM_INIT, None, ALU.add).then_inc(consts_ready, 1)

            residual("ffn1_down", 0.5, "norm1", "mix_norm", constants_in)
            in_kv = layers["in_kv"]

            def read_q_ns(h):
                c = layers["in_q_ns"][h]
                chunk_done(c)
                cols = slice(h * CH, (h + 1) * CH)
                for t in range(TT):
                    ins = v.tensor_scalar(qa[:, t, cols], bank(c, t), rstd[:, t:t + 1], None, ALU.mult)
                ins.then_inc(read_dve, 1)
                dve.wait_ge(read_dve, 2 + c.nth_read)
                for t in range(TT):
                    ins = rotary(qa[:, t, cols], qr[:, t, cols], 8, t, cos, sin)
                steps.done(ins)

            def read_qk(j):
                c = layers["in_qk"][j]
                chunk_done(c)
                for t in range(TT):
                    ins = rotary(bank(c, t), mixbuf[:, j, t, :], 8, t, cos_x, sin_x)
                ins.then_inc(read_dve, 1)

            c = in_kv[0]
            split_next(c)
            rstd_of("norm1")
            for t in range(TT):
                v.tensor_scalar(cos_x[:, t, :], cos[:, t, :], rstd[:, t:t + 1], None, ALU.mult)
                ins = v.tensor_scalar(sin_x[:, t, :], sin[:, t, :], rstd[:, t:t + 1], None, ALU.mult)
            steps.done(ins)

            chunk_done(c)
            for t in range(TT):
                for q in range(2):
                    v.tensor_scalar(kvd[:, t, q], bank(c, t)[:, q * P:(q + 1) * P].rearrange("p (g d) -> p g d", g=2)
                                    .unsqueeze(2).broadcast_to([P, 2, 2, 64]), rstd[:, t:t + 1], None, ALU.mult)
                v.tensor_scalar(vs[:, t, :], bank(c, t)[:, 3 * P:4 * P], rstd[:, t:t + 1], None, ALU.mult)
                ins = rotary(bank(c, t)[:, 2 * P:3 * P], rot_tmp(t), 2, t, cos_x, sin_x)
                if t == TT - 1:
                    ins.then_inc(read_dve, 1)
                    dve.wait_ge(read_dve, 2 + c.nth_read)
                else:
                    steps.done(ins)
            for t in range(TT):
                steps.done(v.tensor_copy(kvd[:, t, 2], rot_tmp(t).rearrange("p (g d) -> p g d", g=2)
                                         .unsqueeze(2).broadcast_to([P, 2, 2, 64])))
            c = in_kv[1]
            split_next(c)
            chunk_done(c)
            for t in range(TT):
                v.tensor_scalar(vw[:, t, :], bank(c, t)[:, P:2 * P], rstd[:, t:t + 1], None, ALU.mult)
                v.tensor_scalar(gl[:, t, :], bank(c, t)[:, 2 * P:2 * P + 48], rstd[:, t:t + 1], None, ALU.mult)
                ins = rotary(bank(c, t)[:, 0:P], rot_tmp(t), 2, t, cos_x, sin_x)
                if t == TT - 1:
                    ins.then_inc(read_dve, 1)
                    dve.wait_ge(read_dve, 2 + c.nth_read)
                else:
                    steps.done(ins)
            for t in range(TT):
                ins = v.tensor_copy(kvd[:, t, 3], rot_tmp(t).rearrange("p (g d) -> p g d", g=2)
                                    .unsqueeze(2).broadcast_to([P, 2, 2, 64]))
                if t == 0:
                    ins.then_inc(gl_ready, 1)
            ins.then_inc(kv_ready, 1)

            split_next(layers["in_q_ns"][0])
            read_q_ns(0)
            split_next(layers["in_q_ns"][1])
            for k in range(2):
                b = aux("raw_cmp", k).rearrange("p (g t) -> p g t", g=2)
                for h in range(2):
                    ins = v.tensor_copy(cin[k][64 * h:64 * h + 64], b[64 * h:64 * h + 64, :, h:T:2])
                copied(ins)
            copied(v.tensor_copy(ksT[:].rearrange("p g t -> p (g t)"), aux("kk", 0)))
            copied(v.tensor_copy(kwT[:].rearrange("p g t -> p (g t)"), aux("kk", 1)))
            dve.wait_ge(aux_cp, A_AT["raw_cmp"] + 2)
            for k in range(2):
                for g_ in range(2):
                    src = cin[k][:, g_, :].rearrange("p (n j) -> p j n", j=8)
                    for jh in range(2):
                        ins = v.tensor_tensor(blk_full[:, k, 8 * jh:8 * jh + 8, 15 * g_:15 * g_ + 15],
                                              src[:, :, jh:jh + 15],
                                              pos[:, k, 8 * jh:8 * jh + 8].unsqueeze(2).broadcast_to([P, 8, 15]), ALU.add)
            steps.done(ins)
            steps.done(v.tensor_copy(blocks_hi[:], blk_full))
            v.tensor_tensor(blocks_lo[:], blk_full, blocks_hi[:].bitcast(F32), ALU.subtract).then_inc(blocks_ready, 1)
            read_q_ns(1)
            split_next(layers["in_v0"][0])
            copy_groups("q_cmp", 0, kT, QSCALE)
            for c in layers["cmp"] + layers["in_v1"]:
                split_next(c)
            b = aux("hidden_cmp")
            v.memset(g1k[:], 0.0)
            v.memset(g1v[:], 0.0)
            v.memset(kcT[:], 0.0)
            steps.done(v.memset(vcb[:], 0.0))
            bh = b[:, 0:128].rearrange("p (v k r) -> p v k r", v=2, k=2)[:, :, :, 0:30]
            for kt in range(2):
                v.tensor_copy(g1k[:, kt, :, 0:15], bh[:, 0, kt, :].rearrange("p (g n) -> p g n", g=2))
                for g_ in range(2):
                    ins = v.tensor_copy(g1v[:, kt, g_, :, 0:15],
                                        bh[:, 1, kt, 15 * g_:15 * g_ + 15].unsqueeze(1).broadcast_to([P, 4, 15]))
            copied(ins)
            split_next(layers["in_qk"][0])
            b = aux("kc")[:, 0:32].rearrange("p (g n) -> p g n", g=2)
            for h in range(2):
                ins = v.tensor_copy(kcT[64 * h:64 * h + 64, :, h, :], b[64 * h:64 * h + 64])
            copied(ins)
            b = aux("vc")[:, 0:128].rearrange("p (g d) -> p g d", g=2)
            for j in range(4):
                ins = v.tensor_copy(vcb[32 * j:32 * j + 32, :, j, :], b[32 * j:32 * j + 32])
            copied(ins)
            b = aux("s_cmp")
            for t in range(TT):
                ins = v.tensor_tensor(sc[:, t], b[:, t * 256:(t + 1) * 256].rearrange("p (h n) -> p h n", h=HEADS),
                                      cmask[:, t, :].unsqueeze(1).broadcast_to([P, HEADS, 16]), ALU.add)
            copied(ins)
            dve.wait_ge(aux_cp, A_AT["s_cmp"] + 1)
            scf = sc.rearrange("p t h n -> p (t h) n")
            steps.done(v.tensor_reduce(cstat[:, 0, :], scf, AX_X, ALU.max))
            v.tensor_tensor(scf, scf, cstat[:, 0, :].unsqueeze(2).broadcast_to([P, 32, 16]), ALU.subtract).then_inc(cmp_sub, 1)
            v.memset(pc, 0.0)
            read_qk(0)
            split_next(layers["in_qk"][1])
            read_qk(1)
            dve.wait_ge(cmp_exp, 1)
            steps.done(v.tensor_reduce(cstat[:, 0, :], scf, AX_X, ALU.add))
            steps.done(v.reciprocal(cstat[:, 1, :], cstat[:, 0, :]))
            dve.wait_ge(gates_ready, 1)
            steps.done(v.tensor_tensor(cstat[:, 2, :].rearrange("p (t h) -> p t h", t=TT),
                                       cstat[:, 1, :].rearrange("p (t h) -> p t h", t=TT),
                                       gates[:].rearrange("p t (h r) -> p t h r", r=3)[:, :, :, 0], ALU.mult))
            for t in range(TT):
                ins = v.tensor_tensor(sc[:, t], sc[:, t], cvalid[:, t, :].unsqueeze(1).broadcast_to([P, HEADS, 16]), ALU.mult)
            steps.done(ins)
            for t in range(TT):
                ins = v.tensor_tensor(pc[:, t, :, 0:16], sc[:, t], cstat[:, 2, t * HEADS:(t + 1) * HEADS].unsqueeze(2)
                                      .broadcast_to([P, HEADS, 16]), ALU.mult)
            ins.then_inc(cmp_p, 1)
            split_next(layers["in_qk"][2])
            for j in range(2):
                copied(v.tensor_copy(pcT[:, j].rearrange("p q t -> p (q t)"), aux("p_cmp", j)))
            read_qk(2)
            copy_groups("qk_da", 0, qaT, QSCALE)
            copy_groups("qk_da", 4, kT, 1.0, range(2))
            split_next(layers["in_qk"][3])
            read_qk(3)
            copy_groups("qk_da", 4, kT, 1.0, range(2, 4))

            def attention(kind, o_out):
                n = ATT_STEPS[kind]
                total = TT * n

                def info(q):
                    tok = q // n
                    return ATT[kind] + q, tok, q % n, P * (tok + 1)

                def maxima(q):
                    st, tok, _, w = info(q)
                    dve.wait_ge(scores_done, st + 1)
                    v.tensor_reduce(negmax[:, st % 2, :], ps[:, 2 * (st % 2):2 * (st % 2) + 2, 0:2 * w]
                                    .rearrange("p b (m w) -> p b m w", m=2), AX_X, ALU.max,
                                    negate=True).then_inc(max_done, 1)

                def scale(q):
                    st, tok, h, w = info(q)
                    dve.wait_ge(exp_done, st + 1)
                    pr = probs[:, st % 2].rearrange("p (m w) -> p m w", m=4)
                    steps_r = v.reciprocal(rowinv[:, st % 8, :], rowsum[:, st % 8, :])
                    if kind == "fox":
                        steps_r.then_inc(probs_ready, 1)
                        return
                    steps.done(steps_r)
                    if kind == "da":
                        steps.done(v.scalar_tensor_tensor(out=weight[:, st % 2, 0:2], in0=rowinv[:, st % 8, 2:4],
                                                          scalar=lam[:, 4:5], in1=rowsum[:, st % 8, 0:2],
                                                          op0=ALU.mult, op1=ALU.mult))
                        for m in range(2):
                            ins = v.scalar_tensor_tensor(out=pr[:, m, 0:w], in0=pr[:, 2 + m, 0:w],
                                                         scalar=weight[:, st % 2, m:m + 1], in1=pr[:, m, 0:w],
                                                         op0=ALU.mult, op1=ALU.add)
                        ins.then_inc(probs_ready, 1)
                    else:
                        if q >= 2:
                            dve.wait_ge(probs_ready, st - 1)
                        v.tensor_tensor(weight[:, st % 2, :].rearrange("p (b m) -> p b m", b=2),
                                        rowinv[:, st % 8, :].rearrange("p (b m) -> p b m", b=2),
                                        gates[:, tok, 6 * h:6 * h + 6].rearrange("p (b r) -> p b r", b=2)[:, :, 1:3],
                                        ALU.mult).then_inc(weight_ready, 1)

                def copy_t(q):
                    st, tok, h, w = info(q)
                    blocks = (2 if kind == "da" else 4) * (tok + 1)
                    dve.wait_ge(probs_tr, st + 1)
                    if q >= 2:
                        dve.wait_ge(pv_done, st - 1)
                    v.tensor_copy(probsT[:, st % 2, 0:blocks * P],
                                  ps[:, 6:8, :].rearrange("p a b -> p (a b)")[:, 0:blocks * P]).then_inc(probsT_ready, 1)

                def read_o(tok, b):
                    st = ATT[kind] + tok * n + (b + 1) * n // 2
                    dve.wait_ge(pv_done, st)
                    o_out(tok, b, st % 8).then_inc(o_read, 1)

                for q in range(total + 4):
                    if q < total:
                        maxima(q)
                    if 1 <= q < total + 1:
                        scale(q - 1)
                    if 2 <= q < total + 2:
                        copy_t(q - 2)
                    done = q - 3
                    if done > 0 and done % (n // 2) == 0 and done <= total:
                        read_o((done - 1) // n, ((done - 1) % n) // (n // 2))

            y_da, y_ns = y_mix[:, 0], y_mix[:, 1]

            def o_da(tok, b, st):
                s0 = (tok * 4 + 2 * b) % 8
                return v.tensor_tensor(y_da[:, tok, b * CH:(b + 1) * CH].rearrange("p (s m e) -> p s m e", s=2, m=2),
                                       ps[:, 4 + b, :].rearrange("p (s m e) -> p s m e", s=2, m=2),
                                       rowinv[:, s0:s0 + 2, 0:2].unsqueeze(3).broadcast_to([P, 2, 2, P]), ALU.mult)

            def o_ns(tok, b, st):
                return v.tensor_copy(y_ns[:, tok, b * CH:(b + 1) * CH], ps[:, 4 + b, :])

            attention("da", o_da)
            copy_groups("q_ns", 0, qaT, QSCALE)
            attention("ns", o_ns)
            dve.wait_ge(o_read, 8)
            split_next(layers["gates"][0])
            sqv = xn[:].rearrange("p t n -> p (t n)")
            yv = y_da.rearrange("p t n -> p (t n)")
            steps.done(v.tensor_tensor(sqv, yv, yv, ALU.mult))
            v.tensor_reduce(cstat[:, 0, 0:16], sqv.rearrange("p (h e) -> p h e", e=P), AX_X, ALU.add).then_inc(y_sum, 1)
            split_next(layers["gates"][1])
            dve.wait_ge(y_rstd, 1)
            yh = yv.rearrange("p (h e) -> p h e", e=P)
            v.tensor_tensor(yh, yh, cstat[:, 2, 0:16].unsqueeze(2).broadcast_to([P, 16, P]), ALU.mult).then_inc(xn_ready, 2)

            for c in layers["gates"][2:]:
                split_next(c)
            lo_groups("y_da", yT_hi, yT_lo, "da_head_norm")

            def merged(name, first, at):
                for n, c in enumerate(layers[name]):
                    split_next(c)
                    if n == 1 and first:
                        lo_groups("y_ns", hT_hi, hT_lo)
                    if n == 1 and not first:
                        lo_groups("m", hT_hi, hT_lo, groups=range(2))
                    chunk_done(c)
                    for t in range(TT):
                        g_ = gatebuf[:, at + n, t, :]
                        d = m_buf[:, t, n * CH:(n + 1) * CH]
                        if first:
                            ins = v.tensor_tensor(d, bank(c, t), g_, ALU.mult)
                        else:
                            ins = v.tensor_tensor(g_, bank(c, t), g_, ALU.mult)
                    ins.then_inc(read_dve, 1)
                    if not first:
                        dve.wait_ge(read_dve, 2 + c.nth_read)
                        for t in range(TT):
                            d = m_buf[:, t, n * CH:(n + 1) * CH]
                            ins = v.tensor_tensor(d, d, gatebuf[:, at + n, t, :], ALU.add)
                        ins.then_inc(xn_ready, 1)

            merged("proj_da", True, 0)
            merged("proj_ns", False, 2)
            lo_groups("m", hT_hi, hT_lo, groups=range(2, 4))
            residual("out", 1.0, "norm2", "ffn2_norm")
            up("ffn2_up", 256, 256, "norm2")
            residual("ffn2_down", 0.5, "fin0", None)
            final_norm("fin0", x_half, 1)

            for h in range(2):
                norm("norm3", "mix_norm_2.0", h)
            dve.wait_ge(conv_in, 32)
            dve.wait_ge(zero_ready, 1)
            bp = b_pw1[:].rearrange("p (h n) -> p h n", h=2)
            chunks = layers["pw1"]
            todo = [(ct, k) for ct in DVE_TILES[:2] for k in range(TAPS)]
            todo += [(ct, k) for k in range(TAPS) for ct in DVE_TILES[2:]]
            last_step = {}

            def convolve(n):
                for ct, k in todo[:n]:
                    if k:
                        dve.wait_ge(dve_step, last_step[ct])
                        ins = v.scalar_tensor_tensor(out=conv[:, ct], in0=ubuf[:, ct, k:k + T],
                                                     scalar=taps[:, ct, k:k + 1], in1=conv[:, ct],
                                                     op0=ALU.mult, op1=ALU.add)
                    else:
                        dve.wait_ge(aux_cp, A_AT["glu"] + ct // 2 + 1)
                        ins = v.tensor_scalar(conv[:, ct], ubuf[:, ct, 0:T], taps[:, ct, 0:1],
                                              gcol[:, GAIN["conv_b_dw_2"], ct:ct + 1], ALU.mult, ALU.add)
                    if k < TAPS - 1:
                        ins.then_inc(dve_step, 1)
                        steps.n += 1
                        last_step[ct] = steps.n
                    else:
                        ins.then_inc(conv_dve, 1)
                del todo[:n]

            for j, c in enumerate(chunks):
                if j < 3:
                    split_next(c)
                if j == 0:
                    rstd_of("norm3")
                chunk_done(c)
                for t in range(TT):
                    ins = v.scalar_tensor_tensor(out=s[:, c.index % 2, t, :].rearrange("p (h n) -> p h n", h=2),
                                                 in0=bank(c, t).rearrange("p (h n) -> p h n", h=2),
                                                 scalar=rstd[:, t:t + 1], in1=bp[:, :, 256 * j:256 * j + 256],
                                                 op0=ALU.mult, op1=ALU.add)
                ins.then_inc(read_dve, 1)
                dve.wait_ge(act_part, ACT_PARTS["pw1"] + j + 1)
                for t in range(TT):
                    ins = v.tensor_tensor(s[:, c.index % 2, t, 0:256], s[:, c.index % 2, t, 0:256],
                                          s[:, c.index % 2, t, 256:512], ALU.mult)
                ins.then_inc(g_ready, 1)
                if j:
                    convolve(4 if j < 3 else 22)
                copied(v.tensor_copy(ubuf[:, 2 * j:2 * j + 2, TAPS - 1:TAPS - 1 + T],
                                     aux("glu", j).rearrange("p (k t) -> p k t", k=2)))
                if j < 3:
                    convolve(4)
            convolve(len(todo))
            dve.wait_ge(mean_done, 1)
            for q in range(KD // 2):
                cp = conv[:, 2 * q:2 * q + 2]
                v.tensor_tensor(cp, cp, ps[:, 2, 0:T].unsqueeze(1).broadcast_to([P, 2, T]),
                                ALU.subtract).then_inc(centred, 1)
            split_next(chunks[3])
            for t in range(TT):
                ins = v.tensor_tensor(x[:, t, :], x[:, t, :], b_pw2[:], ALU.add)
            ins.then_inc(dve_step, 1)
            steps.n += 1
            dve.wait_ge(var_done, 1)
            v.tensor_scalar(stat[:, 0, :], ps[:, 3, 0:TT], EPS, None, ALU.add).then_inc(std_ready, 1)
            dve.wait_ge(std_spread, 1)
            dve.wait_ge(dve_step, steps.n)
            for q in range(KD // 2):
                cp = conv[:, 2 * q:2 * q + 2]
                v.tensor_tensor(cp, cp, ps[:, 2, 0:T].unsqueeze(1).broadcast_to([P, 2, T]), ALU.mult).then_inc(normed, 1)
            for ct in range(KD):
                dve.wait_ge(cT_hi, ct + 1)
                v.tensor_tensor(hT_lo[:, ct, :], conv[:, ct], hT_hi[:, ct, :].bitcast(F32), ALU.subtract).then_inc(cT_lo, 1)
            residual("pw2", 1.0, "norm4", "ffn_norm_2.0")

            def ffn_ple(i, n_a, n_b, n_c, gain_c):
                up(f"up{i}", 512, 0, n_a)
                residual(f"down{i}", 1.0, n_b, f"ple_norm_2.{i}")
                dve.wait_ge(t_hi, T_AT[f"emb{i}"] + 1)
                v.tensor_tensor(eT_lo[:].rearrange("p k t -> p (k t)"), psT[:, 0, :],
                                eT_hi[:].rearrange("p k t -> p (k t)").bitcast(F32), ALU.subtract).then_inc(t_lo, 1)
                for j, c in enumerate(layers[f"ple{i}"]):
                    split_next(c)
                    if j == 0:
                        rstd_of(n_b)
                    if j == 2:
                        norm(n_c, gain_c, 0)
                    if c.reader == "act":
                        continue
                    dve.wait_ge(read_act, 2 + layers[f"ple{i}"][j - 1].nth_read)
                    chunk_done(c)
                    n = j // 2
                    for t in range(TT):
                        ins = v.tensor_tensor(s[:, n, t, :], s[:, n, t, :], bank(c, t), ALU.mult)
                    ins.then_inc(read_dve, 1)
                    dve.wait_ge(read_dve, 2 + c.nth_read)
                    for t in range(TT):
                        d = x[:, t, n * CH:(n + 1) * CH]
                        ins = v.tensor_tensor(d, d, s[:, n, t, :], ALU.add)
                    ins.then_inc(x_half, 1)
                norm(n_c, gain_c, 1)

            ffn_ple(0, "norm4", "norm5", "norm6", "kv_norm_2")
            for j, c in enumerate(layers["kv"]):
                split_next(c)
                if j == 0:
                    rstd_of("norm6")
                chunk_done(c)
                dst = (kf, kf, vf, vf)[j]
                for t in range(TT):
                    ins = v.tensor_scalar(dst[:, t, (j % 2) * CH:(j % 2 + 1) * CH], bank(c, t), rstd[:, t:t + 1],
                                          None, ALU.mult)
                ins.then_inc(read_dve, 1)
            c = layers["f"][0]
            split_next(c)
            chunk_done(c)
            dve.wait_ge(bf_in, 16)
            for t in range(TT):
                ins = v.scalar_tensor_tensor(out=fz[:, 0, t], in0=bank(c, t)[:, 0:HEADS], scalar=rstd[:, t:t + 1],
                                             in1=b_f[:], op0=ALU.mult, op1=ALU.add)
            ins.then_inc(read_dve, 1)
            dve.wait_ge(read_dve, 2 + c.nth_read)
            steps.done(v.tensor_scalar(fz[:, 1], fz[:, 0], -1.0, None, ALU.mult))
            v.tensor_tensor(fz[:, 1], fz[:, 1], fz[:, 0], ALU.min).then_inc(f_abs, 1)
            steps.done(v.tensor_scalar(fz[:, 0], fz[:, 0], 0.0, None, ALU.min))
            lo_groups("norm6q", hT_hi, hT_lo, "mix_norm_2.1")
            dve.wait_ge(f_ln, 1)
            for d_ in range(3):
                ins = v.tensor_tensor(lfd[:, :, d_, :], fz[:, 0], fz[:, 3], ALU.subtract)
            ins.then_inc(lf_ready, 1)
            for n, c in enumerate(layers["q"]):
                if n == 0:
                    split_next(c)
                else:
                    copied(v.tensor_copy(cum[:], aux("cum")[0:48, 0:T]))
                    copy_groups("k_fox", 0, kTf, 1.0)
                    dve.wait_ge(aux_cp, A_AT["cum"] + 1)
                    dve.wait_ge(zero_ready, 2)
                    v.tensor_copy(bias_l[0:16, :], cum[0:16, :])
                    for h in range(4):
                        v.tensor_tensor(bias_r[32:48, 4 * h:4 * h + 4], cum[32:48, :].unsqueeze(1).broadcast_to([16, 4, T]),
                                        const("onehot_c")[32:48, 4 * h:4 * h + 4].unsqueeze(2).broadcast_to([16, 4, T]),
                                        ALU.mult).then_inc(bias_rows, 1)
                    copy_groups("q_fox", 0, qT, QSCALE, range(2))
                    split_next(c)
                chunk_done(c)
                for t in range(TT):
                    ins = v.tensor_scalar(qf[:, t, n * CH:(n + 1) * CH], bank(c, t), rstd[:, t:t + 1], None, ALU.mult)
                ins.then_inc(read_dve, 1)
            copy_groups("q_fox", 0, qT, QSCALE, range(2, 4))

            def o_fox(tok, b, st):
                s0 = (tok * 4 + 2 * b) % 8
                return v.tensor_tensor(qf[:, tok, b * CH:(b + 1) * CH].rearrange("p (h e) -> p h e", e=64),
                                       ps[:, 4 + b, :].rearrange("p (h e) -> p h e", e=64),
                                       rowinv[:, s0:s0 + 2, :].rearrange("p s m -> p (s m)").unsqueeze(2)
                                       .broadcast_to([P, 8, 64]), ALU.mult)

            attention("fox", o_fox)
            dve.wait_ge(o_read, 12)
            v.tensor_copy(weight[:, 0, 1:2], qf[:, 0, 0:1]).then_inc(xn_ready, 1)
            lo_groups("y_fox", hT_hi, hT_lo)
            residual("o", 1.0, "norm7", "ffn_norm_2.1")
            ffn_ple(1, "norm7", "norm8", "fin1", None)
            final_norm("fin1", out_ready, 2)

        @block.tensor
        def _(pe):
            t_ = nc.tensor

            def products(c, lhs_hi, lhs_lo, i=None, per=0, need=None, rows=P, tiles=TT, before=()):
                k_ = 0 if i is None else per * i
                w = width(c)
                n_k = sum(c.units)
                k0 = 0
                for q, nk in enumerate(c.units):
                    u = c.u0 + q
                    hi, lo = (unit_view(x_, u % RING, nk, w) for x_ in (w_hi, w_lo))
                    for k in range(nk):
                        kt = k0 + k
                        for at, do in before:
                            if at == kt:
                                do()
                        if k == 0:
                            pe.wait_ge(lo_ready, RING + u + 1 + k_)
                        if need and kt % 2 == 0:
                            need(kt)
                        for t in range(tiles):
                            o = ps[0:rows, 2 * (c.index % 2) + t, 0:w]
                            ah, al = lhs_hi(kt, t), lhs_lo(kt, t)
                            t_.matmul(o, ah, hi[:, k, :], start=(kt == 0), stop=False)
                            t_.matmul(o, ah, lo[:, k, :], start=False, stop=False)
                            ins = t_.matmul(o, al, hi[:, k, :], start=False, stop=(kt == n_k - 1))
                    ins.then_inc(unit_used, 1)
                    k0 += nk

            def banks_free(c):
                if c.index >= 2:
                    b = order[c.index - 2]
                    pe.wait_ge({"dve": read_dve, "act": read_act}[b.reader], 2 + b.nth_read)

            def tokens(t, hi):
                return lambda kt, tok: t[:, kt, tok * P:(tok + 1) * P]

            h_hi, h_lo = tokens(hT_hi, 1), tokens(hT_lo, 0)
            g_hi, g_lo = tokens(gT_hi, 1), tokens(gT_lo, 0)
            y_hi, y_lo = tokens(yT_hi, 1), tokens(yT_lo, 0)

            def need_groups(name):
                return lambda kt: pe.wait_ge(t_lo, 2 + T_AT[name] + kt // 2 + 1)

            def transposes(name, src, src_count, groups=range(4)):
                if src_count:
                    pe.wait_ge(xn_ready, src_count)
                if groups[0] == 0:
                    pe.wait_ge(t_lo, 2 + T_AT[name])
                for j in groups:
                    for k in range(2):
                        for t in range(TT):
                            kt = 2 * j + k
                            ins = t_.transpose(psT[:, j, (k * TT + t) * P:(k * TT + t + 1) * P],
                                               src(t)[:, kt * P:(kt + 1) * P], ident)
                    ins.then_inc(tr_done, 1)

            def norm_t(name, h):
                if h == 0 and T_AT[name]:
                    pe.wait_ge(t_lo, 2 + T_AT[name])
                pe.wait_ge(*half_ready(name, h))
                for j in (2 * h, 2 * h + 1):
                    for k in range(2):
                        for t in range(TT):
                            kt = 2 * j + k
                            ins = t_.transpose(psT[:, j, (k * TT + t) * P:(k * TT + t + 1) * P],
                                               x[:, t, kt * P:(kt + 1) * P], ident)
                    ins.then_inc(tr_done, 1)

            def plain(name, lhs_hi, lhs_lo, need, norm_in=None, norm_out=None, between=None):
                for j, c in enumerate(layers[name]):
                    banks_free(c)
                    before = []
                    if j == 0 and between:
                        before += between
                    if j == 0 and norm_in:
                        before.append((3, norm_in))
                    if j == len(layers[name]) - 1 and norm_out:
                        before.append((4 * (len(c.units) - (1 if len(c.units) < 4 else 2)), norm_out))
                    products(c, lhs_hi, lhs_lo, need=need if j == 0 else None, before=before)

            def up(name, w, norm_name):
                chunks = layers[name]
                n = len(chunks)
                loops = (n - 2) // 2
                groups = w // 256

                def tr(j, i=None):
                    c = chunks[j]
                    k_ = 0 if i is None else 2 * i
                    pe.wait_ge(read_dve, 2 + c.nth_read + k_)
                    for q in range(groups):
                        t0 = T_AT[name] + j * groups + q
                        pe.wait_ge(t_lo, t0 + 1 + k_ * groups)
                        for f in range(2):
                            for t in range(TT):
                                ins = t_.transpose(psT[:, t0 % 2, (f * TT + t) * P:(f * TT + t + 1) * P],
                                                   s[:, c.index % 2, t, (2 * q + f) * P:(2 * q + f + 1) * P], ident)
                        ins.then_inc(tr_done, 1)

                need = need_groups(norm_name)
                banks_free(chunks[0])
                products(chunks[0], h_hi, h_lo, need=need,
                         before=[(3, lambda: norm_t(norm_name, 1))] if norm_name != "norm0" else ())
                banks_free(chunks[1])

                def one(j, i=None):
                    c = chunks[j]
                    pe.wait_ge(read_dve, c.nth_read + (0 if i is None else 2 * i))
                    products(c, h_hi, h_lo, i, 4)
                    tr(j - 1, i)

                with pe.Fori(0, loops) as i:
                    one(1, i)
                    one(2, i)
                for j in range(1 + 2 * loops, n):
                    one(j)
                return lambda: tr(n - 1)

            def down(name, up_name, last_turn, norm_out, between=()):
                need = lambda kt: pe.wait_ge(t_lo, 2 + T_AT[up_name] + kt // 2 + 1)
                plain(name, g_hi, g_lo, need, norm_out=(lambda: norm_t(norm_out, 0)) if norm_out else None,
                      between=[(4, last_turn)] + list(between))

            def aux_bank(name, j=0):
                n = A_AT[name] + j
                if n >= 4:
                    pe.wait_ge(aux_cp, n - 3)
                return psT[:, n % 4, :]

            def aux_groups(name, first, src, count=4, src_first=0):
                for j in range(count):
                    b = aux_bank(name, first + j)
                    for k in range(2):
                        for t in range(TT):
                            ins = t_.transpose(b[:, (k * TT + t) * P:(k * TT + t + 1) * P],
                                               src(2 * (src_first + j) + k, t), ident)
                    ins.then_inc(aux_tr, 1)

            pe.wait_ge(pool_step, 1)
            pe.wait_ge(const_first, 32)
            t_.transpose(aux_bank("gain0")[:, 0:KD], rows_f[0:KD, :], ident[0:KD, 0:KD]).then_inc(aux_tr, 1)

            def turn_constants():
                pe.wait_ge(const_in, 16 * (len(GAINS) + 5))
                pe.wait_ge(t_lo, 2 + T_AT["ffn1_up"] + 11)
                n_g = KD * len(GAINS)
                t_.transpose(aux_bank("const")[:, 0:n_g], rows_g[0:n_g, :], ident[0:n_g, 0:n_g]).then_inc(aux_tr, 1)
                for h in range(2):
                    b = aux_bank("const", 1 + h)
                    for k in range(4):
                        kt = 4 * h + k
                        ins = t_.transpose(b[:, k * P:k * P + TAPS], rows_w[0:TAPS, kt * P:(kt + 1) * P], ident[0:TAPS, 0:TAPS])
                    ins.then_inc(aux_tr, 1)
                b = aux_bank("const", 3)
                for k in range(2):
                    ins = t_.transpose(b[:, 16 * k:16 * k + 16], rows_p[0:16, k * P:(k + 1) * P], ident[0:16, 0:16])
                ins.then_inc(aux_tr, 1)

            pe.wait_ge(aux_cp, 1)
            norm_t("norm0", 0)
            norm_t("norm0", 1)
            last = up("ffn1_up", 256, "norm0")
            down("ffn1_down", "ffn1_up", last, "norm1", [(12, turn_constants)])
            plain("in_kv", h_hi, h_lo, need_groups("norm1"), norm_in=lambda: norm_t("norm1", 1))

            def turn_kv():
                pe.wait_ge(kv_ready, 1)
                pe.wait_ge(t_lo, 2 + T_AT["norm1"] + 4)
                for name, v0 in (("raw_cmp", 0), ("kk", 2)):
                    for k in range(2):
                        b = aux_bank(name, k)
                        for g_ in range(2):
                            for t in range(TT):
                                ins = t_.transpose(b[:, (g_ * TT + t) * P:(g_ * TT + t + 1) * P],
                                                   kvd[:, t, v0 + k, g_].rearrange("p u d -> p (u d)"), ident)
                        ins.then_inc(aux_tr, 1)

            def turn_hidden():
                pe.wait_ge(read_act, 2 + layers["cmp"][1].nth_read)
                b = aux_bank("hidden_cmp")
                for k in range(2):
                    for kt in range(2):
                        ins = t_.transpose(b[:, (k * 2 + kt) * 32:(k * 2 + kt) * 32 + 30], g1[0:30, k, kt * P:(kt + 1) * P],
                                           ident[0:30, 0:30])
                ins.then_inc(aux_tr, 1)

            def compress():
                pe.wait_ge(aux_cp, A_AT["hidden_cmp"] + 1)
                pe.wait_ge(w2_in, 48)
                b = aux_bank("kc")
                for kt in range(2):
                    ins = t_.matmul(b[:, 0:32], w2k[:, kt].rearrange("p u d -> p (u d)"),
                                    g1k[:, kt].rearrange("p g n -> p (g n)"), start=(kt == 0), stop=(kt == 1))
                ins.then_inc(aux_tr, 1)
                b = aux_bank("vc")
                for g_ in range(2):
                    for kt in range(2):
                        ins = t_.matmul(b[:, g_ * 64:(g_ + 1) * 64], g1v[:, kt, g_].rearrange("p u n -> p (u n)"),
                                        w2v[:, kt], start=(kt == 0), stop=(kt == 1))
                ins.then_inc(aux_tr, 1)

            def score_compressed():
                pe.wait_ge(aux_cp, A_AT["vc"] + 1)
                b = aux_bank("s_cmp")
                for t in range(TT):
                    for hp in range(8):
                        at = (t * 8 + hp) * 32
                        ins = t_.matmul(b[:, at:at + 32], kT[:, hp, t * P:(t + 1) * P],
                                        kcT[:, hp // 4].rearrange("p u n -> p (u n)"), start=True, stop=True)
                ins.then_inc(aux_tr, 1)

            def turn_p_cmp():
                pe.wait_ge(cmp_p, 1)
                for t in range(TT):
                    b = aux_bank("p_cmp", t)
                    for q in range(4):
                        ins = t_.transpose(b[:, q * P:(q + 1) * P], pc[:, t, 4 * q:4 * q + 4, :].rearrange("p h n -> p (h n)"),
                                           ident)
                    ins.then_inc(aux_tr, 1)

            def w_in_chunk(c, *before):
                banks_free(c)
                products(c, h_hi, h_lo, before=before)

            w_in_chunk(layers["in_q_ns"][0])
            w_in_chunk(layers["in_q_ns"][1], (0, turn_kv))
            w_in_chunk(layers["in_v0"][0])
            pe.wait_ge(read_dve, 2 + layers["in_q_ns"][1].nth_read)
            aux_groups("q_cmp", 0, lambda kt, t: qa[:, t, kt * P:(kt + 1) * P])
            pe.wait_ge(blocks_ready, 1)
            for k, c in enumerate(layers["cmp"]):
                banks_free(c)
                products(c, lambda kt, t, k=k: blocks_hi[:, k, kt, :], lambda kt, t, k=k: blocks_lo[:, k, kt, :],
                         rows=30, tiles=1)
            w_in_chunk(layers["in_v1"][0], (4, turn_hidden))
            in_qk = layers["in_qk"]
            banks_free(in_qk[0])
            compress()
            products(in_qk[0], h_hi, h_lo, before=[(6, score_compressed)])
            w_in_chunk(in_qk[1])
            w_in_chunk(in_qk[2], (6, turn_p_cmp))

            def turn_qk_da(first, count):
                pe.wait_ge(read_dve, 2 + in_qk[(first + count - 1) // 2].nth_read)
                aux_groups("qk_da", first, lambda kt, t: mixbuf[:, kt // 4, t, (kt % 4) * P:(kt % 4 + 1) * P], count, first)

            w_in_chunk(in_qk[3], (0, lambda: turn_qk_da(0, 4)), (4, lambda: turn_qk_da(4, 2)))
            turn_qk_da(6, 2)

            def attention(kind, q_op, k_op, v_op, o_at):
                n = ATT_STEPS[kind]
                total = TT * n

                def scores(q):
                    st, tok, h = ATT[kind] + q, q // n, q % n
                    w = P * (tok + 1)
                    if kind == "fox" and q < n:
                        pe.wait_ge(bias_rows, h + 1)
                    if q >= 2:
                        pe.wait_ge(exp_done, st - 1)
                    for b in range(2):
                        for m in range(2):
                            o = ps[:, 2 * (st % 2) + b, m * w:(m + 1) * w]
                            first = True
                            if kind == "fox":
                                t_.matmul(o, bias_l[:, tok * P:(tok + 1) * P], bias_r[:, 4 * h + 2 * m + b, 0:w],
                                          start=True, stop=False)
                                first = False
                            t_.matmul(o, q_op(h, b, m, tok), k_op(h, b, m, w), start=first, stop=False)
                            ins = t_.matmul(o, identb[:], causalb[:, 2 * P - w:2 * P], start=False, stop=True)
                    ins.then_inc(scores_done, 1)

                def turn(q):
                    st, tok = ATT[kind] + q, q // n
                    pe.wait_ge(probs_ready, st + 1)
                    if q >= 1:
                        pe.wait_ge(probsT_ready, st)
                    maps = 2 if kind == "da" else 4
                    for m in range(maps):
                        for kb in range(tok + 1):
                            r = m * (tok + 1) + kb
                            o = ps[:, 6 + r // 4, (r % 4) * P:(r % 4 + 1) * P]
                            pr = probs[:, st % 2, m * T + kb * P:m * T + (kb + 1) * P]
                            if kind == "ns":
                                ins = t_.matmul(o, pr, diag[:, st % 2, m, :], start=True, stop=True)
                            else:
                                ins = t_.transpose(o, pr, ident)
                    ins.then_inc(probs_tr, 1)

                def pv(q):
                    st, tok, h = ATT[kind] + q, q // n, q % n
                    pe.wait_ge(probsT_ready, st + 1)
                    bank = h // (n // 2)
                    fresh = h % (n // 2) == 0
                    if fresh and (kind != "da" or tok > 0):
                        reads = {"da": 0, "ns": 4, "fox": 8}[kind] + 2 * tok + bank
                        pe.wait_ge(o_read, reads - 1)
                    if fresh and kind == "ns":
                        for quad in range(2):
                            t_.matmul(ps[:, 4 + bank, quad * 256:(quad + 1) * 256], pcT[:, tok, 2 * bank + quad, :],
                                      vcb[:, bank].rearrange("p j d -> p (j d)"), start=(quad == 0), stop=False,
                                      skip_group_check=True)
                        fresh = False
                    maps = 2 if kind == "da" else 4
                    for m in range(maps):
                        for kb in range(tok + 1):
                            r = m * (tok + 1) + kb
                            rhs = v_op(h, m, kb)
                            at = o_at(h, m)
                            last = h % (n // 2) == n // 2 - 1 and m == maps - 1 and kb == tok
                            ins = t_.matmul(ps[:, 4 + bank, at:at + rhs.shape[-1]], probsT[:, st % 2, r * P:(r + 1) * P],
                                            rhs, start=fresh, stop=last, skip_group_check=True)
                            fresh = False
                    ins.then_inc(pv_done, 1)

                for q in range(total + 3):
                    if q < total:
                        scores(q)
                    if 2 <= q < total + 2:
                        turn(q - 2)
                    if q >= 3:
                        pv(q - 3)

            pe.wait_ge(aux_cp, A_AT["qk_da"] + 8)
            attention("da", lambda h, b, m, tok: qaT[64 * b:64 * b + 64, 2 * h + m, tok * P:(tok + 1) * P],
                      lambda h, b, m, w: kT[64 * b:64 * b + 64, 2 * h + m, 0:w],
                      lambda h, m, kb: v_da[:, kb, (2 * h + m) * P:(2 * h + m + 1) * P],
                      lambda h, m: ((2 * h + m) % 4) * P)
            pe.wait_ge(o_read, 4)
            aux_groups("q_ns", 0, lambda kt, t: qr[:, t, kt * P:(kt + 1) * P])
            pe.wait_ge(aux_cp, A_AT["q_ns"] + 4)
            attention("ns", lambda h, b, m, tok: qaT[64 * b:64 * b + 64, h, tok * P:(tok + 1) * P],
                      lambda h, b, m, w: (ksT, kwT)[m][64 * b:64 * b + 64, h // 4, 0:w],
                      lambda h, m, kb: (vs, vw)[m % 2][:, kb, 64 * (h // 4):64 * (h // 4) + 64],
                      lambda h, m: ((2 * h + m // 2) % 8) * 64)

            pe.wait_ge(exp_done, ATT["ns"] + 16)
            y_da_t = lambda t: y_mix[:, 0, t, :]
            y_ns_t = lambda t: y_mix[:, 1, t, :]
            m_t = lambda t: m_buf[:, t, :]
            plain("gates", h_hi, h_lo, None, norm_out=lambda: transposes("y_da", y_da_t, SRC["y_da"]))
            plain("proj_da", y_hi, y_lo, need_groups("y_da"), norm_out=lambda: transposes("y_ns", y_ns_t, SRC["y_ns"]))
            plain("proj_ns", h_hi, h_lo, need_groups("y_ns"),
                  norm_out=lambda: transposes("m", m_t, SRC["m"], range(2)))
            plain("out", h_hi, h_lo, need_groups("m"),
                  norm_in=lambda: transposes("m", m_t, SRC["m second half"], range(2, 4)),
                  norm_out=lambda: norm_t("norm2", 0))
            last = up("ffn2_up", 256, "norm2")
            down("ffn2_down", "ffn2_up", last, None)

            norm_t("norm3", 0)
            chunks = layers["pw1"]

            def turn_glu(j):
                c = chunks[j]
                pe.wait_ge(g_ready, j + 1)
                b = aux_bank("glu", j)
                for f in range(2):
                    for t in range(TT):
                        ins = t_.transpose(b[:, (f * TT + t) * P:(f * TT + t + 1) * P],
                                           s[:, c.index % 2, t, f * P:(f + 1) * P], ident)
                ins.then_inc(aux_tr, 1)

            for j, c in enumerate(chunks):
                banks_free(c)
                first = (lambda: norm_t("norm3", 1)) if j == 0 else (lambda: turn_glu(j - 1))
                products(c, h_hi, h_lo, need=need_groups("norm3") if j == 0 else None, before=[(3 if j == 0 else 4, first)])

            pe.wait_ge(zero_ready, 1)
            pe.wait_ge(read_dve, 2 + chunks[3].nth_read)

            def convolve(n):
                ct = PE_TILES[n]
                pe.wait_ge(aux_cp, A_AT["glu"] + ct // 2 + 1)
                for b, ks in enumerate(TAP_BATCHES):
                    pe.wait_ge(diag_ready, n * len(TAP_BATCHES) + b + 1)
                    for k in ks:
                        ins = t_.matmul(ps[:, CONV_BANKS[n], 0:T], diag_w[:, k, :], ubuf[:, ct, k:k + T],
                                        start=(k == 0), stop=(k == TAPS - 1))
                    if b < len(TAP_BATCHES) - 1:
                        ins.then_inc(diag_used, 1)
                ins.then_inc(conv_pe, 1)

            convolve(0)
            turn_glu(3)
            convolve(1)
            convolve(2)
            ready = [(conv_dve, 1, 0), (conv_dve, 2, 2), (conv_pool, 1, 1), (conv_act, 1, 3), (conv_act, 2, 6),
                     (conv_dve, 3, 4), (conv_dve, 4, 5), (conv_act, 3, 7)]
            for n, (sem_, count, ct) in enumerate(ready):
                pe.wait_ge(sem_, count)
                ins = t_.matmul(ps[:, 2, 0:T], const("inv_d"), conv[:, ct], start=(n == 0), stop=(n == KD - 1))
            ins.then_inc(mean_done, 1)
            for q in range(KD // 2):
                pe.wait_ge(squared, q + 1)
                for ct in (2 * q, 2 * q + 1):
                    for t in range(TT):
                        ins = t_.matmul(ps[:, 3, t:t + 1], sq[:, ct, t * P:(t + 1) * P], const("inv_d")[:, 0:1],
                                        start=(ct == 0 and t == 0), stop=(ct == KD - 1 and t == TT - 1),
                                        skip_group_check=True)
            ins.then_inc(var_done, 1)
            pe.wait_ge(std_ready, 2)
            for t in range(TT):
                ins = t_.matmul(ps[:, 2, t * P:(t + 1) * P], tri[:, 2 * P:3 * P], diag_w[:, t, :], start=True, stop=True)
            ins.then_inc(std_spread, 1)
            plain("pw2", h_hi, h_lo, lambda kt: pe.wait_ge(cT_lo, kt + 2), norm_out=lambda: norm_t("norm4", 0))

            def ffn_ple(i, n_a, n_b, n_c):
                last = up(f"up{i}", 512, n_a)
                down(f"down{i}", f"up{i}", last, n_b)
                t0 = T_AT[f"emb{i}"]

                def turn_embedding():
                    pe.wait_ge(emb_in, 16 * (i + 1))
                    pe.wait_ge(t_lo, 2 + t0)
                    for k in range(2):
                        for t in range(TT):
                            ins = t_.transpose(psT[:, 0, (k * TT + t) * P:(k * TT + t + 1) * P],
                                               emb[:, t, k * P:(k + 1) * P], ident)
                    ins.then_inc(tr_done, 1)

                e_hi, e_lo = tokens(eT_hi, 1), tokens(eT_lo, 0)
                for j, c in enumerate(layers[f"ple{i}"]):
                    banks_free(c)
                    if c.reader == "act":
                        if j == 0:
                            before = [(3, lambda: norm_t(n_b, 1)), (6, turn_embedding)]
                        else:
                            before = [(4, lambda: norm_t(n_c, 0))] if n_c else ()
                        products(c, h_hi, h_lo, need=need_groups(n_b) if j == 0 else None, before=before)
                    else:
                        products(c, e_hi, e_lo, need=lambda kt: pe.wait_ge(t_lo, 2 + t0 + 1))

            ffn_ple(0, "norm4", "norm5", "norm6")
            plain("kv", h_hi, h_lo, need_groups("norm6"), norm_in=lambda: norm_t("norm6", 1))
            plain("f", h_hi, h_lo, None)
            transposes("norm6q", lambda t: x[:, t, :], 0)

            def cumulate_and_turn_k():
                pe.wait_ge(lf_ready, 1)
                pe.wait_ge(t_lo, 2 + T_AT["norm6q"] + 4)
                b = aux_bank("cum")
                t_.matmul(b[0:48, 0:T], lfd[:, 0].rearrange("p u h -> p (u h)"), tri[:, P:3 * P], start=True, stop=False)
                t_.matmul(b[0:48, 0:T], lfd[:, 1].rearrange("p u h -> p (u h)"), tri[:, 0:2 * P], start=False,
                          stop=True).then_inc(aux_tr, 1)
                pe.wait_ge(read_dve, 2 + layers["kv"][1].nth_read)
                aux_groups("k_fox", 0, lambda kt, t: kf[:, t, kt * P:(kt + 1) * P])

            def turn_q(h):
                pe.wait_ge(read_dve, 2 + layers["q"][h].nth_read)
                aux_groups("q_fox", 2 * h, lambda kt, t: qf[:, t, kt * P:(kt + 1) * P], 2, 2 * h)

            for j, c in enumerate(layers["q"]):
                banks_free(c)
                products(c, h_hi, h_lo, need=need_groups("norm6q") if j == 0 else None,
                         before=[(0, cumulate_and_turn_k), (4, lambda: turn_q(0))] if j == 1 else ())
            turn_q(1)
            pe.wait_ge(aux_cp, A_AT["q_fox"] + 4)
            attention("fox", lambda h, b, m, tok: qT[64 * b:64 * b + 64, 2 * h + m, tok * P:(tok + 1) * P],
                      lambda h, b, m, w: kTf[64 * b:64 * b + 64, 2 * h + m, 0:w],
                      lambda h, m, kb: vf[:, kb, (4 * h + 2 * (m % 2) + m // 2) * 64:(4 * h + 2 * (m % 2) + m // 2 + 1) * 64],
                      lambda h, m: ((4 * h + 2 * (m % 2) + m // 2) % 8) * 64)
            transposes("y_fox", lambda t: qf[:, t, :], SRC["y_fox"])
            plain("o", h_hi, h_lo, need_groups("y_fox"), norm_out=lambda: norm_t("norm7", 0))
            ffn_ple(1, "norm7", "norm8", None)


_INS = ["x", "ffn1_norm", "ffn1_w1", "ffn1_w3", "ffn1_w2", "mix_norm", "w_in", "da_lambda", "da_head_norm",
        "cmp_pos", "cmp_w1", "cmp_w2", "w_proj_da", "w_proj_nsa", "w_out", "ffn2_norm", "ffn2_w1", "ffn2_w3",
        "ffn2_w2", "final_norm", "p_2", "mix_norm_2", "conv_w_pw1_2", "conv_b_pw1_2", "conv_w_dw_2", "conv_b_dw_2",
        "conv_ln_g_2", "conv_ln_b_2", "conv_w_pw2_2", "conv_b_pw2_2", "kv_norm_2", "w_kvf_2", "b_f_2",
        "attn_w_q_2", "attn_w_o_2", "ffn_norm_2", "ffn_w1_2", "ffn_w2_2", "ple_norm_2", "ple_w_gate_2",
        "ple_w_proj_2", "final_norm_2"]


def kernel(**inputs):
    import numpy as _np
    import concourse.bacc as _bacc
    from concourse import mybir as _mybir
    from concourse.bass_utils import run_bass_kernel_spmd as _run

    nc = _bacc.Bacc("TRN2", target_bir_lowering=False, num_devices=1)
    arrays, args = {}, {}
    for name in _INS:
        a = _np.ascontiguousarray(inputs[name])
        arrays[f"in_{name}_dram"] = a
        args[name] = nc.dram_tensor(f"in_{name}_dram", a.shape, _mybir.dt.from_np(a.dtype), kind="ExternalInput").ap()
    table = constants()[0]
    arrays["in_constants_dram"] = table
    consts = nc.dram_tensor("in_constants_dram", table.shape, _mybir.dt.from_np(table.dtype), kind="ExternalInput").ap()
    out = nc.dram_tensor("out_0_dram", (1, T, D), F32, kind="ExternalOutput").ap()
    block_kernel(nc, args, consts, out)
    r = _run(nc, [arrays], core_ids=[0])
    return r.results[0]["out_0_dram"]
```
